# Optimizing a Trainium2 kernel written in Bass

```python
import jax, jax.numpy as jnp
from jax import lax
import numpy as np

D_MODEL = 1024
BATCH = 1
SEQ = 1024
DEPTH = 1
DEC_BATCH = 8
DEC_SEQ = 1
PAST_LEN = 1024
PAGE_SIZE = 128

MIX_WIDTH = D_MODEL
HEAD_DIM = 64
CONV_A_WIDTH = MIX_WIDTH // 4
CONV_A_KERNEL = 31
H_DELTA = (3 * MIX_WIDTH) // (8 * HEAD_DIM)
H_FOX = (3 * MIX_WIDTH) // (8 * HEAD_DIM)
DELTA_WIDTH = H_DELTA * HEAD_DIM
FOX_WIDTH = H_FOX * HEAD_DIM
SHORT_CONV = 4
DELTA_CHUNK = 64
Q_BLOCK = 128
FORGET_BIAS_INIT = 2.0
D_FF = ((-(-8 * D_MODEL // 3) + 255) // 256) * 256
SPLITS = [
    CONV_A_WIDTH,
    2 * CONV_A_WIDTH,
    2 * CONV_A_WIDTH + 3 * DELTA_WIDTH,
    2 * CONV_A_WIDTH + 4 * DELTA_WIDTH,
    2 * CONV_A_WIDTH + 4 * DELTA_WIDTH + H_DELTA,
    2 * CONV_A_WIDTH + 4 * DELTA_WIDTH + 2 * H_DELTA,
    2 * CONV_A_WIDTH + 4 * DELTA_WIDTH + 2 * H_DELTA + 3 * FOX_WIDTH,
]
N_IN = SPLITS[-1] + H_FOX

kernel_name = 'hymba_conformer_gdn_fox_step'

def rmsnorm(x, g, eps=1e-6):
    xf = x.astype(jnp.float32)
    y = xf * lax.rsqrt(jnp.mean(xf * xf, axis=-1, keepdims=True) + eps)
    return (y * g.astype(jnp.float32)).astype(x.dtype)

def layernorm(x, g, b, eps=1e-5):
    xf = x.astype(jnp.float32)
    mu = jnp.mean(xf, axis=-1, keepdims=True)
    xc = xf - mu
    var = jnp.mean(xc * xc, axis=-1, keepdims=True)
    return (xc * lax.rsqrt(var + eps) * g.astype(jnp.float32) + b.astype(jnp.float32)).astype(x.dtype)

def l2norm(x, eps=1e-6):
    xf = x.astype(jnp.float32)
    return xf * lax.rsqrt(jnp.sum(xf * xf, axis=-1, keepdims=True) + eps)

def causal_dwconv(x, buf, w):
    width = w.shape[0]
    x_ext = jnp.concatenate([buf.astype(x.dtype), x], axis=1)
    y = lax.conv_general_dilated(
        x_ext, w.astype(x.dtype)[:, None, :], window_strides=(1,), padding='VALID',
        dimension_numbers=('NWC', 'WIO', 'NWC'), feature_group_count=x.shape[-1])
    return y, x_ext[:, x_ext.shape[1] - (width - 1):]

def gated_delta_rule(q, k, v, g, beta, s0):
    B, T, H, Dk = q.shape
    Dv = v.shape[-1]
    C = DELTA_CHUNK
    n = -(-T // C)
    pad = n * C - T

    def chunks(a):
        a = a.astype(jnp.float32)
        a = jnp.pad(a, [(0, 0), (0, pad)] + [(0, 0)] * (a.ndim - 2))
        a = a.reshape((B, n, C) + a.shape[2:])
        return jnp.moveaxis(a, (1, 3), (0, 2))

    qc = chunks(q) * (Dk ** -0.5)
    kc, vc, gc, bc = chunks(k), chunks(v), chunks(g), chunks(beta)
    gcum = jnp.cumsum(gc, axis=-1)
    idx = jnp.arange(C)
    causal = idx[:, None] >= idx[None, :]
    strict = idx[:, None] > idx[None, :]
    decay = jnp.exp(jnp.where(causal, gcum[..., :, None] - gcum[..., None, :], -jnp.inf))
    kb = kc * bc[..., None]
    lower = jnp.where(strict, jnp.einsum('nbhid,nbhjd->nbhij', kb, kc) * decay, 0.0)
    eye = jnp.eye(C, dtype=jnp.float32)
    tmat = lax.linalg.triangular_solve(lower + eye, jnp.broadcast_to(eye, lower.shape),
                                       left_side=True, lower=True, unit_diagonal=True)
    u = tmat @ (vc * bc[..., None])
    w = tmat @ (kb * jnp.exp(gcum)[..., None])
    qk = jnp.where(causal, jnp.einsum('nbhid,nbhjd->nbhij', qc, kc) * decay, 0.0)

    def step(S, xs):
        q_i, k_i, u_i, w_i, qk_i, g_i = xs
        v_new = u_i - jnp.einsum('bhck,bhkv->bhcv', w_i, S)
        o_i = (jnp.einsum('bhck,bhkv->bhcv', q_i * jnp.exp(g_i)[..., None], S)
               + jnp.einsum('bhij,bhjv->bhiv', qk_i, v_new))
        g_last = g_i[..., -1]
        S = (S * jnp.exp(g_last)[..., None, None]
             + jnp.einsum('bhck,bhcv->bhkv', k_i * jnp.exp(g_last[..., None] - g_i)[..., None], v_new))
        return S, o_i

    S, o = lax.scan(step, s0.astype(jnp.float32), (qc, kc, u, w, qk, gcum))
    o = jnp.moveaxis(o, (0, 2), (1, 3)).reshape(B, n * C, H, Dv)[:, :T]
    return o, S

def forgetting_attention(q, k_all, v_all, logf_all, past_len):
    B, T, H, D = q.shape
    S = k_all.shape[1]
    ck = jnp.moveaxis(jnp.cumsum(logf_all.astype(jnp.float32), axis=1), 2, 1)
    qb = Q_BLOCK if T % Q_BLOCK == 0 else T
    nb = T // qb
    q_blocks = jnp.moveaxis(q.reshape(B, nb, qb, H, D), 1, 0)
    cq_blocks = jnp.moveaxis(ck[:, :, past_len:].reshape(B, H, nb, qb), 2, 0)
    kpos = jnp.arange(S)
    scale = D ** -0.5

    def block(args):
        qi, cqi, bi = args
        s = jnp.einsum('bqhd,bkhd->bhqk', qi, k_all).astype(jnp.float32) * scale
        s = s + cqi[..., :, None] - ck[:, :, None, :]
        qpos = past_len + bi * qb + jnp.arange(qb)
        s = jnp.where(kpos[None, :] <= qpos[:, None], s, -jnp.inf)
        p = jax.nn.softmax(s, axis=-1)
        return jnp.einsum('bhqk,bkhd->bqhd', p.astype(v_all.dtype), v_all)

    out = lax.map(block, (q_blocks, cq_blocks, jnp.arange(nb)))
    return jnp.moveaxis(out, 0, 1).reshape(B, T, H, D)

def trunk_layer(x, p, l, buf_a, buf_b, s_delta, past_k, past_v, past_logf):
    B, T, _ = x.shape
    h = rmsnorm(x, p['g_pre_mix'][l])
    proj = h @ p['w_in'][l]
    a_val, a_gate, qkv_b, z_b, beta_raw, alpha_raw, qkv_c, f_raw = jnp.split(proj, SPLITS, axis=-1)

    u = a_val * jax.nn.sigmoid(a_gate)
    ca, new_buf_a = causal_dwconv(u, buf_a, p['conv_a_w'][l])
    y_a = jax.nn.silu(layernorm(ca + p['conv_a_b'][l], p['ln_a_g'][l], p['ln_a_b'][l]))

    cb, new_buf_b = causal_dwconv(qkv_b, buf_b, p['conv_b_w'][l])
    cb = jax.nn.silu(cb).reshape(B, T, 3, H_DELTA, HEAD_DIM)
    beta = jax.nn.sigmoid(beta_raw.astype(jnp.float32))
    g = -jnp.exp(p['a_log'][l].astype(jnp.float32)) * jax.nn.softplus(
        alpha_raw.astype(jnp.float32) + p['dt_bias'][l].astype(jnp.float32))
    o_d, new_s = gated_delta_rule(l2norm(cb[:, :, 0]), l2norm(cb[:, :, 1]), cb[:, :, 2], g, beta, s_delta)
    y_b = rmsnorm(o_d, p['norm_b_g'][l]) * jax.nn.silu(
        z_b.reshape(B, T, H_DELTA, HEAD_DIM).astype(jnp.float32))
    y_b = y_b.reshape(B, T, DELTA_WIDTH).astype(x.dtype)

    qkv = qkv_c.reshape(B, T, 3, H_FOX, HEAD_DIM)
    qf, kf, vf = qkv[:, :, 0], qkv[:, :, 1], qkv[:, :, 2]
    logf = jax.nn.log_sigmoid((f_raw + p['f_bias'][l]).astype(jnp.float32))
    k_all = jnp.concatenate([past_k.astype(kf.dtype), kf], axis=1)
    v_all = jnp.concatenate([past_v.astype(vf.dtype), vf], axis=1)
    logf_all = jnp.concatenate([past_logf.astype(jnp.float32), logf], axis=1)
    o_f = forgetting_attention(qf, k_all, v_all, logf_all, past_k.shape[1])
    y_c = o_f.reshape(B, T, FOX_WIDTH).astype(x.dtype)

    mix = jnp.concatenate([y_a, y_b, y_c], axis=-1) @ p['w_out'][l]
    x = x + rmsnorm(mix, p['g_post_mix'][l])
    h = rmsnorm(x, p['g_pre_ffn'][l])
    f = (jax.nn.silu(h @ p['w_gate'][l]) * (h @ p['w_up'][l])) @ p['w_down'][l]
    x = x + rmsnorm(f, p['g_post_ffn'][l])
    return x, (kf, vf, logf, new_buf_a, new_buf_b, new_s)

def setup_inputs(seed: int = 0) -> dict:
    key = jax.random.key(seed)
    ks = jax.random.split(key, 32)
    n_pages = PAST_LEN // PAGE_SIZE
    n_phys = (DEC_BATCH * n_pages * 5) // 4

    def nrm(k, shape, s):
        return jax.random.normal(k, shape, jnp.float32) * s

    x_prompt = nrm(ks[0], (BATCH, SEQ, D_MODEL), 1.0)
    x_sample = nrm(ks[1], (DEC_BATCH, DEC_SEQ, D_MODEL), 1.0)
    cache_k = nrm(ks[2], (DEPTH, n_phys, PAGE_SIZE, H_FOX, HEAD_DIM), 1.0)
    cache_v = nrm(ks[3], (DEPTH, n_phys, PAGE_SIZE, H_FOX, HEAD_DIM), 1.0)
    cache_logf = jax.nn.log_sigmoid(FORGET_BIAS_INIT + nrm(ks[4], (DEPTH, n_phys, PAGE_SIZE, H_FOX), 1.0))
    page_table = jax.random.permutation(ks[5], n_phys)[: DEC_BATCH * n_pages].reshape(
        DEC_BATCH, n_pages).astype(jnp.int32)
    state_conv_a = nrm(ks[6], (DEPTH, DEC_BATCH, CONV_A_KERNEL - 1, CONV_A_WIDTH), 0.5)
    state_conv_b = nrm(ks[7], (DEPTH, DEC_BATCH, SHORT_CONV - 1, 3 * DELTA_WIDTH), 1.0)
    state_delta = nrm(ks[8], (DEPTH, DEC_BATCH, H_DELTA, HEAD_DIM, HEAD_DIM), 0.1)

    w_in = nrm(ks[9], (DEPTH, D_MODEL, N_IN), D_MODEL ** -0.5)
    conv_a_w = nrm(ks[10], (DEPTH, CONV_A_KERNEL, CONV_A_WIDTH), CONV_A_KERNEL ** -0.5)
    conv_a_b = nrm(ks[11], (DEPTH, CONV_A_WIDTH), 0.02)
    ln_a_g = 1.0 + nrm(ks[12], (DEPTH, CONV_A_WIDTH), 0.05)
    ln_a_b = nrm(ks[13], (DEPTH, CONV_A_WIDTH), 0.02)
    conv_b_w = nrm(ks[14], (DEPTH, SHORT_CONV, 3 * DELTA_WIDTH), SHORT_CONV ** -0.5)
    a_log = jnp.log(jax.random.uniform(ks[15], (DEPTH, H_DELTA), jnp.float32, 1.0, 16.0))
    dt = jax.random.uniform(ks[16], (DEPTH, H_DELTA), jnp.float32, 0.001, 0.1)
    dt_bias = jnp.log(jnp.expm1(dt))
    norm_b_g = 1.0 + nrm(ks[17], (DEPTH, HEAD_DIM), 0.05)
    f_bias = FORGET_BIAS_INIT + nrm(ks[18], (DEPTH, H_FOX), 0.1)
    w_out = nrm(ks[19], (DEPTH, MIX_WIDTH, D_MODEL), MIX_WIDTH ** -0.5)
    g_pre_mix = 1.0 + nrm(ks[20], (DEPTH, D_MODEL), 0.05)
    g_post_mix = 1.0 + nrm(ks[21], (DEPTH, D_MODEL), 0.05)
    g_pre_ffn = 1.0 + nrm(ks[22], (DEPTH, D_MODEL), 0.05)
    g_post_ffn = 1.0 + nrm(ks[23], (DEPTH, D_MODEL), 0.05)
    w_gate = nrm(ks[24], (DEPTH, D_MODEL, D_FF), D_MODEL ** -0.5)
    w_up = nrm(ks[25], (DEPTH, D_MODEL, D_FF), D_MODEL ** -0.5)
    w_down = nrm(ks[26], (DEPTH, D_FF, D_MODEL), D_FF ** -0.5)
    return {
        'x_prompt': x_prompt, 'x_sample': x_sample,
        'cache_k': cache_k, 'cache_v': cache_v, 'cache_logf': cache_logf, 'page_table': page_table,
        'state_conv_a': state_conv_a, 'state_conv_b': state_conv_b, 'state_delta': state_delta,
        'w_in': w_in, 'conv_a_w': conv_a_w, 'conv_a_b': conv_a_b, 'ln_a_g': ln_a_g, 'ln_a_b': ln_a_b,
        'conv_b_w': conv_b_w, 'a_log': a_log, 'dt_bias': dt_bias, 'norm_b_g': norm_b_g, 'f_bias': f_bias,
        'w_out': w_out, 'g_pre_mix': g_pre_mix, 'g_post_mix': g_post_mix, 'g_pre_ffn': g_pre_ffn,
        'g_post_ffn': g_post_ffn, 'w_gate': w_gate, 'w_up': w_up, 'w_down': w_down,
    }

def reference(x_prompt, x_sample, cache_k, cache_v, cache_logf, page_table, state_conv_a, state_conv_b,
              state_delta, w_in, conv_a_w, conv_a_b, ln_a_g, ln_a_b, conv_b_w, a_log, dt_bias, norm_b_g,
              f_bias, w_out, g_pre_mix, g_post_mix, g_pre_ffn, g_post_ffn, w_gate, w_up, w_down):
    p = dict(w_in=w_in, conv_a_w=conv_a_w, conv_a_b=conv_a_b, ln_a_g=ln_a_g, ln_a_b=ln_a_b,
             conv_b_w=conv_b_w, a_log=a_log, dt_bias=dt_bias, norm_b_g=norm_b_g, f_bias=f_bias,
             w_out=w_out, g_pre_mix=g_pre_mix, g_post_mix=g_post_mix, g_pre_ffn=g_pre_ffn,
             g_post_ffn=g_post_ffn, w_gate=w_gate, w_up=w_up, w_down=w_down)
    B = x_prompt.shape[0]
    Bd = x_sample.shape[0]
    n_pages = page_table.shape[1]
    past_len = n_pages * PAGE_SIZE
    dt = x_prompt.dtype
    zero_buf_a = jnp.zeros((B, CONV_A_KERNEL - 1, CONV_A_WIDTH), dt)
    zero_buf_b = jnp.zeros((B, SHORT_CONV - 1, 3 * DELTA_WIDTH), dt)
    zero_s = jnp.zeros((B, H_DELTA, HEAD_DIM, HEAD_DIM), jnp.float32)
    empty_kv = jnp.zeros((B, 0, H_FOX, HEAD_DIM), dt)
    empty_logf = jnp.zeros((B, 0, H_FOX), jnp.float32)

    xp, xs = x_prompt, x_sample
    prompt_states, sample_states = [], []
    for l in range(DEPTH):
        xp, sp = trunk_layer(xp, p, l, zero_buf_a, zero_buf_b, zero_s, empty_kv, empty_kv, empty_logf)
        prompt_states.append(sp)
        past_k = cache_k[l][page_table].reshape(Bd, past_len, H_FOX, HEAD_DIM)
        past_v = cache_v[l][page_table].reshape(Bd, past_len, H_FOX, HEAD_DIM)
        past_logf = cache_logf[l][page_table].reshape(Bd, past_len, H_FOX)
        xs, ss = trunk_layer(xs, p, l, state_conv_a[l], state_conv_b[l], state_delta[l],
                             past_k, past_v, past_logf)
        sample_states.append(ss)

    k_p, v_p, logf_p, conv_a_p, conv_b_p, delta_p = [jnp.stack(t) for t in zip(*prompt_states)]
    k_s, v_s, logf_s, conv_a_s, conv_b_s, delta_s = [jnp.stack(t) for t in zip(*sample_states)]
    return (xp, xs, k_p, v_p, logf_p, conv_a_p, conv_b_p, delta_p,
            k_s, v_s, logf_s, conv_a_s, conv_b_s, delta_s)


_drawn_inputs = setup_inputs


def setup_inputs(seed=0):
    import zlib

    import numpy as np

    out = dict(_drawn_inputs(seed))
    spreads = {}
    factors = {'conv_a_b': 3.082, 'ln_a_b': 5.624}
    for name, (base, spread) in spreads.items():
        noise = np.random.default_rng([zlib.crc32(name.encode()), seed]).standard_normal(out[name].shape)
        drawn = base * np.exp(spread * noise) if base else spread * noise
        out[name] = __import__('jax').numpy.asarray(drawn.astype(out[name].dtype))
    for name, factor in factors.items():
        out[name] = (out[name] * factor).astype(out[name].dtype)
    return out
```

```python
from contextlib import ExitStack

import concourse.bass as bass
import numpy as np
from concourse import mybir

F32 = mybir.dt.float32
F32R = mybir.dt.float32r
I32 = mybir.dt.int32
ALU = mybir.AluOpType
ACT = mybir.ActivationFunctionType
AX_X = mybir.AxisListType.X

P = 128
D = 1024
SEQ = 1024
NS = 8
T = SEQ + NS
KD = D // P
NG = 3
TG = T // NG
NT = 12
TT = T // NT
HD = 64
H = 6
PAIRS = H // 2
DW = H * HD
CA = 256
KA = 31
KB = 4
DFF = 2816
NF = DFF // P
NC = SEQ // P
PAGE = 128
NPAGE = 8
NPHYS = 80
COL_BETA = 2 * CA + 4 * DW
COL_QC = COL_BETA + 2 * H
COL_VC = COL_QC + 2 * DW
N_IN = COL_VC + DW + H
NV = DW + 3 * H
FIRST_TILES = COL_BETA // P
QC_TILES = 2 * DW // P
NPROJ = FIRST_TILES + QC_TILES
T_A, T_GATE, T_QB, T_KB, T_VB, T_Z, T_QC, T_KC = 0, 2, 4, 7, 10, 13, 16, 19
NEG = -1e30
SCALE = HD ** -0.5
RMS_EPS = 1e-6
LN_EPS = 1e-5

G_PRE_MIX, G_POST_MIX, G_PRE_FFN, G_POST_FFN, CONV_A_B, LN_G, LN_B, CONV_A_W = 0, 8, 16, 24, 32, 34, 36, 38
N_COLS_A = 38 + 2 * KA
CONV_B_W, NORM_B_G = 0, KB * 9
N_COLS_B = NORM_B_G + 1

BASE = 16512
O_CONST = BASE
O_VTOK = O_CONST + 16640
O_PROJ = O_VTOK + 9 * NV * 4 + 24
O_H = O_PROJ + NPROJ * T * 4
O_W = O_H + 2 * KD * T * 4
O_END = 229344
COLS = KD * T * 4
O_FFN = O_PROJ + 3 * COLS


class Mem:
    pass


class Phase(ExitStack):

    def __init__(self, nc):
        super().__init__()
        self.nc, self.own = nc, []

    def __exit__(self, *error):
        if self.own:
            self.nc.clear_and_free_semaphores(self.own)
            self.nc.all_engine_barrier()
        return super().__exit__(*error)


def semaphores(nc, ctx, *names):
    got = [nc.alloc_semaphore(n) for n in names]
    ctx.own.extend(got)
    return got


def constants(nc, m):
    off = O_CONST

    def put(name, shape, dt=F32):
        nonlocal off
        t = nc.alloc_sbuf_tensor_at(name, shape, dt, offset=off)
        n = 4
        for s in shape[1:]:
            n *= s
        off += (n + 31) // 32 * 32
        return t

    m.ident = put("ident", [P, P])
    m.cumul = put("cumul", [P, P])
    m.later = put("later", [P, P])
    m.ones = put("ones", [P, P])
    m.head_ones = put("head_ones", [P, P])
    m.level_mask = put("level_mask", [P, 7, P])
    m.level1_t = put("level1_t", [P, P])
    m.keep_t = put("keep_t", [P, P])
    m.causal = put("causal", [P, P])
    m.head_rows = put("head_rows", [2 * H, H, P])
    m.cols_a = put("cols_a", [P, N_COLS_A])
    m.cols_b = put("cols_b", [P, N_COLS_B])
    m.rows6 = put("rows6", [P, 3 * H])
    m.state = put("state", [P, PAIRS, HD])
    m.eps = put("eps", [P, 4])
    m.gates = put("gates", [P, NC + 1, 3 * H])
    m.pages = put("pages", [1, NS * NPAGE], I32)
    assert off <= O_VTOK, off


def load_and_transpose(nc, m):
    with Phase(nc) as ctx:
        sb = lambda n, s, o, dt=F32: nc.alloc_sbuf_tensor_at(n, s, dt, offset=o)
        m.xT = sb("xT", [P, KD, T], O_PROJ)
        x_rows = sb("x_rows", [P, 4, D], O_W)
        rows_a = sb("rows_a", [N_COLS_A, P], O_H)
        rows_b = sb("rows_b", [N_COLS_B, P], O_H + 512)
        ps = ctx.enter_context(nc.psum_tensor("ps_xT", [P, 2, KD, P], F32))
        ps_cols = ctx.enter_context(nc.psum_tensor("ps_cols", [P, 512], F32))
        const_in, params_in, cols_done, x_turned, x_copied_even, x_spilled = semaphores(
            nc, ctx, "const_in", "params_in", "cols_done", "x_turned", "x_copied_even", "x_spilled")
        x_in = semaphores(nc, ctx, *[f"x_in{n}" for n in range(4)])
        cols_turned, x_copied_odd = semaphores(nc, ctx, "cols_turned", "x_copied_odd")
        x_copied = (x_copied_even, x_copied_odd)
        tiles = NC + 1
        with nc.Block() as block:

            @block.sync
            def _(sp):
                sp.dma_start(m.ident[:], m.tables[0]).then_inc(const_in, 16)
                for n in range(tiles):
                    if n >= 4:
                        sp.wait_ge(x_turned, n - 3)
                    if n < NC:
                        sp.dma_start(x_rows[:, n % 4], m.x_prompt[0, n * P:(n + 1) * P]).then_inc(x_in[n % 4], 16)
                    else:
                        sp.dma_start(x_rows[0:NS, n % 4], m.x_sample[:, 0]).then_inc(x_in[n % 4], 16)
                sp.wait_ge(x_copied_even, (tiles + 1) // 2)
                sp.wait_ge(x_copied_odd, tiles // 2)
                sp.dma_start(m.xT_dram, m.xT[:]).then_inc(x_spilled, 16)
                sp.wait_ge(x_spilled, 16)

            @block.scalar
            def _(act):
                for t, s in ((m.cumul, 1), (m.later, 2), (m.ones, 3), (m.head_ones, 4), (m.level1_t, 5), (m.keep_t, 6),
                             (m.causal, 7)):
                    act.dma_start(t[:], m.tables[s]).then_inc(const_in, 16)
                act.dma_start(m.level_mask[:], m.tables[8:15].rearrange("l p n -> p l n")).then_inc(const_in, 16)
                act.dma_start(m.head_rows[:], m.head_table).then_inc(const_in, 16)
                for v, r in ((m.g_pre_mix, G_PRE_MIX), (m.g_post_mix, G_POST_MIX), (m.g_pre_ffn, G_PRE_FFN),
                             (m.g_post_ffn, G_POST_FFN)):
                    act.dma_start(rows_a[r:r + KD, :], v.rearrange("l (k p) -> (l k) p", p=P)).then_inc(params_in, 16)
                for v, r in ((m.conv_a_b, CONV_A_B), (m.ln_a_g, LN_G), (m.ln_a_b, LN_B)):
                    act.dma_start(rows_a[r:r + 2, :], v.rearrange("l (k p) -> (l k) p", p=P)).then_inc(params_in, 16)
                act.dma_start(rows_a[CONV_A_W:N_COLS_A, :],
                              m.conv_a_w.rearrange("l w (k p) -> (l w k) p", p=P)).then_inc(params_in, 16)
                act.dma_start(rows_b[0:NORM_B_G, :],
                              m.conv_b_w.rearrange("l w (k p) -> (l w k) p", p=P)).then_inc(params_in, 16)
                for e in range(2):
                    act.dma_start(rows_b[NORM_B_G:N_COLS_B, e * HD:(e + 1) * HD], m.norm_b_g).then_inc(params_in, 16)
                for v, c in ((m.f_bias, 0), (m.a_log, 1), (m.dt_bias, 2)):
                    act.dma_start(m.rows6[:, c * H:(c + 1) * H], v[0:1, :].to_broadcast([P, H])).then_inc(params_in, 16)
                act.dma_start(m.pages[:], m.page_table.rearrange("b n -> (b n)")[None, :]).then_inc(params_in, 16)
                act.wait_ge(params_in, 15 * 16)
                for n in range(1, tiles, 2):
                    act.wait_ge(x_turned, n + 1)
                    act.copy(m.xT[:, :, n * P:n * P + P], ps[:, 1]).then_inc(x_copied_odd, 1)

            @block.tensor
            def _(pe):
                pe.wait_ge(const_in, 10 * 16)
                for n in range(tiles):
                    rows = P if n < NC else NS
                    pe.wait_ge(x_in[n % 4], 16 * (n // 4 + 1))
                    if n >= 2:
                        pe.wait_ge(x_copied[n % 2], n // 2)
                    for k in range(KD):
                        last = pe.transpose(ps[:, n % 2, k, 0:rows], x_rows[0:rows, n % 4, k * P:(k + 1) * P],
                                            m.ident[0:rows, 0:rows])
                    last.then_inc(x_turned, 1)
                pe.wait_ge(params_in, 15 * 16)
                pe.transpose(ps_cols[:, 0:N_COLS_A], rows_a[:], m.ident[0:N_COLS_A, 0:N_COLS_A])
                pe.transpose(ps_cols[:, P:P + N_COLS_B], rows_b[:], m.ident[0:N_COLS_B, 0:N_COLS_B]).then_inc(
                    cols_turned, 1)

            @block.vector
            def _(dve):
                for n in range(0, tiles, 2):
                    w = P if n < NC else NS
                    dve.wait_ge(x_turned, n + 1)
                    dve.tensor_copy(m.xT[:, :, n * P:n * P + w], ps[:, 0, :, 0:w]).then_inc(x_copied_even, 1)
                for c, v in enumerate((RMS_EPS, LN_EPS, 1.0)):
                    dve.memset(m.eps[:, c:c + 1], v).then_inc(cols_done, 1)
                dve.wait_ge(cols_turned, 1)
                dve.tensor_copy(m.cols_a[:], ps_cols[:, 0:N_COLS_A]).then_inc(cols_done, 1)
                dve.tensor_copy(m.cols_b[:], ps_cols[:, P:P + N_COLS_B]).then_inc(cols_done, 1)


class Chain:

    def __init__(self, eng, sem):
        self.eng, self.sem, self.n = eng, sem, 0

    def __call__(self, instruction):
        instruction.then_inc(self.sem, 1)
        self.n += 1
        self.eng.wait_ge(self.sem, self.n)


def root(act, small, eps_ready):
    act.wait_ge(eps_ready, 1)
    return act.activation(small[:, 1], small[:, 0], ACT.Sqrt)


def inverse_root(dve, step, small, rooted):
    dve.wait_ge(rooted, 1)
    step(dve.reciprocal(small[:, 1], small[:, 1]))
    step(dve.tensor_tensor(small[:, 2], small[:, 1], small[:, 1], ALU.mult))
    step(dve.tensor_tensor(small[:, 2], small[:, 2], small[:, 0], ALU.mult))
    step(dve.tensor_scalar(small[:, 2], small[:, 2], -0.5, 1.5, ALU.mult, ALU.add))
    return dve.tensor_tensor(small[:, 1], small[:, 1], small[:, 2], ALU.mult)


def spread_tokens(pe, m, ps, inv):
    for c in range(NT):
        g, t = divmod(c * TT, TG)
        last = pe.matmul(ps[:, g, t:t + TT], inv[:, c:c + 1].to_broadcast([TT, P]), m.ident[0:TT, 0:TT], start=True, stop=True)
    return last


def rms_norm(nc, m, tag, src, g, hi, lo, tmp_at):
    with Phase(nc) as ctx:
        sq = nc.alloc_sbuf_tensor_at(f"{tag}_sq", [P, 2, T], F32, offset=tmp_at)
        small = nc.alloc_sbuf_tensor_at(f"{tag}_small", [TT, 3, NT], F32, offset=tmp_at + 2 * T * 4)
        ps_sum = ctx.enter_context(nc.psum_tensor(f"{tag}_ps_sum", [TT, 512], F32))
        ps = ctx.enter_context(nc.psum_tensor(f"{tag}_ps", [P, NG, 512], F32))
        squared, summed, with_eps, rooted, inverted, spread, scaled, hi_done, lo_done, chain = semaphores(
            nc, ctx, *[f"{tag}_{n}" for n in ("squared", "summed", "with_eps", "rooted", "inverted", "spread",
                                              "scaled", "hi_done", "lo_done", "chain")])
        with nc.Block() as block:

            @block.scalar
            def _(act):
                for k in range(KD):
                    if k >= 2:
                        act.wait_ge(summed, k - 1)
                    act.activation(sq[:, k % 2], src[:, k], ACT.Square).then_inc(squared, 1)
                root(act, small, with_eps).then_inc(rooted, 1)
                for k in range(KD):
                    act.wait_ge(scaled, k + 1)
                    act.copy(hi[:, k], sq[:, k % 2]).then_inc(hi_done, 1)

            @block.tensor
            def _(pe):
                for k in range(KD):
                    pe.wait_ge(squared, k + 1)
                    for c in range(NT):
                        last = pe.matmul(ps_sum[:, c:c + 1], sq[:, k % 2, c * TT:(c + 1) * TT], m.ones[:, 0:1],
                                         start=(k == 0 and c == 0), stop=(k == KD - 1), skip_group_check=True)
                    last.then_inc(summed, 1)
                pe.wait_ge(inverted, 1)
                spread_tokens(pe, m, ps, small[:, 1]).then_inc(spread, 1)

            @block.vector
            def _(dve):
                step = Chain(dve, chain)
                dve.wait_ge(summed, KD)
                dve.tensor_scalar(small[:, 0], ps_sum[:, 0:NT], 1.0 / D, RMS_EPS, ALU.mult, ALU.add).then_inc(
                    with_eps, 1)
                inverse_root(dve, step, small, rooted).then_inc(inverted, 1)
                dve.wait_ge(spread, 1)

                def scale(k):
                    if k >= 2:
                        dve.wait_ge(lo_done, k - 1)
                    dve.scalar_tensor_tensor(
                        out=sq[:, k % 2].rearrange("p (g t) -> p g t", g=NG),
                        in0=src[:, k].rearrange("p (g t) -> p g t", g=NG), scalar=m.cols_a[:, g + k:g + k + 1],
                        in1=ps[:, :, 0:TG], op0=ALU.mult, op1=ALU.mult).then_inc(scaled, 1)

                scale(0)
                for k in range(KD):
                    if k + 1 < KD:
                        scale(k + 1)
                    dve.wait_ge(hi_done, k + 1)
                    dve.tensor_tensor(lo[:, k], sq[:, k % 2], hi[:, k].bitcast(F32), ALU.subtract).then_inc(lo_done, 1)


class WeightRing:

    def __init__(self, nc, ctx, tag, off):
        at = nc.alloc_sbuf_tensor_at
        self.raw = [at(f"{tag}_raw{s}", [P, KD, P], F32, offset=off + s * 4096) for s in range(2)]
        self.hi = [at(f"{tag}_whi{s}", [P, KD, P], F32R, offset=off + 8192 + s * 4096) for s in range(2)]
        self.lo = [at(f"{tag}_wlo{s}", [P, KD, P], F32R, offset=off + 16384 + s * 4096) for s in range(2)]


def project(nc, m, tag, w, spans, hi, lo, out):
    with Phase(nc) as ctx:
        ring = WeightRing(nc, ctx, tag, O_W)
        ps = [ctx.enter_context(nc.psum_tensor(f"{tag}_ps{s}", [P, NG, 512], F32)) for s in range(2)]
        w_hi, w_lo_2_ahead, multiplied_2_ahead, copied_2_ahead = semaphores(
            nc, ctx, *[f"{tag}_{n}" for n in ("w_hi", "w_lo_2_ahead", "multiplied_2_ahead", "copied_2_ahead")])
        w_in = semaphores(nc, ctx, f"{tag}_w_in0", f"{tag}_w_in1")
        firsts = [sum(n for _, n in spans[:i]) for i in range(len(spans))]
        with nc.Block() as block:

            @block.sync
            def _(sp):
                for (col, tiles), t0 in zip(spans, firsts):
                    with sp.Fori(0, tiles // 2) as i:
                        for s in range(2):
                            sp.wait_ge(w_lo_2_ahead, i * 2 + (t0 + s + 1))
                            sp.dma_start(ring.raw[s][:], w.rearrange("(k p) n -> p k n", p=P)[
                                :, :, bass.ds(i * (2 * P) + (col + s * P), P)]).then_inc(w_in[s], 16)

            @block.scalar
            def _(act):
                for (col, tiles), t0 in zip(spans, firsts):
                    with act.Fori(0, tiles // 2) as i:
                        for s in range(2):
                            act.wait_ge(w_in[s], i * 16 + (t0 // 2 + 1) * 16)
                            act.wait_ge(multiplied_2_ahead, i * 2 + (t0 + s + 1))
                            act.copy(ring.hi[s][:], ring.raw[s][:]).then_inc(w_hi, 1)

            @block.vector
            def _(dve):
                dve.sem_inc(w_lo_2_ahead, 2)
                dve.sem_inc(copied_2_ahead, 2)
                for (col, tiles), t0 in zip(spans, firsts):
                    with dve.Fori(0, tiles // 2) as i:
                        for s in range(2):
                            dve.wait_ge(w_hi, i * 2 + (t0 + s + 1))
                            dve.tensor_tensor(ring.lo[s][:], ring.raw[s][:], ring.hi[s][:].bitcast(F32),
                                              ALU.subtract).then_inc(w_lo_2_ahead, 1)
                        for s in range(2):
                            dve.wait_ge(multiplied_2_ahead, i * 2 + (t0 + s + 3))
                            dve.tensor_copy(out[:, bass.ds(i * 2 + (t0 + s), 1), :].rearrange(
                                "p a (g t) -> p (a g) t", g=NG), ps[s][:, :, 0:TG]).then_inc(copied_2_ahead, 1)

            @block.tensor
            def _(pe):
                pe.sem_inc(multiplied_2_ahead, 2)
                for (col, tiles), t0 in zip(spans, firsts):
                    with pe.Fori(0, tiles // 2) as i:
                        for s in range(2):
                            pe.wait_ge(w_lo_2_ahead, i * 2 + (t0 + s + 3))
                            pe.wait_ge(copied_2_ahead, i * 2 + (t0 + s + 1))
                            for k in range(KD):
                                for n, (a, b) in enumerate(((ring.hi, hi), (ring.hi, lo), (ring.lo, hi))):
                                    for g in range(NG):
                                        last = pe.matmul(ps[s][:, g, 0:TG], a[s][:, k],
                                                         b[:, k, g * TG:(g + 1) * TG],
                                                         start=(k == 0 and n == 0),
                                                         stop=(k == KD - 1 and n == 2))
                            last.then_inc(multiplied_2_ahead, 1)


def project_rows(nc, m, hi, lo):
    with Phase(nc) as ctx:
        at = nc.alloc_sbuf_tensor_at
        raw = at("wv_raw", [P, KD, NV], F32, offset=O_PROJ)
        w_hi = at("wv_hi", [P, KD, NV], F32R, offset=O_PROJ + KD * NV * 4)
        w_lo = at("wv_lo", [P, KD, NV], F32R, offset=O_PROJ + 2 * KD * NV * 4)
        ps = ctx.enter_context(nc.psum_tensor("ps_rows", [P, 4, 512], F32))
        w_in, hi_cut, lo_cut, multiplied, copied = semaphores(
            nc, ctx, "wv_in", "wv_hi_cut", "wv_lo_cut", "rows_multiplied", "rows_copied")
        w = m.w_in[0].rearrange("(k p) n -> p k n", p=P)
        cleared, = semaphores(nc, ctx, "rows_cleared")
        with nc.Block() as block:

            @block.gpsimd
            def _(pool):
                pool.memset(m.vtok[:, NC], 0.0).then_inc(cleared, 1)

            @block.sync
            def _(sp):
                for k in range(KD):
                    sp.dma_start(raw[:, k, 0:DW + H], w[:, k, COL_VC:N_IN]).then_inc(w_in, 16)
                sp.dma_start(raw[:, :, DW + H:NV], w[:, :, COL_BETA:COL_QC]).then_inc(w_in, 16)

            @block.scalar
            def _(act):
                act.wait_ge(w_in, 16 * (KD + 1))
                for k in range(KD):
                    act.copy(w_hi[:, k], raw[:, k]).then_inc(hi_cut, 1)

            @block.vector
            def _(dve):
                for k in range(KD):
                    dve.wait_ge(hi_cut, k + 1)
                    dve.tensor_tensor(w_lo[:, k], raw[:, k], w_hi[:, k].bitcast(F32), ALU.subtract).then_inc(lo_cut, 1)
                for c in range(NC + 1):
                    rows = P if c < NC else NS
                    dve.wait_ge(multiplied, c + 1)
                    if c == NC:
                        dve.wait_ge(cleared, 1)
                    dve.tensor_copy(m.vtok[0:rows, c], ps[0:rows, c % 4, 0:NV]).then_inc(copied, 1)

            @block.tensor
            def _(pe):
                for c in range(NC + 1):
                    rows = P if c < NC else NS
                    if c >= 4:
                        pe.wait_ge(copied, c - 3)
                    for k in range(KD):
                        if c == 0:
                            pe.wait_ge(lo_cut, k + 1)
                        for n, (a, b) in enumerate(((hi, w_hi), (lo, w_hi), (hi, w_lo))):
                            last = pe.matmul(ps[0:rows, c % 4, 0:NV], a[:, k, c * P:c * P + rows], b[:, k],
                                             start=(k == 0 and n == 0), stop=(k == KD - 1 and n == 2))
                    last.then_inc(multiplied, 1)


def convolve(nc, m):
    with Phase(nc) as ctx:
        at = nc.alloc_sbuf_tensor_at
        off = O_H + KD * T * 4
        pad = at("cv_pad", [P, 2, KA - 1 + SEQ], F32, offset=off)
        off += (2 * (KA - 1 + SEQ) * 4 + 31) // 32 * 32
        acc = at("cv_acc", [P, 3, T], F32, offset=off)
        off += 3 * T * 4
        sa_rows = at("cv_sa_rows", [4 * (KA - 1), 2, CA], F32, offset=off)
        sb_rows = at("cv_sb_rows", [NS * (KB - 1), 3 * DW], F32, offset=off + 2048)
        sa = at("cv_sa", [P, 2, NS, KA - 1], F32, offset=off + 6656)
        sb = at("cv_sb", [P, 9, NS, KB - 1], F32, offset=off + 8576)
        tap_a = at("cv_tap_a", [P, NS, KA - 1], F32, offset=off + 9440)
        part = at("cv_part", [P, NS], F32, offset=off + 10400)
        part_b = at("cv_part_b", [P, 9 * NS], F32, offset=off + 10432)
        tap_b = at("cv_tap_b", [P, 9, NS, KB - 1], F32, offset=off + 21344)
        a_rows = at("cv_a_rows", [KA - 1 + NS, CA], F32, offset=off + 10720)
        b_rows = at("cv_b_rows", [KB - 1 + NS, 3 * DW], F32, offset=off + 11744)
        k_rows = at("cv_k_rows", [P, 2, DW], F32, offset=off + 16384)
        small = at("cv_small", [TT, 3, NT * 2 * H], F32, offset=off + 19456)
        small_a = at("cv_small_a", [TT, 3, NT], F32, offset=off + 21184)
        assert off + 22208 <= O_END
        a_val, gate = m.proj[:, T_A:T_A + 2], m.proj[:, T_GATE:T_GATE + 2]
        ps_state = ctx.enter_context(nc.psum_tensor("cv_ps_state", [P, 2, 512], F32))
        ps_rows = ctx.enter_context(nc.psum_tensor("cv_ps_rows", [P, 3, 512], F32))
        ps_k = ctx.enter_context(nc.psum_tensor("cv_ps_k", [P, 2, 512], F32))
        ps_a = ctx.enter_context(nc.psum_tensor("cv_ps_a", [P, 512], F32))
        names = ("states_in", "states_turned", "states_copied", "gated", "u_done", "padded", "a_conv", "a_turned",
                 "a_rows_done", "b_turned", "b_rows_done", "k_turned", "k_copied", "b_conv", "b_silu_3_ahead", "b_squared",
                 "b_summed", "b_eps", "b_rooted", "b_inverted", "b_inv_turned", "b_inv_copied", "b_spread", "b_normed", "chain", "z_silu",
                 "a_mean", "a_centred", "a_squared", "a_summed", "a_eps", "a_rooted", "a_inverted", "a_spread",
                 "a_scaled", "zeroed", "stored")
        (states_in, states_turned, states_copied, gated, u_done, padded, a_conv, a_turned, a_rows_done, b_turned,
         b_rows_done, k_turned, k_copied, b_conv, b_silu_3_ahead, b_squared, b_summed, b_eps, b_rooted, b_inverted, b_inv_turned, b_inv_copied, b_spread,
         b_normed, chain, z_silu, a_mean, a_centred, a_squared, a_summed, a_eps, a_rooted, a_inverted,
         a_spread, a_scaled, zeroed, stored) = semaphores(nc, ctx, *["cv_" + n for n in names])
        k_stored = semaphores(nc, ctx, "cv_k_stored0", "cv_k_stored1")
        grouped = lambda x: x.rearrange("p (g t) -> p g t", g=NG)
        w_a = lambda j, tap, n=1: m.cols_a[:, CONV_A_W + 2 * tap + j:CONV_A_W + 2 * (tap + n - 1) + j + 1:2]
        w_b = lambda j, tap, n=1: m.cols_b[:, 9 * tap + j:9 * (tap + n - 1) + j + 1:9]
        y_a = m.yT[:, 0:2]
        with nc.Block() as block:

            @block.sync
            def _(sp):
                for e in range(2):
                    sp.dma_start(sa_rows[:, e], m.state_conv_a[0, e * 4:(e + 1) * 4].rearrange(
                        "b w c -> (b w) c")).then_inc(states_in, 16)
                sp.dma_start(sb_rows[:], m.state_conv_b[0].rearrange("b w c -> (b w) c")).then_inc(states_in, 16)
                sp.dma_start(m.o_conv_a_s[0, :, 0:KA - 2], m.state_conv_a[0, :, 1:KA - 1]).then_inc(stored, 16)
                sp.dma_start(m.o_conv_b_s[0, :, 0:KB - 2], m.state_conv_b[0, :, 1:KB - 1]).then_inc(stored, 16)
                sp.wait_ge(b_rows_done, 1)
                sp.dma_start(m.o_conv_b_p[0, 0], b_rows[0:KB - 1]).then_inc(stored, 16)
                sp.dma_start(m.o_conv_b_s[0, :, KB - 2], b_rows[KB - 1:KB - 1 + NS]).then_inc(stored, 16)
                sp.wait_ge(a_rows_done, 1)
                sp.dma_start(m.o_conv_a_p[0, 0], a_rows[0:KA - 1]).then_inc(stored, 16)
                sp.dma_start(m.o_conv_a_s[0, :, KA - 2], a_rows[KA - 1:KA - 1 + NS]).then_inc(stored, 16)
                sp.dma_start(m.o_v_p[0, 0].rearrange("(c p) h d -> p c (h d)", p=P), m.vtok[:, 0:NC, 0:DW]).then_inc(
                    stored, 16)
                sp.dma_start(m.o_v_s[0, :, 0].rearrange("b h d -> b (h d)"), m.vtok[0:NS, NC, 0:DW]).then_inc(
                    stored, 16)
                for c in range(NC + 1):
                    sp.wait_ge(k_copied, c + 1)
                    if c < NC:
                        sp.dma_start(m.o_k_p[0, 0, c * P:(c + 1) * P].rearrange("t h d -> t (h d)"),
                                     k_rows[:, c % 2]).then_inc(k_stored[c % 2], 16)
                    else:
                        sp.dma_start(m.o_k_s[0, :, 0].rearrange("b h d -> b (h d)"),
                                     k_rows[0:NS, c % 2]).then_inc(k_stored[c % 2], 16)
                sp.wait_ge(k_stored[0], 16 * 5)
                sp.wait_ge(k_stored[1], 16 * 4)
                sp.wait_ge(stored, 16 * 8)

            @block.tensor
            def _(pe):
                for j in range(9):
                    last = pe.transpose(ps_rows[0:11, j // 3, j % 3 * P:j % 3 * P + P],
                                        m.proj[:, T_QB + j, SEQ - KB + 1:T], m.ident[:])
                last.then_inc(b_turned, 1)
                pe.wait_ge(states_in, 48)
                for e in range(2):
                    for j in range(2):
                        pe.transpose(ps_state[:, 0, (2 * j + e) * 120:(2 * j + e + 1) * 120],
                                     sa_rows[:, e, j * P:(j + 1) * P], m.ident[0:120, 0:120])
                for j in range(9):
                    last = pe.transpose(ps_state[:, 1, j * 24:(j + 1) * 24], sb_rows[:, j * P:(j + 1) * P],
                                        m.ident[0:24, 0:24])
                last.then_inc(states_turned, 1)
                pe.wait_ge(u_done, 1)
                for j in range(2):
                    last = pe.transpose(ps_a[0:KA - 1 + NS, j * P:(j + 1) * P], a_val[:, j, SEQ - KA + 1:T], m.ident[:])
                last.then_inc(a_turned, 1)
                for c in range(NC + 1):
                    rows = P if c < NC else NS
                    if c >= 2:
                        pe.wait_ge(k_copied, c - 1)
                    for j in range(PAIRS):
                        last = pe.transpose(ps_k[0:rows, c % 2, j * P:(j + 1) * P],
                                            m.proj[:, T_KC + j, c * P:c * P + rows], m.ident[:])
                    last.then_inc(k_turned, 1)
                pe.wait_ge(k_copied, NC)
                for j in range(6):
                    pe.wait_ge(b_squared, j + 1)
                    for c in range(NT):
                        last = pe.matmul(ps_k[0:TT, 0, c * 12 + 2 * j:c * 12 + 2 * j + 2],
                                         acc[:, j % 3, c * TT:(c + 1) * TT], m.head_ones[:, 0:P:HD],
                                         start=True, stop=True)
                    last.then_inc(b_summed, 1)
                pe.wait_ge(b_inverted, 1)
                for c in range(NT):
                    g, t = divmod(c * TT, TG)
                    last = pe.transpose(ps_rows[0:2 * H, g, t:t + TT], small[:, 1, c * 2 * H:(c + 1) * 2 * H],
                                        m.ident[0:TT, 0:TT])
                last.then_inc(b_inv_turned, 1)
                pe.wait_ge(b_inv_copied, 1)
                for j in range(6):
                    if j >= 1:
                        pe.wait_ge(b_normed, j)
                    for g in range(NG):
                        last = pe.matmul(ps_rows[:, g, 0:TG], m.head_rows[:, j], acc[0:2 * H, 0, g * TG:(g + 1) * TG],
                                         start=True, stop=True)
                    last.then_inc(b_spread, 1)
                pe.wait_ge(a_conv, 2 * KA)
                pe.wait_ge(b_normed, 6)
                for j in range(2):
                    for g in range(NG):
                        last = pe.matmul(ps_rows[:, g, 0:TG], m.ones[:], y_a[:, j, g * TG:(g + 1) * TG],
                                         start=(j == 0), stop=(j == 1))
                last.then_inc(a_mean, 1)
                for j in range(2):
                    pe.wait_ge(a_squared, j + 1)
                    for c in range(NT):
                        last = pe.matmul(ps_k[0:TT, 1, c:c + 1], acc[:, j, c * TT:(c + 1) * TT], m.ones[:, 0:1],
                                         start=(j == 0 and c == 0), stop=(j == 1), skip_group_check=True)
                last.then_inc(a_summed, 1)
                pe.wait_ge(a_inverted, 1)
                spread_tokens(pe, m, ps_rows, small_a[:, 1]).then_inc(a_spread, 1)

            @block.scalar
            def _(act):
                act.sem_inc(b_silu_3_ahead, 3)
                act.activation(gate, gate, ACT.Sigmoid).then_inc(gated, 1)
                act.wait_ge(b_turned, 1)
                for g in range(NG):
                    last = act.copy(b_rows[:, g * DW:(g + 1) * DW], ps_rows[0:11, g, 0:DW])
                last.then_inc(b_rows_done, 1)
                act.wait_ge(states_turned, 1)
                act.copy(sa[:].rearrange("p j b w -> p (j b w)"), ps_state[:, 0, 0:480])
                act.copy(sb[:].rearrange("p j b w -> p (j b w)"), ps_state[:, 1, 0:216]).then_inc(states_copied, 1)
                act.wait_ge(u_done, 1)
                act.copy(pad[:, :, KA - 1:], a_val[:, :, 0:SEQ]).then_inc(padded, 1)
                act.wait_ge(a_turned, 1)
                act.copy(a_rows[:], ps_a[0:KA - 1 + NS, 0:CA]).then_inc(a_rows_done, 1)
                for c in range(NC + 1):
                    rows = P if c < NC else NS
                    act.wait_ge(k_turned, c + 1)
                    if c >= 2:
                        act.wait_ge(k_stored[c % 2], 16 * (c // 2))
                    act.copy(k_rows[0:rows, c % 2], ps_k[0:rows, c % 2, 0:DW]).then_inc(k_copied, 1)
                for j in range(3):
                    act.activation(m.proj[:, T_Z + j], m.proj[:, T_Z + j], ACT.Silu).then_inc(z_silu, 1)
                with act.Fori(0, 3) as i:
                    for s in range(3):
                        act.wait_ge(b_conv, i * 15 + 5 * (s + 1))
                        act.activation(m.proj[:, bass.ds(i * 3 + (T_QB + s), 1), :].rearrange("p a t -> p (a t)"),
                                       acc[:, s], ACT.Silu).then_inc(b_silu_3_ahead, 1)
                for j in range(6):
                    if j >= 3:
                        act.wait_ge(b_summed, j - 2)
                    else:
                        act.wait_ge(b_silu_3_ahead, 3 + 7 + j)
                    act.activation(acc[:, j % 3], m.proj[:, T_QB + j], ACT.Square).then_inc(b_squared, 1)
                act.wait_ge(b_eps, 1)
                act.activation(small[:, 1], small[:, 0], ACT.Sqrt).then_inc(b_rooted, 1)
                act.wait_ge(b_inv_turned, 1)
                act.copy(grouped(acc[0:2 * H, 0]), ps_rows[0:2 * H, :, 0:TG]).then_inc(b_inv_copied, 1)
                for j in range(2):
                    act.wait_ge(a_centred, j + 1)
                    act.activation(acc[:, j], y_a[:, j], ACT.Square).then_inc(a_squared, 1)
                root(act, small_a, a_eps).then_inc(a_rooted, 1)
                for j in range(2):
                    act.wait_ge(a_scaled, j + 1)
                    act.activation(y_a[:, j], y_a[:, j], ACT.Silu, scale=m.cols_a[:, LN_G + j:LN_G + j + 1],
                                   bias=m.cols_a[:, LN_B + j:LN_B + j + 1])

            @block.gpsimd
            def _(pool):
                pool.memset(pad[:, :, 0:KA - 1], 0.0).then_inc(zeroed, 1)

            @block.vector
            def _(dve):
                step = Chain(dve, chain)
                dve.wait_ge(gated, 1)
                dve.tensor_tensor(a_val, a_val, gate, ALU.mult).then_inc(u_done, 1)

                dve.wait_ge(states_copied, 1)
                for j in range(2):
                    step(dve.tensor_tensor(tap_a[:], sa[:, j], w_a(j, 0, KA - 1).unsqueeze(1).broadcast_to(
                        [P, NS, KA - 1]), ALU.mult))
                    step(dve.tensor_reduce(part[:], tap_a[:], AX_X, ALU.add))
                    step(dve.scalar_tensor_tensor(out=part[:], in0=a_val[:, j, SEQ:T], scalar=w_a(j, KA - 1),
                                                  in1=part[:], op0=ALU.mult, op1=ALU.add))
                    step(dve.tensor_scalar(y_a[:, j, SEQ:T], part[:], m.cols_a[:, CONV_A_B + j:CONV_A_B + j + 1],
                                           None, ALU.add))
                for j in range(9):
                    last = dve.tensor_tensor(tap_b[:, j], sb[:, j], w_b(j, 0, KB - 1).unsqueeze(1).broadcast_to(
                        [P, NS, KB - 1]), ALU.mult)
                step(last)
                step(dve.tensor_reduce(part_b[:], tap_b[:].rearrange("p j b w -> p (j b) w"), AX_X, ALU.add))

                dve.wait_ge(b_turned, 1)
                with dve.Fori(0, 3) as i:
                    for s in range(3):
                        tile = m.proj[:, bass.ds(i * 3 + (T_QB + s), 1), :].rearrange("p a t -> p (a t)")
                        w = lambda tap: m.cols_b[:, bass.ds(i * 3 + (9 * tap + s), 1)]
                        dve.wait_ge(b_silu_3_ahead, i * 3 + (s + 1))
                        dve.tensor_scalar(acc[:, s, 0:T], tile, w(3), None, ALU.mult).then_inc(b_conv, 1)
                        for n, tap in enumerate((2, 1, 0)):
                            dve.wait_ge(b_conv, i * 15 + (s * 5 + n + 1))
                            dve.scalar_tensor_tensor(out=acc[:, s, n + 1:SEQ], in0=tile[:, 0:SEQ - n - 1],
                                                     scalar=w(tap), in1=acc[:, s, n + 1:SEQ],
                                                     op0=ALU.mult, op1=ALU.add).then_inc(b_conv, 1)
                        dve.tensor_tensor(acc[:, s, SEQ:T], acc[:, s, SEQ:T], part_b[:, bass.ds(i * 24 + s * 8, NS)],
                                          ALU.add).then_inc(b_conv, 1)

                dve.wait_ge(zeroed, 1)
                dve.wait_ge(padded, 1)
                for j in range(2):
                    dve.tensor_scalar(y_a[:, j, 0:SEQ], pad[:, j, 0:SEQ], w_a(j, 0),
                                      m.cols_a[:, CONV_A_B + j:CONV_A_B + j + 1], ALU.mult, ALU.add).then_inc(a_conv, 1)
                with dve.Fori(1, KA) as tap:
                    for j in range(2):
                        dve.wait_ge(a_conv, tap * 2 + (j - 1))
                        dve.scalar_tensor_tensor(
                            out=y_a[:, j, 0:SEQ], in0=pad[:, j, bass.ds(tap, SEQ)],
                            scalar=m.cols_a[:, bass.ds(tap * 2 + (CONV_A_W + j), 1)], in1=y_a[:, j, 0:SEQ],
                            op0=ALU.mult, op1=ALU.add).then_inc(a_conv, 1)

                dve.wait_ge(b_summed, 6)
                dve.tensor_scalar(small[:, 0], ps_k[0:TT, 0, 0:NT * 2 * H], 1e-6, None, ALU.add).then_inc(b_eps, 1)
                inverse_root(dve, step, small, b_rooted).then_inc(b_inverted, 1)
                for j in range(6):
                    dve.wait_ge(b_spread, j + 1)
                    tile = grouped(m.proj[:, T_QB + j])
                    dve.scalar_tensor_tensor(out=tile, in0=tile, scalar=SCALE if j < 3 else 1.0,
                                             in1=ps_rows[:, :, 0:TG], op0=ALU.mult, op1=ALU.mult).then_inc(b_normed, 1)

                dve.wait_ge(a_mean, 1)
                for j in range(2):
                    dve.scalar_tensor_tensor(out=grouped(y_a[:, j]), in0=ps_rows[:, :, 0:TG], scalar=-1.0 / CA,
                                             in1=grouped(y_a[:, j]), op0=ALU.mult, op1=ALU.add).then_inc(a_centred, 1)
                dve.wait_ge(a_summed, 1)
                dve.tensor_scalar(small_a[:, 0], ps_k[0:TT, 1, 0:NT], 1.0 / CA, LN_EPS, ALU.mult, ALU.add).then_inc(
                    a_eps, 1)
                inverse_root(dve, step, small_a, a_rooted).then_inc(a_inverted, 1)
                dve.wait_ge(a_spread, 1)
                for j in range(2):
                    dve.tensor_tensor(grouped(y_a[:, j]), grouped(y_a[:, j]), ps_rows[:, :, 0:TG],
                                      ALU.mult).then_inc(a_scaled, 1)


def gates(nc, m):
    with Phase(nc) as ctx:
        off = O_H + KD * T * 4
        at = nc.alloc_sbuf_tensor_at
        n = NC + 1
        x = at("gt_x", [P, n, 2 * H], F32, offset=off)
        e = at("gt_e", [P, n, 2 * H], F32, offset=off + 512)
        w = at("gt_w", [P, n, 2 * H], F32, offset=off + 1024)
        ln = at("gt_ln", [P, n, 2 * H], F32, offset=off + 1536)
        rate = at("gt_rate", [P, H], F32, offset=off + 2048)
        b = at("gt_b", [P, n, H], F32, offset=off + 2080)
        args, exps, ones, logs, chain, stored, done = semaphores(
            nc, ctx, "gt_args", "gt_exps", "gt_ones", "gt_logs", "gt_chain", "gt_stored", "gt_done")
        spread = lambda v: v.unsqueeze(1).broadcast_to([P, n, H])
        raw = m.vtok[:, :, DW:NV]
        with nc.Block() as block:

            @block.sync
            def _(sp):
                sp.wait_ge(done, 1)
                sp.dma_start(m.o_f_p[0, 0].rearrange("(c p) h -> p c h", p=P), m.gates[:, 0:NC, 0:H]).then_inc(
                    stored, 16)
                sp.dma_start(m.o_f_s[0, :, 0], m.gates[0:NS, NC, 0:H]).then_inc(stored, 16)
                sp.wait_ge(stored, 32)

            @block.scalar
            def _(act):
                act.activation(rate[:], m.rows6[:, H:2 * H], ACT.Exp).then_inc(exps, 1)
                act.activation(b[:], raw[:, :, H:2 * H], ACT.Exp, scale=-1.0).then_inc(exps, 1)
                act.wait_ge(args, 1)
                act.activation(e[:], w[:], ACT.Exp, scale=-1.0).then_inc(exps, 1)
                act.wait_ge(ones, 1)
                act.activation(ln[:], w[:], ACT.Ln).then_inc(logs, 1)

            @block.vector
            def _(dve):
                step = Chain(dve, chain)
                step(dve.tensor_tensor(x[:, :, 0:H], raw[:, :, 0:H], spread(m.rows6[:, 0:H]), ALU.add))
                step(dve.tensor_scalar(x[:, :, 0:H], x[:, :, 0:H], -1.0, None, ALU.mult))
                step(dve.tensor_tensor(x[:, :, H:2 * H], raw[:, :, 2 * H:3 * H], spread(m.rows6[:, 2 * H:3 * H]),
                                       ALU.add))
                step(dve.scalar_tensor_tensor(out=w[:], in0=x[:], scalar=-1.0, in1=x[:], op0=ALU.mult, op1=ALU.max))
                dve.sem_inc(args, 1)
                dve.wait_ge(exps, 3)
                step(dve.tensor_scalar(w[:], e[:], 1.0, None, ALU.add))
                dve.sem_inc(ones, 1)
                dve.wait_ge(logs, 1)
                step(dve.scalar_tensor_tensor(out=e[:], in0=w[:], scalar=-1.0, in1=e[:], op0=ALU.add,
                                              op1=ALU.subtract))
                step(dve.reciprocal(w[:], w[:]))
                step(dve.tensor_tensor(e[:], e[:], w[:], ALU.mult))
                step(dve.tensor_tensor(ln[:], ln[:], e[:], ALU.subtract))
                step(dve.scalar_tensor_tensor(out=ln[:], in0=x[:], scalar=0.0, in1=ln[:], op0=ALU.max, op1=ALU.add))
                step(dve.tensor_scalar(m.gates[:, :, 0:H], ln[:, :, 0:H], -1.0, None, ALU.mult))
                dve.sem_inc(done, 1)
                step(dve.tensor_scalar(rate[:], rate[:], -1.0, None, ALU.mult))
                step(dve.tensor_tensor(m.gates[:, :, H:2 * H], ln[:, :, H:2 * H], spread(rate[:]), ALU.mult))
                step(dve.tensor_scalar(b[:], b[:], 1.0, None, ALU.add))
                step(dve.reciprocal(m.gates[:, :, 2 * H:3 * H], b[:]))


def delta_rule(nc, m):
    with Phase(nc) as ctx:
        off = O_H + KD * T * 4

        def put(name, shape):
            nonlocal off
            t = nc.alloc_sbuf_tensor_at("dl_" + name, shape, F32, offset=off)
            n = 4
            for d in shape[1:]:
                n *= d
            off += (n + 31) // 32 * 32
            return t

        qkv = put("qkv", [P, 9, P])
        gb = put("gb", [P, 2 * H])
        cums = put("cums", [P, 3 * H])
        exps = put("exps", [P, 3 * H])
        beta_exp = put("beta_exp", [P, H])
        decay = put("decay", [P, 2, 3, P])
        beta_decay = put("beta_decay", [P, 2, 3, P])
        lower_t = put("lower_t", [P, 2, 3, P])
        qk_t = put("qk_t", [P, 2, 3, P])
        y = put("y", [P, 2, 3, P])
        t_tt = put("t_tt", [P, 2, 2, 3, P])
        rhs = put("rhs", [P, H, P])
        k_decayed = put("k_decayed", [P, H, HD])
        q_exp = put("q_exp", [P, PAIRS, P])
        q_decayed = put("q_decayed", [P, PAIRS, P])
        neg_w = put("neg_w", [P, PAIRS, P])
        v_new = put("v_new", [P, 2, 3, HD])
        assert off <= O_END
        ps = ctx.enter_context(nc.psum_tensor("dl_ps", [P, 8, 512], F32))
        three = lambda b: ps[:, b, 0:3 * P].rearrange("p (m t) -> p m t", m=3)
        bx = lambda e: three(e)
        btt = lambda e, n: three(2 + 2 * e + n)
        bs = lambda e: three(6 + e)
        half = lambda e: slice(e * HD, (e + 1) * HD)
        LEVELS = 6
        names = ("staged_1", "gate_staged", "cum_ready", "exp_ready", "beta_ready", "prod_ready", "diff_done",
                 "decay_done", "q_exp_done", "beta_used", "lower_done", "qk_done", "lower_turned", "t_init", "tt_init",
                 "kv_turned_1", "rhs_done", "x_done", "y_done", "tt_done", "t_done", "w_done", "neg_w_done",
                 "v_done", "v_copied", "q_decayed_1", "o_done", "o_copied_2", "s_done", "s_updated_1", "chain",
                 "s_zero", "final_stored", "cums_copied")
        (staged, gate_staged, cum_ready, exp_ready, beta_ready, prod_ready, diff_done, decay_done, q_exp_done,
         beta_used, lower_done, qk_done, lower_turned, t_init, tt_init, kv_turned_1, rhs_done, x_done, y_done,
         tt_done, t_done, w_done, neg_w_done, v_done, v_copied, q_decayed_1, o_done, o_copied_2, s_done,
         s_updated_1, chain, s_zero, final_stored, cums_copied) = semaphores(nc, ctx, *["dl_" + n for n in names])
        with nc.Block() as block:

            @block.sync
            def _(sp):
                sp.wait_ge(s_updated_1, NC + 1)
                for e in range(2):
                    sp.dma_start(m.o_delta_p[0, 0].rearrange("(m e) k v -> e k m v", e=2)[e],
                                 m.state[half(e)]).then_inc(final_stored, 16)
                sp.wait_ge(final_stored, 32)

            @block.scalar
            def _(act):
                act.sem_inc(o_copied_2, 2)
                with act.Fori(0, NC) as c:
                    act.wait_ge(kv_turned_1, c + 1)
                    act.wait_ge(q_decayed_1, c + 1)
                    act.copy(qkv[:], m.proj[:, T_QB:T_QB + 9, bass.ds(c * P, P)]).then_inc(staged, 1)
                    act.wait_ge(cums_copied, c + 1)
                    act.wait_ge(s_updated_1, c + 1)
                    act.activation(exps[:], cums[:], ACT.Exp).then_inc(exp_ready, 1)
                    for e in range(2):
                        act.wait_ge(diff_done, c * 2 + (e + 1))
                        act.activation(q_exp[half(e)], bx(e)[half(e)], ACT.Exp).then_inc(q_exp_done, 1)
                        act.activation(decay[:, e], decay[:, e], ACT.Exp).then_inc(decay_done, 1)
                    for lv in range(LEVELS):
                        for e in range(2):
                            act.wait_ge(tt_done, c * (2 * LEVELS) + (2 * lv + e + 1))
                            if lv < LEVELS - 1:
                                act.copy(t_tt[:, e].rearrange("p n m t -> p n (m t)"),
                                         ps[:, 2 + 2 * e:4 + 2 * e, 0:3 * P]).then_inc(t_done, 1)
                            else:
                                act.copy(t_tt[:, e, 1], btt(e, 1)).then_inc(t_done, 1)
                    for e in range(2):
                        act.wait_ge(w_done, c * 2 + (e + 1))
                        act.mul(neg_w[half(e)], bs(e)[half(e)], -1.0).then_inc(neg_w_done, 1)
                    for e in range(2):
                        act.wait_ge(v_done, c * 2 + (e + 1))
                        act.copy(v_new[:, e], bx(e)[:, :, 0:HD]).then_inc(v_copied, 1)
                    for e in range(2):
                        act.wait_ge(o_done, c * 2 + (e + 1))
                        act.copy(m.yT[half(e), 2:2 + PAIRS, bass.ds(c * P, P)], bs(e)[half(e)]).then_inc(o_copied_2, 1)

            @block.gpsimd
            def _(pool):
                pool.sem_inc(q_decayed_1, 1)
                with pool.Fori(0, NC) as c:
                    pool.wait_ge(q_exp_done, c * 2 + 2)
                    pool.wait_ge(staged, c + 1)
                    pool.tensor_tensor(q_decayed[:], qkv[:, 0:3], q_exp[:], ALU.mult).then_inc(q_decayed_1, 1)
                    for e in range(2):
                        pool.wait_ge(lower_done, c * 2 + (e + 1))
                        pool.tensor_tensor(t_tt[:, e, 1], lower_t[:, e],
                                           m.level1_t[:].unsqueeze(1).broadcast_to([P, 3, P]), ALU.mult).then_inc(
                                               chain, 1)
                        pool.wait_ge(chain, c * 2 + (e + 1))
                        pool.tensor_tensor(t_tt[:, e, 1], t_tt[:, e, 1],
                                           m.ident[:].unsqueeze(1).broadcast_to([P, 3, P]), ALU.add).then_inc(
                                               tt_init, 1)

            @block.vector
            def _(dve):
                dve.sem_inc(s_updated_1, 1)
                dve.memset(m.state[:], 0.0).then_inc(s_zero, 1)
                ident3 = m.ident[:].unsqueeze(1).broadcast_to([P, 3, P])
                mask3 = lambda lv: m.level_mask[:, lv].unsqueeze(1).broadcast_to([P, 3, P])
                dve.wait_ge(s_zero, 1)
                with dve.Fori(0, NC) as c:
                    dve.tensor_copy(gb[:].rearrange("p (a h) -> p a h", a=1),
                                    m.gates[:, bass.ds(c, 1), H:3 * H]).then_inc(gate_staged, 1)
                    dve.wait_ge(cum_ready, c + 1)
                    dve.tensor_copy(cums[:], ps[:, 5, 0:3 * H]).then_inc(cums_copied, 1)
                    dve.wait_ge(cums_copied, c + 1)
                    for e in range(2):
                        dve.wait_ge(beta_ready, c * 2 + (e + 1))
                        for i in range(3):
                            last = dve.scalar_tensor_tensor(
                                out=decay[:, e, i], in0=bx(e)[:, i], scalar=cums[:, 2 * i + e:2 * i + e + 1],
                                in1=m.keep_t[:], op0=ALU.subtract, op1=ALU.min)
                        last.then_inc(diff_done, 1)
                    for e in range(2):
                        dve.wait_ge(decay_done, c * 2 + (e + 1))
                        dve.tensor_tensor(beta_decay[:, e], bs(e), decay[:, e], ALU.mult).then_inc(beta_used, 1)
                        dve.wait_ge(prod_ready, c * 2 + (e + 1))
                        dve.wait_ge(beta_used, c * 2 + (e + 1))
                        dve.tensor_tensor(lower_t[:, e], btt(e, 0), beta_decay[:, e], ALU.mult).then_inc(lower_done, 1)
                        dve.tensor_tensor(qk_t[:, e], btt(e, 1), decay[:, e], ALU.mult).then_inc(qk_done, 1)
                    for e in range(2):
                        dve.wait_ge(lower_turned, c * 2 + (e + 1))
                        dve.tensor_tensor(t_tt[:, e, 0], bx(e), mask3(0), ALU.mult).then_inc(t_init, 1)
                        dve.wait_ge(t_init, c * 4 + (2 * e + 1))
                        dve.tensor_tensor(t_tt[:, e, 0], t_tt[:, e, 0], ident3, ALU.add).then_inc(t_init, 1)
                    for lv in range(LEVELS):
                        for e in range(2):
                            dve.wait_ge(x_done, c * (2 * LEVELS) + (2 * lv + e + 1))
                            dve.tensor_tensor(y[:, e], bx(e), mask3(lv + 1), ALU.mult).then_inc(y_done, 1)
                            dve.wait_ge(y_done, c * (4 * LEVELS) + (4 * lv + 2 * e + 1))
                            dve.tensor_tensor(y[:, e], y[:, e], ident3, ALU.add).then_inc(y_done, 1)
                        if lv == 0:
                            dve.wait_ge(exp_ready, c + 1)
                            dve.wait_ge(kv_turned_1, c + 2)
                            heads = lambda v: v.unsqueeze(2).broadcast_to([P, H, HD])
                            rows = lambda b: ps[:, b, 0:DW].rearrange("p (h d) -> p h d", h=H)
                            dve.tensor_tensor(beta_exp[:], gb[:, H:2 * H], exps[:, 0:H], ALU.mult).then_inc(rhs_done, 1)
                            dve.tensor_tensor(rhs[:, :, 0:HD], rows(7), heads(gb[:, H:2 * H]), ALU.mult).then_inc(
                                rhs_done, 1)
                            dve.tensor_tensor(k_decayed[:], rows(6), heads(exps[:, H:2 * H]), ALU.mult).then_inc(
                                rhs_done, 1)
                            dve.wait_ge(rhs_done, c * 4 + 1)
                            dve.tensor_tensor(rhs[:, :, HD:P], rows(6), heads(beta_exp[:]), ALU.mult).then_inc(
                                rhs_done, 1)
                    dve.wait_ge(s_done, c * 2 + 2)
                    for e in range(2):
                        dve.tensor_tensor(m.state[half(e)], m.state[half(e)],
                                          exps[half(e), 2 * H + e:3 * H:2].unsqueeze(2).broadcast_to([HD, PAIRS, HD]),
                                          ALU.mult).then_inc(s_zero, 1)
                    dve.wait_ge(s_zero, c * 4 + 3)
                    dve.tensor_tensor(m.state[half(0)], m.state[half(0)], btt(0, 0)[half(0), :, 0:HD], ALU.add).then_inc(
                        s_zero, 1)
                    dve.tensor_tensor(m.state[half(1)], m.state[half(1)], btt(1, 0)[half(1), :, 0:HD], ALU.add).then_inc(
                        s_zero, 1)
                    dve.wait_ge(s_zero, c * 4 + 5)
                    dve.sem_inc(s_updated_1, 1)

            @block.tensor
            def _(pe):
                pe.sem_inc(kv_turned_1, 1)
                with pe.Fori(0, NC) as c:
                    pe.wait_ge(gate_staged, c + 1)
                    pe.wait_ge(o_copied_2, c * 2 + 2)
                    for n, t in enumerate((m.cumul, m.later, m.ones)):
                        last = pe.matmul(ps[:, 5, n * H:(n + 1) * H], t[:], gb[:, 0:H],
                                         start=True, stop=True)
                    last.then_inc(cum_ready, 1)
                    for e in range(2):
                        for i in range(3):
                            h = 2 * i + e
                            pe.matmul(bx(e)[:, i], gb[:, h:h + 1].to_broadcast([P, P]), m.cumul[:], start=True, stop=True)
                            last = pe.matmul(bs(e)[:, i], gb[:, H + h:H + h + 1].to_broadcast([P, P]), m.ident[:],
                                             start=True, stop=True)
                        last.then_inc(beta_ready, 1)
                    pe.wait_ge(staged, c + 1)
                    pe.wait_ge(cums_copied, c + 1)
                    pe.wait_ge(s_updated_1, c + 1)
                    for e in range(2):
                        for i in range(3):
                            k = qkv[half(e), 3 + i]
                            pe.matmul(btt(e, 0)[:, i], k, k, start=True, stop=True)
                            last = pe.matmul(btt(e, 1)[:, i], k, qkv[half(e), i], start=True, stop=True)
                        last.then_inc(prod_ready, 1)
                    pe.wait_ge(beta_used, c * 2 + 2)
                    for i in range(3):
                        pe.transpose(bs(0)[:, i], qkv[:, 3 + i], m.ident[:])
                        last = pe.transpose(bs(1)[:, i], qkv[:, 6 + i], m.ident[:])
                    last.then_inc(kv_turned_1, 1)
                    for e in range(2):
                        pe.wait_ge(lower_done, c * 2 + (e + 1))
                        pe.wait_ge(q_exp_done, c * 2 + (e + 1))
                        for i in range(3):
                            last = pe.transpose(bx(e)[:, i], lower_t[:, e, i], m.ident[:])
                        last.then_inc(lower_turned, 1)
                    for lv in range(LEVELS):
                        for e in range(2):
                            if lv == 0:
                                pe.wait_ge(t_init, c * 4 + (2 * e + 2))
                                pe.wait_ge(tt_init, c * 2 + (e + 1))
                                pe.wait_ge(qk_done, c * 2 + (e + 1))
                            else:
                                pe.wait_ge(t_done, c * (2 * LEVELS) + (2 * lv + e - 1))
                            for i in range(3):
                                last = pe.matmul(bx(e)[:, i], lower_t[:, e, i], t_tt[:, e, 0, i], start=True, stop=True)
                            last.then_inc(x_done, 1)
                        for e in range(2):
                            pe.wait_ge(y_done, c * (4 * LEVELS) + (4 * lv + 2 * e + 2))
                            for i in range(3):
                                if lv < LEVELS - 1:
                                    pe.matmul(btt(e, 0)[:, i], t_tt[:, e, 1, i], y[:, e, i], start=True, stop=True)
                                last = pe.matmul(btt(e, 1)[:, i], y[:, e, i], t_tt[:, e, 1, i], start=True, stop=True)
                            last.then_inc(tt_done, 1)
                    pe.wait_ge(rhs_done, c * 4 + 4)
                    for e in range(2):
                        pe.wait_ge(t_done, c * (2 * LEVELS) + (2 * LEVELS - 1 + e))
                        for i in range(3):
                            last = pe.matmul(bs(e)[half(e), i], rhs[:, 2 * i + e, HD:P], t_tt[:, e, 1, i],
                                             start=True, stop=True)
                        last.then_inc(w_done, 1)
                    for e in range(2):
                        pe.wait_ge(neg_w_done, c * 2 + (e + 1))
                        for i in range(3):
                            pe.matmul(bx(e)[:, i, 0:HD], t_tt[:, e, 1, i], rhs[:, 2 * i + e, 0:HD],
                                      start=True, stop=False)
                            last = pe.matmul(bx(e)[:, i, 0:HD], neg_w[half(e), i], m.state[half(e), i],
                                             start=False, stop=True)
                        last.then_inc(v_done, 1)
                    pe.wait_ge(q_decayed_1, c + 2)
                    for e in range(2):
                        pe.wait_ge(v_copied, c * 2 + (e + 1))
                        for i in range(3):
                            pe.matmul(bs(e)[half(e), i], v_new[:, e, i], qk_t[:, e, i], start=True, stop=False)
                            last = pe.matmul(bs(e)[half(e), i], m.state[half(e), i], q_decayed[half(e), i],
                                             start=False, stop=True)
                        last.then_inc(o_done, 1)
                    for e in range(2):
                        for i in range(3):
                            last = pe.matmul(btt(e, 0)[half(e), i, 0:HD], k_decayed[:, 2 * i + e], v_new[:, e, i],
                                             start=True, stop=True)
                        last.then_inc(s_done, 1)


def delta_sample(nc, m):
    with Phase(nc) as ctx:
        off = O_H + KD * T * 4
        at = nc.alloc_sbuf_tensor_at
        state = at("ds_state", [P, NS, PAIRS, HD], F32, offset=off)
        x = at("ds_x", [P, NS, PAIRS, HD], F32, offset=off + 6144)
        v_rows = at("ds_v_rows", [NS, DW], F32, offset=off + 12288)
        ab = at("ds_ab", [NS, 2 * H], F32, offset=off + 13824)
        ab_all = at("ds_ab_all", [P, NS, 2 * H], F32, offset=off + 13888)
        sq = at("ds_sq", [P, PAIRS, T], F32, offset=off + 14272)
        small = at("ds_small", [TT, 3, NT * H], F32, offset=off + 14272 + PAIRS * T * 4)
        inv_rows = at("ds_inv_rows", [H, T], F32, offset=off + 27584)
        ps = ctx.enter_context(nc.psum_tensor("ds_ps", [P, 8, 512], F32))
        (states_in, decay_done, turned, rows_done, ab_turned, ab_done, ks_done, ks_used, v_spread, x_chain, o_done,
         o_copied, stored, squared, summed, with_eps, rooted, inverted, inv_turned, inv_copied, spread, normed,
         chain) = semaphores(
             nc, ctx, *["ds_" + n for n in (
                 "states_in", "decay_done", "turned", "rows_done", "ab_turned", "ab_done", "ks_done", "ks_used",
                 "v_spread", "x_chain", "o_done", "o_copied", "stored", "squared", "summed", "with_eps", "rooted",
                 "inverted", "inv_turned", "inv_copied", "spread", "normed", "chain")])
        half = lambda e: slice(e * HD, (e + 1) * HD)
        seq_banks = lambda e: ps[:, 3 * e:3 * e + 3].rearrange("p b n -> p (b n)").rearrange(
            "p (b m v) -> p b m v", b=NS, m=PAIRS)
        per_head = lambda e, c: ab_all[half(e), :, c + e:c + H:2].unsqueeze(3).broadcast_to([HD, NS, PAIRS, HD])
        with nc.Block() as block:

            @block.sync
            def _(sp):
                for e in range(2):
                    for i in range(PAIRS):
                        sp.dma_start(state[half(e), :, i], m.state_delta[0, :, 2 * i + e].rearrange(
                            "b k v -> k b v")).then_inc(states_in, 16)
                sp.wait_ge(x_chain, 12)
                for e in range(2):
                    for i in range(PAIRS):
                        sp.dma_start(m.o_delta_s[0, :, 2 * i + e].rearrange("b k v -> k b v"),
                                     state[half(e), :, i]).then_inc(stored, 16)
                sp.wait_ge(stored, 96)

            @block.tensor
            def _(pe):
                for i in range(PAIRS):
                    last = pe.transpose(ps[0:NS, 6, i * P:(i + 1) * P], m.proj[:, T_VB + i, SEQ:T], m.ident[:])
                last.then_inc(turned, 1)
                pe.wait_ge(decay_done, 2)
                for b in range(NS):
                    last = pe.matmul(ps[:, 7, b * 2 * H:(b + 1) * 2 * H], m.ident[0:NS, b:b + 1].to_broadcast([NS, P]),
                                     ab[:], start=True, stop=True)
                last.then_inc(ab_turned, 1)
                pe.wait_ge(states_in, 96)
                for e in range(2):
                    for b in range(NS):
                        for i in range(PAIRS):
                            k = m.proj[half(e), T_KB + i, SEQ + b:SEQ + b + 1].to_broadcast([HD, HD])
                            last = pe.matmul(seq_banks(e)[half(e), b, i], k, state[half(e), b, i], start=True, stop=True)
                last.then_inc(ks_done, 1)
                pe.wait_ge(rows_done, 1)
                pe.wait_ge(ks_used, 2)
                for e in range(2):
                    for b in range(NS):
                        for i in range(PAIRS):
                            h = 2 * i + e
                            last = pe.matmul(seq_banks(e)[:, b, i], m.ident[0:NS, b:b + 1].to_broadcast([NS, P]),
                                             v_rows[:, h * HD:(h + 1) * HD], start=True, stop=True)
                last.then_inc(v_spread, 1)
                pe.wait_ge(x_chain, 12)
                for e in range(2):
                    for b in range(NS):
                        for i in range(PAIRS):
                            last = pe.matmul(ps[half(e), 6 + e, i * NS + b:i * NS + b + 1], state[half(e), b, i],
                                             m.proj[half(e), T_QB + i, SEQ + b:SEQ + b + 1], start=True, stop=True)
                last.then_inc(o_done, 1)
                for i in range(PAIRS):
                    pe.wait_ge(squared, i + 1)
                    for c in range(NT):
                        last = pe.matmul(ps[0:TT, 3, c * H + 2 * i:c * H + 2 * i + 2], sq[:, i, c * TT:(c + 1) * TT],
                                         m.head_ones[:, 0:P:HD], start=True, stop=True)
                last.then_inc(summed, 1)
                pe.wait_ge(inverted, 1)
                for c in range(NT):
                    g, t = divmod(c * TT, TG)
                    last = pe.transpose(ps[0:H, g, t:t + TT], small[:, 1, c * H:(c + 1) * H], m.ident[0:TT, 0:TT])
                last.then_inc(inv_turned, 1)
                pe.wait_ge(inv_copied, 1)
                for i in range(PAIRS):
                    if i >= 1:
                        pe.wait_ge(normed, 2 * i - 1)
                    for g in range(NG):
                        last = pe.matmul(ps[:, g, 0:TG], m.head_rows[0:H, i], inv_rows[:, g * TG:(g + 1) * TG],
                                         start=True, stop=True)
                    last.then_inc(spread, 1)

            @block.scalar
            def _(act):
                act.copy(ab[:, H:2 * H], m.gates[0:NS, NC, 2 * H:3 * H]).then_inc(decay_done, 1)
                act.activation(ab[:, 0:H], m.gates[0:NS, NC, H:2 * H], ACT.Exp).then_inc(decay_done, 1)
                act.wait_ge(turned, 1)
                act.copy(v_rows[:], ps[0:NS, 6, 0:DW]).then_inc(rows_done, 1)
                act.wait_ge(ab_turned, 1)
                act.copy(ab_all[:].rearrange("p b n -> p (b n)"), ps[:, 7, 0:NS * 2 * H]).then_inc(ab_done, 1)
                act.wait_ge(o_done, 1)
                for e in range(2):
                    last = act.copy(m.yT[half(e), 2:2 + PAIRS, SEQ:T], ps[half(e), 6 + e, 0:PAIRS * NS].rearrange(
                        "p (m b) -> p m b", m=PAIRS)).then_inc(o_copied, 1)
                act.wait_ge(o_copied, 2)
                for i in range(PAIRS):
                    act.activation(sq[:, i], m.yT[:, 2 + i], ACT.Square).then_inc(squared, 1)
                root(act, small, with_eps).then_inc(rooted, 1)
                act.wait_ge(inv_turned, 1)
                act.copy(inv_rows[:].rearrange("p (g t) -> p g t", g=NG), ps[0:H, 0:NG, 0:TG]).then_inc(inv_copied, 1)

            @block.vector
            def _(dve):
                step = Chain(dve, chain)
                dve.wait_ge(ab_done, 1)
                dve.wait_ge(ks_done, 1)
                for e in range(2):
                    dve.tensor_tensor(x[half(e)], seq_banks(e)[half(e)], per_head(e, 0), ALU.mult).then_inc(ks_used, 1)
                dve.wait_ge(v_spread, 1)
                dve.wait_ge(ks_used, 2)
                for e in range(2):
                    dve.tensor_tensor(x[half(e)], seq_banks(e)[half(e)], x[half(e)], ALU.subtract).then_inc(x_chain, 1)
                dve.wait_ge(x_chain, 2)
                for e in range(2):
                    dve.tensor_tensor(x[half(e)], x[half(e)], per_head(e, H), ALU.mult).then_inc(x_chain, 1)
                dve.wait_ge(x_chain, 4)
                for e in range(2):
                    keys = m.proj[half(e), T_KB:T_KB + PAIRS, SEQ:T].rearrange("p m b -> p b m").unsqueeze(3)
                    dve.tensor_tensor(x[half(e)], x[half(e)], keys.broadcast_to([HD, NS, PAIRS, HD]),
                                      ALU.mult).then_inc(x_chain, 1)
                for e in range(2):
                    dve.tensor_tensor(state[half(e)], state[half(e)], per_head(e, 0), ALU.mult).then_inc(x_chain, 1)
                dve.wait_ge(x_chain, 8)
                for e in range(2):
                    dve.tensor_tensor(state[half(e)], state[half(e)], x[half(e)], ALU.add).then_inc(x_chain, 2)

                dve.wait_ge(summed, 1)
                dve.tensor_scalar(small[:, 0], ps[0:TT, 3, 0:NT * H], 1.0 / HD, RMS_EPS, ALU.mult, ALU.add).then_inc(
                    with_eps, 1)
                inverse_root(dve, step, small, rooted).then_inc(inverted, 1)
                for i in range(PAIRS):
                    dve.wait_ge(spread, i + 1)
                    tile = m.yT[:, 2 + i]
                    group = tile.rearrange("p (g t) -> p g t", g=NG)
                    dve.scalar_tensor_tensor(out=group, in0=group, scalar=m.cols_b[:, NORM_B_G:NORM_B_G + 1],
                                             in1=ps[:, 0:NG, 0:TG], op0=ALU.mult, op1=ALU.mult).then_inc(normed, 1)
                    dve.wait_ge(normed, 2 * i + 1)
                    dve.tensor_tensor(tile, tile, m.proj[:, T_Z + i], ALU.mult).then_inc(normed, 1)


def fox_prompt(nc, m):
    with Phase(nc) as ctx:
        off = O_H + KD * T * 4

        def put(name, shape):
            nonlocal off
            t = nc.alloc_sbuf_tensor_at("fx_" + name, shape, F32, offset=off)
            n = 4
            for d in shape[1:]:
                n *= d
            off += (n + 31) // 32 * 32
            return t

        before = put("before", [P, NC, H])
        neg_c = put("neg_c", [P, H, NC])
        neg_c2 = put("neg_c2", [P, 2, NC])
        q = put("q", [P, SEQ])
        k = put("k", [P, SEQ])
        v = put("v", [P, NC, P])
        bias = [put(f"bias{e}", [P, SEQ]) for e in range(2)]
        x = [put(f"x{s}", [P, SEQ]) for s in range(2)]
        pt = [put(f"pt{s}", [P, NC, P]) for s in range(2)]
        o = put("o", [P, NC, P])
        neg_max = put("neg_max", [P, 16])
        total = put("total", [P, 2, NC])
        assert off <= O_END
        ps_s = [ctx.enter_context(nc.psum_tensor(f"fx_s{s}", [P, 2 * 512], F32)) for s in range(2)]
        ps_t = [ctx.enter_context(nc.psum_tensor(f"fx_t{s}", [P, 512], F32)) for s in range(2)]
        ps_o = [ctx.enter_context(nc.psum_tensor(f"fx_o{e}", [P, NC, HD], F32)) for e in range(2)]
        (summed_before, cum_done, neg_c_done, staged, pair_done_1, bias_spread, bias_done, s_done, shifted, maxed,
         exp_done, turned, copied_dve, copied_act, pv_done, inv_done, o_scaled, o_turned, y_done, waited,
         mask_done) = semaphores(
             nc, ctx, *["fx_" + n for n in (
                 "summed_before", "cum_done", "neg_c_done", "staged", "pair_done_1", "bias_spread", "bias_done",
                 "s_done", "shifted", "maxed", "exp_done", "turned", "copied_dve", "copied_act", "pv_done",
                 "inv_done", "o_scaled", "o_turned", "y_done", "waited", "mask_done")])
        half = lambda e: slice(e * HD, (e + 1) * HD)
        units = [(e, i) for e in range(2) for i in reversed(range(NC))]
        U = len(units)
        groups, of_unit = [], []
        for u, (e, i) in enumerate(units):
            mine = [(u, b, min(b + 4, i + 1)) for b in range(0, i + 1, 4)]
            of_unit.append(range(len(groups), len(groups) + len(mine)))
            groups += mine
        G = len(groups)
        assert G % 2 == 0

        with nc.Block() as block:

            @block.gpsimd
            def _(pool):
                pool.wait_ge(neg_c_done, 1)
                with pool.Fori(0, PAIRS) as j:
                    pool.wait_ge(pair_done_1, j + 1)
                    one = lambda t: t.rearrange("p a t -> p (a t)")
                    pool.tensor_copy(q[:], one(m.proj[:, bass.ds(j + T_QC, 1), 0:SEQ])).then_inc(staged, 1)
                    pool.tensor_copy(k[:], one(m.proj[:, bass.ds(j + T_KC, 1), 0:SEQ])).then_inc(staged, 1)
                    pool.tensor_copy(v[:], m.vtok[:, 0:NC, bass.ds(j * P, P)]).then_inc(staged, 1)
                    pool.tensor_copy(neg_c2[:], neg_c[:, bass.ds(j * 2, 2)]).then_inc(staged, 1)

            @block.tensor
            def _(pe):
                logf = m.gates[:, 0:NC, 0:H]
                pe.wait_ge(summed_before, NC)
                pe.matmul(ps_t[0][:, 0:NC * H], m.cumul[:], logf, start=True, stop=False)
                pe.matmul(ps_t[0][:, 0:NC * H], m.ones[:], before[:], start=False, stop=True).then_inc(cum_done, 1)
                pe.sem_inc(pair_done_1, 1)

                def scores(j, u):
                    e, i = units[u]
                    if u >= 2:
                        pe.wait_ge(maxed, j * U + (u - 1))
                    else:
                        pe.wait_ge(bias_done, j * 2 + (u + 1))
                    n = (i + 1) * P
                    for b in range(0, n, 512):
                        w = min(512, n - b)
                        last = pe.matmul(ps_s[u % 2][:, b:b + w], q[half(e), i * P:(i + 1) * P], k[half(e), b:b + w],
                                         start=True, stop=True)
                    last.then_inc(s_done, 1)

                def turns(j, u):
                    pe.wait_ge(exp_done, j * U + (u + 1))
                    for n in of_unit[u]:
                        _, b0, b1 = groups[n]
                        pe.wait_ge((copied_dve, copied_act)[n % 2], j * (G // 2) + (n // 2 + 1))
                        for b in range(b0, b1):
                            last = pe.transpose(ps_t[n % 2][:, (b - b0) * P:(b - b0 + 1) * P],
                                                x[u % 2][:, b * P:(b + 1) * P], m.ident[:])
                        last.then_inc(turned, 1)

                def values(j, u):
                    e, i = units[u]
                    for n in of_unit[u]:
                        pe.wait_ge((copied_dve, copied_act)[n % 2], j * (G // 2) + (n // 2 + 2))
                    for b in range(i + 1):
                        last = pe.matmul(ps_o[e][:, i], pt[u % 2][:, b], v[:, b, half(e)], start=(b == 0), stop=(b == i))
                    last.then_inc(pv_done, 1)

                with pe.Fori(0, PAIRS) as j:
                    pe.wait_ge(staged, j * 4 + 4)
                    for e in range(2):
                        for b in range(NC):
                            last = pe.matmul(ps_s[e][:, b * P:(b + 1) * P], neg_c2[:, e, b:b + 1].to_broadcast([P, P]),
                                             m.ident[:], start=True, stop=True)
                        last.then_inc(bias_spread, 1)
                    scores(j, 0)
                    for u in range(U):
                        if u + 1 < U:
                            scores(j, u + 1)
                        turns(j, u)
                        if u >= 1:
                            values(j, u - 1)
                    values(j, U - 1)
                    pe.wait_ge(o_scaled, j * 2 + 2)
                    for b in range(NC):
                        last = pe.transpose(ps_s[b // 4][:, b % 4 * P:(b % 4 + 1) * P], o[:, b], m.ident[:])
                        if b % 4 == 3:
                            last.then_inc(o_turned, 1)
                    pe.wait_ge(y_done, j * 2 + 2)
                    pe.sem_inc(pair_done_1, 1)

            @block.scalar
            def _(act):
                act.sem_inc(copied_act, 1)
                act.wait_ge(cum_done, 1)
                act.mul(neg_c[:], ps_t[0][:, 0:NC * H].rearrange("p (t h) -> p h t", h=H), -1.0 / SCALE).then_inc(
                    neg_c_done, 1)
                with act.Fori(0, PAIRS) as j:
                    for e in range(2):
                        act.wait_ge(bias_spread, j * 2 + (e + 1))
                        act.copy(bias[e][:], ps_s[e][:]).then_inc(bias_done, 1)
                    for u, (e, i) in enumerate(units):
                        act.wait_ge(maxed, j * U + (u + 1))
                        w = (i + 1) * P
                        act.activation(x[u % 2][:, 0:w], x[u % 2][:, 0:w], ACT.Exp, bias=neg_max[:, u:u + 1], scale=-1.0,
                                       accum_out=total[:, e, i:i + 1]).then_inc(exp_done, 1)
                        for n in of_unit[u]:
                            if n % 2:
                                _, b0, b1 = groups[n]
                                act.wait_ge(turned, j * G + (n + 1))
                                if u >= 2:
                                    act.wait_ge(pv_done, j * U + (u - 1))
                                act.copy(pt[u % 2][:, b0:b1].rearrange("p b t -> p (b t)"),
                                         ps_t[1][:, 0:(b1 - b0) * P]).then_inc(copied_act, 1)
                    for b in range(2):
                        act.wait_ge(o_turned, j * 2 + (b + 1))
                        act.copy(m.yT[:, bass.ds(j + 5, 1), b * 512:(b + 1) * 512].rearrange("p a t -> p (a t)"),
                                 ps_s[b][:, 0:512]).then_inc(y_done, 1)

            @block.vector
            def _(dve):
                dve.sem_inc(copied_dve, 1)
                dve.memset(before[:, 0], 0.0).then_inc(summed_before, 1)
                for t in range(1, NC):
                    dve.wait_ge(summed_before, t)
                    dve.tensor_tensor(before[:, t], before[:, t - 1], m.gates[:, t - 1, 0:H], ALU.add).then_inc(
                        summed_before, 1)
                dve.wait_ge(neg_c_done, 1)
                with dve.Fori(0, PAIRS) as j:

                    def shift(u):
                        e, i = units[u]
                        if i == NC - 1:
                            dve.wait_ge(bias_done, j * 2 + (e + 1))
                        if u >= 1:
                            dve.wait_ge(maxed, j * U + u)
                        diag = bias[e][:, i * P:(i + 1) * P]
                        dve.tensor_tensor(diag, diag, m.causal[:], ALU.add).then_inc(mask_done, 1)
                        dve.wait_ge(mask_done, j * U + (u + 1))
                        dve.wait_ge(s_done, j * U + (u + 1))
                        if u >= 2:
                            dve.wait_ge(turned, j * G + (of_unit[u - 2][-1] + 1))
                        dve.sem_inc(waited, 1)
                        w = (i + 1) * P
                        dve.tensor_tensor_reduce(x[u % 2][:, 0:w], ps_s[u % 2][:, 0:w], bias[e][:, 0:w], -SCALE, 3e38,
                                                 ALU.add, ALU.min, neg_max[:, u:u + 1]).then_inc(maxed, 1)

                    shift(0)
                    for u in range(U):
                        if u + 1 < U:
                            shift(u + 1)
                        for n in of_unit[u]:
                            if n % 2 == 0:
                                _, b0, b1 = groups[n]
                                dve.wait_ge(turned, j * G + (n + 1))
                                if u >= 2:
                                    dve.wait_ge(pv_done, j * U + (u - 1))
                                dve.tensor_copy(pt[u % 2][:, b0:b1].rearrange("p b t -> p (b t)"),
                                                ps_t[0][:, 0:(b1 - b0) * P]).then_inc(copied_dve, 1)
                    for e in range(2):
                        dve.wait_ge(exp_done, j * U + NC * (e + 1))
                        dve.reciprocal(total[:, e], total[:, e]).then_inc(inv_done, 1)
                        dve.wait_ge(inv_done, j * 2 + (e + 1))
                        dve.wait_ge(pv_done, j * U + NC * (e + 1))
                        dve.tensor_tensor(o[:, :, half(e)], ps_o[e][:], total[:, e].unsqueeze(2).broadcast_to(
                            [P, NC, HD]), ALU.mult).then_inc(o_scaled, 1)


def fox_sample(nc, m):
    with Phase(nc) as ctx:
        off = O_H + KD * T * 4

        def put(name, shape, dt=F32):
            nonlocal off
            t = nc.alloc_sbuf_tensor_at("fs_" + name, shape, dt, offset=off)
            n = 4
            for d in shape[1:]:
                n *= d
            off += (n + 31) // 32 * 32
            return t

        N = NS * H
        kv = [put(f"kv{s}", [P, NPAGE, DW]) for s in range(3)]
        logf = put("logf", [P, NS, NPAGE, H])
        later = put("later", [P, NS, NPAGE, H])
        s_raw = put("s", [P, NS, NPAGE, H])
        p = put("p", [P, NS, NPAGE, H])
        q_rows = put("q_rows", [NS, DW])
        k_rows = put("k_rows", [NS, DW])
        own = put("own", [NS, H])
        v_cols = put("v_cols", [P, PAIRS, NS])
        own_all = put("own_all", [P, N])
        peak = put("peak", [P, N])
        top = put("top", [N, 1])
        top_diag = put("top_diag", [N, N])
        p_own = put("p_own", [P, N])
        den = put("den", [P, N])
        out = put("out", [P, PAIRS, NS])
        assert off <= O_END, off
        ps_q = [ctx.enter_context(nc.psum_tensor(f"fs_q{s}", [P, 512], F32)) for s in range(2)]
        ps_turn = ctx.enter_context(nc.psum_tensor("fs_turn", [P, 512], F32))
        ps_small = ctx.enter_context(nc.psum_tensor("fs_small", [P, 512], F32))
        ps_bias = ctx.enter_context(nc.psum_tensor("fs_bias", [P, 512], F32))
        ps_o = ctx.enter_context(nc.psum_tensor("fs_o", [P, PAIRS, NS, 2], F32))
        (logf_in, summed, turned, rows_done, own_done, own_spread, own_copied, q_spread, q_used, scored, biased,
         peaked, peak_turned, topped, diag_done, top_spread, shifted, exp_done, added, den_spread, den_done, o_done,
         mixed, chain) = semaphores(
             nc, ctx, *["fs_" + n for n in (
                 "logf_in", "summed", "turned", "rows_done", "own_done", "own_spread", "own_copied", "q_spread",
                 "q_used", "scored", "biased", "peaked", "peak_turned", "topped", "diag_done", "top_spread", "shifted",
                 "exp_done", "added", "den_spread", "den_done", "o_done", "mixed", "chain")])
        kv_in = semaphores(nc, ctx, *[f"fs_kv_in{s}" for s in range(3)])
        half = lambda e: slice(e * HD, (e + 1) * HD)
        flat = lambda t: t.rearrange("p b g h -> p (b g h)")
        with nc.Block() as block:

            def load(eng, cache, b, s):
                for g in range(NPAGE):
                    page = eng.value_load(m.pages[0:1, b * NPAGE + g:b * NPAGE + g + 1], min_val=0, max_val=NPHYS - 1)
                    eng.dma_start(kv[s][:, g], cache[0, bass.ds(page, 1)].rearrange("a t h d -> (a t) (h d)")).then_inc(
                        kv_in[s], 16)

            @block.sync
            def _(sp):
                for n in range(2 * NS):
                    if 3 <= n < NS + 3:
                        sp.wait_ge(scored, n - 2)
                    elif n >= NS + 3:
                        sp.wait_ge(o_done, n - NS - 2)
                    load(sp, m.cache_k if n < NS else m.cache_v, n % NS, n % 3)

            @block.gpsimd
            def _(pool):
                for b in range(NS):
                    for g in range(NPAGE):
                        page = pool.value_load(m.pages[0:1, b * NPAGE + g:b * NPAGE + g + 1], min_val=0,
                                               max_val=NPHYS - 1)
                        pool.dma_start(logf[:, b, g], m.cache_logf[0, bass.ds(page, 1)].rearrange(
                            "a t h -> (a t) h")).then_inc(logf_in, 16)

            @block.tensor
            def _(pe):
                for i in range(PAIRS):
                    pe.transpose(ps_turn[0:NS, i * P:(i + 1) * P], m.proj[:, T_QC + i, SEQ:T], m.ident[:])
                    pe.transpose(ps_small[0:NS, i * P:(i + 1) * P], m.proj[:, T_KC + i, SEQ:T], m.ident[:])
                    last = pe.transpose(ps_o[:, i, :, 0], m.vtok[0:NS, NC, i * P:(i + 1) * P], m.ident[0:NS, 0:NS])
                last.then_inc(turned, 1)
                pe.wait_ge(rows_done, 3)
                for b in range(NS):
                    if b >= 2:
                        pe.wait_ge(q_used, b - 1)
                    pe.matmul(ps_q[b % 2][:, 0:DW], m.ident[0:NS, b:b + 1].to_broadcast([NS, P]), q_rows[:],
                              start=True, stop=True).then_inc(q_spread, 1)
                pe.wait_ge(own_done, 1)
                for b in range(NS):
                    last = pe.matmul(ps_small[:, b * H:(b + 1) * H], m.ident[0:NS, b:b + 1].to_broadcast([NS, P]), own[:],
                                     start=True, stop=True)
                last.then_inc(own_spread, 1)
                pe.wait_ge(summed, NPAGE)
                pe.matmul(ps_bias[:, 0:N * NPAGE], m.later[:], flat(logf[:]), start=True, stop=False)
                pe.matmul(ps_bias[:, 0:N * NPAGE], m.ones[:], flat(later[:]), start=False, stop=True).then_inc(biased, 1)
                pe.wait_ge(peaked, 1)
                pe.transpose(ps_turn[0:N, 0:P], peak[:], m.ident[:]).then_inc(peak_turned, 1)
                pe.wait_ge(diag_done, 1)
                pe.matmul(ps_small[:, 0:N], m.ones[0:N, :], top_diag[:], start=True, stop=True).then_inc(top_spread, 1)
                pe.wait_ge(added, 1)
                pe.matmul(ps_turn[:, 0:N], m.ones[:], den[:], start=True, stop=True).then_inc(den_spread, 1)
                for b in range(NS):
                    n = NS + b
                    pe.wait_ge(kv_in[n % 3], 16 * NPAGE * (n // 3 + 1))
                    for i in range(PAIRS):
                        for g in range(NPAGE):
                            last = pe.matmul(ps_o[:, i, b], kv[n % 3][:, g, i * P:(i + 1) * P],
                                             p[:, b, g, 2 * i:2 * i + 2], start=(g == 0), stop=(g == NPAGE - 1))
                    last.then_inc(o_done, 1)

            @block.scalar
            def _(act):
                act.wait_ge(turned, 1)
                act.mul(q_rows[:], ps_turn[0:NS, 0:DW], SCALE).then_inc(rows_done, 1)
                act.copy(k_rows[:], ps_small[0:NS, 0:DW]).then_inc(rows_done, 1)
                act.copy(v_cols[:], ps_o[:, :, :, 0]).then_inc(rows_done, 1)
                act.wait_ge(own_spread, 1)
                act.copy(own_all[:], ps_small[:, 0:N]).then_inc(own_copied, 1)
                act.wait_ge(shifted, 2)
                act.activation(flat(p[:]), flat(s_raw[:]), ACT.Exp).then_inc(exp_done, 1)
                act.activation(p_own[:], p_own[:], ACT.Exp).then_inc(exp_done, 1)

            @block.vector
            def _(dve):
                step = Chain(dve, chain)
                dve.wait_ge(rows_done, 3)
                step(dve.tensor_tensor(k_rows[:], k_rows[:], q_rows[:], ALU.mult))
                step(dve.tensor_reduce(own[:], k_rows[:].rearrange("p (h d) -> p h d", h=H), AX_X, ALU.add))
                dve.tensor_tensor(own[:], own[:], m.gates[0:NS, NC, 0:H], ALU.subtract).then_inc(own_done, 1)
                dve.memset(later[:, :, NPAGE - 1], 0.0).then_inc(summed, 1)
                dve.wait_ge(logf_in, 16 * NS * NPAGE)
                for g in reversed(range(NPAGE - 1)):
                    dve.wait_ge(summed, NPAGE - 1 - g)
                    dve.tensor_tensor(later[:, :, g], later[:, :, g + 1], logf[:, :, g + 1], ALU.add).then_inc(summed, 1)
                for b in range(NS):
                    keys = kv[b % 3]
                    dve.wait_ge(kv_in[b % 3], 16 * NPAGE * (b // 3 + 1))
                    dve.wait_ge(q_spread, b + 1)
                    dve.tensor_tensor(keys[:], keys[:], ps_q[b % 2][:, 0:DW].unsqueeze(1).broadcast_to([P, NPAGE, DW]),
                                      ALU.mult).then_inc(q_used, 1)
                    dve.wait_ge(q_used, b + 1)
                    dve.tensor_reduce(s_raw[:, b].rearrange("p g h -> p (g h)"),
                                      keys[:].rearrange("p g (h d) -> p (g h) d", h=H), AX_X, ALU.add).then_inc(scored, 1)
                dve.wait_ge(biased, 1)
                dve.wait_ge(scored, NS)
                step(dve.tensor_tensor(flat(s_raw[:]), flat(s_raw[:]), ps_bias[:, 0:N * NPAGE], ALU.add))
                for b in range(NS):
                    last = dve.tensor_reduce(peak[:, b * H:(b + 1) * H], s_raw[:, b].rearrange("p g h -> p h g"), AX_X,
                                             ALU.max)
                step(last)
                dve.wait_ge(own_copied, 1)
                dve.tensor_tensor(peak[:], peak[:], own_all[:], ALU.max).then_inc(peaked, 1)
                dve.wait_ge(peak_turned, 1)
                dve.tensor_reduce(top[:], ps_turn[0:N, 0:P], AX_X, ALU.max).then_inc(topped, 1)
                dve.wait_ge(topped, 1)
                dve.tensor_scalar(top_diag[:], m.ident[0:N, 0:N], top[:], None, ALU.mult).then_inc(diag_done, 1)
                dve.wait_ge(top_spread, 1)
                for b in range(NS):
                    last = dve.tensor_tensor(s_raw[:, b], s_raw[:, b], ps_small[:, b * H:(b + 1) * H].unsqueeze(
                        1).broadcast_to([P, NPAGE, H]), ALU.subtract)
                last.then_inc(shifted, 1)
                dve.tensor_tensor(p_own[:], own_all[:], ps_small[:, 0:N], ALU.subtract).then_inc(shifted, 1)
                dve.wait_ge(exp_done, 2)
                for b in range(NS):
                    last = dve.tensor_reduce(den[:, b * H:(b + 1) * H], p[:, b].rearrange("p g h -> p h g"), AX_X, ALU.add)
                last.then_inc(added, 1)
                dve.wait_ge(den_spread, 1)
                step(dve.tensor_tensor(den[:], ps_turn[:, 0:N], p_own[:], ALU.add))
                step(dve.reciprocal(den[:], den[:]))
                dve.wait_ge(o_done, NS)
                for e in range(2):
                    of_heads = lambda t: t[half(e), :].rearrange("p (b m e) -> p e m b", m=PAIRS, e=2)[:, e]
                    step(dve.tensor_tensor(out[half(e)], v_cols[half(e)], of_heads(p_own), ALU.mult))
                    step(dve.tensor_tensor(out[half(e)], out[half(e)], ps_o[half(e), :, :, e], ALU.add))
                    dve.tensor_tensor(m.yT[half(e), 5:8, SEQ:T], out[half(e)], of_heads(den), ALU.mult).then_inc(mixed, 1)


def split(nc, m, src, hi, lo):
    with Phase(nc) as ctx:
        hi_cut, lo_cut = semaphores(nc, ctx, "y_hi_cut", "y_lo_cut")
        with nc.Block() as block:

            @block.scalar
            def _(act):
                for k in range(KD):
                    act.copy(hi[:, k], src[:, k]).then_inc(hi_cut, 1)

            @block.vector
            def _(dve):
                for k in range(KD):
                    dve.wait_ge(hi_cut, k + 1)
                    dve.tensor_tensor(lo[:, k], src[:, k], hi[:, k].bitcast(F32), ALU.subtract).then_inc(lo_cut, 1)


def add_normed(nc, m, tag, src, g, base, tmp_at, spill=None, rows_out=None):
    with Phase(nc) as ctx:
        sq = nc.alloc_sbuf_tensor_at(f"{tag}_sq", [P, 2, T], F32, offset=tmp_at)
        small = nc.alloc_sbuf_tensor_at(f"{tag}_small", [TT, 3, NT], F32, offset=tmp_at + 2 * T * 4)
        rows = nc.alloc_sbuf_tensor_at(f"{tag}_rows", [P, 2, D], F32, offset=tmp_at + 2 * T * 4 + 160)
        ps_sum = ctx.enter_context(nc.psum_tensor(f"{tag}_ps_sum", [TT, 512], F32))
        ps = ctx.enter_context(nc.psum_tensor(f"{tag}_ps", [P, NG, 512], F32))
        ps_rows = ctx.enter_context(nc.psum_tensor(f"{tag}_ps_rows", [P, 2, 2, 512], F32))
        (squared, summed, with_eps, rooted, inverted, spread, scaled, added, base_in, stored, rows_turned, chain,
         copied_act, copied_dve) = semaphores(
            nc, ctx, *[f"{tag}_{n}" for n in ("squared", "summed", "with_eps", "rooted", "inverted", "spread",
                                              "scaled", "added", "base_in", "stored", "rows_turned", "chain",
                                              "copied_act", "copied_dve")])
        rows_stored = semaphores(nc, ctx, f"{tag}_rows_stored0", f"{tag}_rows_stored1")
        grouped = lambda t: t.rearrange("p (g t) -> p g t", g=NG)
        with nc.Block() as block:

            @block.sync
            def _(sp):
                sp.dma_start(base[:], m.xT_dram if spill is not None else m.x1_dram).then_inc(base_in, 16)
                if spill is not None:
                    sp.wait_ge(added, KD)
                    sp.dma_start(spill, base[:]).then_inc(stored, 16)
                    sp.wait_ge(stored, 16)
                else:
                    for c in range(NC + 1):
                        sp.wait_ge((copied_dve, copied_act)[c % 2], c // 2 + 1)
                        if c < NC:
                            sp.dma_start(m.o_y_p[0, c * P:(c + 1) * P], rows[:, c % 2]).then_inc(rows_stored[c % 2], 16)
                        else:
                            sp.dma_start(m.o_y_s[:, 0], rows[0:NS, c % 2]).then_inc(rows_stored[c % 2], 16)
                    sp.wait_ge(rows_stored[0], 16 * ((NC + 2) // 2))
                    sp.wait_ge(rows_stored[1], 16 * ((NC + 1) // 2))

            @block.scalar
            def _(act):
                for k in range(KD):
                    if k >= 2:
                        act.wait_ge(summed, k - 1)
                    act.activation(sq[:, k % 2], src[:, k], ACT.Square).then_inc(squared, 1)
                root(act, small, with_eps).then_inc(rooted, 1)
                if spill is None:
                    for c in range(1, NC + 1, 2):
                        act.wait_ge(rows_turned, c + 1)
                        if c >= 2:
                            act.wait_ge(rows_stored[1], 16 * (c // 2))
                        act.copy(rows[:, 1].rearrange("p (a n) -> p a n", a=2), ps_rows[:, 1]).then_inc(copied_act, 1)

            @block.tensor
            def _(pe):
                for k in range(KD):
                    pe.wait_ge(squared, k + 1)
                    for c in range(NT):
                        last = pe.matmul(ps_sum[:, c:c + 1], sq[:, k % 2, c * TT:(c + 1) * TT], m.ones[:, 0:1],
                                         start=(k == 0 and c == 0), stop=(k == KD - 1), skip_group_check=True)
                    last.then_inc(summed, 1)
                pe.wait_ge(inverted, 1)
                spread_tokens(pe, m, ps, small[:, 1]).then_inc(spread, 1)
                if spill is None:
                    pe.wait_ge(added, KD)
                    for c in range(NC + 1):
                        n = P if c < NC else NS
                        if c >= 2:
                            pe.wait_ge((copied_dve, copied_act)[c % 2], c // 2)
                        for k in range(KD):
                            last = pe.transpose(ps_rows[0:n, c % 2, k // 4, k % 4 * P:(k % 4 + 1) * P],
                                                base[:, k, c * P:c * P + n], m.ident[:])
                        last.then_inc(rows_turned, 1)

            @block.vector
            def _(dve):
                step = Chain(dve, chain)
                dve.wait_ge(summed, KD)
                dve.tensor_scalar(small[:, 0], ps_sum[:, 0:NT], 1.0 / D, RMS_EPS, ALU.mult, ALU.add).then_inc(
                    with_eps, 1)
                inverse_root(dve, step, small, rooted).then_inc(inverted, 1)
                dve.wait_ge(spread, 1)
                dve.wait_ge(base_in, 16)
                for k in range(KD + 1):
                    if k < KD:
                        dve.scalar_tensor_tensor(out=grouped(src[:, k]), in0=grouped(src[:, k]),
                                                 scalar=m.cols_a[:, g + k:g + k + 1], in1=ps[:, :, 0:TG],
                                                 op0=ALU.mult, op1=ALU.mult).then_inc(scaled, 1)
                    if k >= 1:
                        dve.wait_ge(scaled, k)
                        dve.tensor_tensor(base[:, k - 1], base[:, k - 1], src[:, k - 1], ALU.add).then_inc(added, 1)
                if spill is None:
                    for c in range(0, NC + 1, 2):
                        n = P if c < NC else NS
                        dve.wait_ge(rows_turned, c + 1)
                        if c >= 2:
                            dve.wait_ge(rows_stored[0], 16 * (c // 2))
                        dve.tensor_copy(rows[0:n, 0].rearrange("p (a n) -> p a n", a=2), ps_rows[0:n, 0]).then_inc(
                            copied_dve, 1)


def feed_forward(nc, m, hi, lo, acc):
    with Phase(nc) as ctx:
        off = O_FFN
        at = nc.alloc_sbuf_tensor_at

        def put(name, shape, dt=F32):
            nonlocal off
            t = at("ff_" + name, shape, dt, offset=off)
            n = 4
            for d in shape[1:]:
                n *= d
            off += n
            return t

        raw = [put(f"raw{s}", [P, KD, P]) for s in range(2)]
        w_hi = [put(f"w_hi{s}", [P, KD, P], F32R) for s in range(2)]
        w_lo = [put(f"w_lo{s}", [P, KD, P], F32R) for s in range(2)]
        d_raw = [put(f"d_raw{s}", [P, D]) for s in range(2)]
        d_hi = [put(f"d_hi{s}", [P, D], F32R) for s in range(2)]
        d_lo = [put(f"d_lo{s}", [P, D], F32R) for s in range(2)]
        h_hi = [put(f"h_hi{s}", [P, T], F32R) for s in range(2)]
        h_lo = [put(f"h_lo{s}", [P, T], F32R) for s in range(2)]
        hid = put("hid", [P, T])
        assert off <= O_END, off
        ps_w = [ctx.enter_context(nc.psum_tensor(f"ff_ps{s}", [P, NG, 512], F32)) for s in range(2)]
        ps_d = [ctx.enter_context(nc.psum_tensor(f"ff_psd{s}", [P, 512], F32)) for s in range(2)]
        (w_hi_cut, w_lo_cut, d_hi_cut, d_lo_cut, multiplied, gated, hidden, hid_hi, hid_lo, down_done, down_added,
         cleared) = semaphores(
             nc, ctx, *["ff_" + n for n in ("w_hi_cut", "w_lo_cut", "d_hi_cut", "d_lo_cut", "multiplied", "gated",
                                            "hidden", "hid_hi", "hid_lo", "down_done", "down_added", "cleared")])
        w_in = semaphores(nc, ctx, "ff_w_in0", "ff_w_in1")
        d_in = semaphores(nc, ctx, "ff_d_in0", "ff_d_in1")
        pairs = NF // 2
        units = [(n, g) for n in range(KD) for g in range(NG)]
        U = len(units)
        by_k = lambda w: w[0].rearrange("(k p) n -> p k n", p=P)
        weights = (by_k(m.w_gate), by_k(m.w_up))

        def over_pairs(eng, body):
            body(0, True, False)
            with eng.Fori(1, pairs - 1) as i:
                body(i, False, False)
            body(pairs - 1, False, True)

        with nc.Block() as block:

            @block.sync
            def _(sp):
                def load(i, t, first_use):
                    if not first_use:
                        sp.wait_ge(w_lo_cut, i * 4 + (t - 1))
                    sp.dma_start(raw[t % 2][:], weights[t % 2][:, :, bass.ds(i * (2 * P) + t // 2 * P, P)]).then_inc(
                        w_in[t % 2], 16)

                def body(i, first, last):
                    load(i, 2, False)
                    load(i, 3, False)
                    for f in range(2):
                        if not first:
                            sp.wait_ge(d_lo_cut, i * 2)
                        sp.dma_start(d_raw[f][:], m.w_down[0, bass.ds(i * (2 * P) + f * P, P)]).then_inc(d_in[f], 16)
                    if not last:
                        load(i, 4, False)
                        load(i, 5, False)

                load(0, 0, True)
                load(0, 1, True)
                over_pairs(sp, body)

            @block.scalar
            def _(act):
                def cut(i, t, first_use=False):
                    act.wait_ge(w_in[t % 2], i * 32 + (t // 2 + 1) * 16)
                    if not first_use:
                        act.wait_ge(multiplied, i * 4 + (t - 1))
                    act.copy(w_hi[t % 2][:], raw[t % 2][:]).then_inc(w_hi_cut, 1)

                def silu(i, f, first=False):
                    act.wait_ge(multiplied, i * 4 + (2 * f + 1))
                    if not first:
                        act.wait_ge(hid_lo, i * 2 + f)
                    act.activation(hid[:].rearrange("p (g t) -> p g t", g=NG), ps_w[0][:, :, 0:TG], ACT.Silu).then_inc(
                        gated, 1)

                def cut_hidden(i, f):
                    act.wait_ge(hidden, i * 2 + (f + 1))
                    act.copy(h_hi[f][:], hid[:]).then_inc(hid_hi, 1)

                def body(i, first, last):
                    cut(i, 1, first)
                    silu(i, 0, first)
                    cut(i, 2)
                    for f in range(2):
                        act.wait_ge(d_in[f], i * 16 + 16)
                        if not first:
                            act.wait_ge(down_done, i * U)
                        act.copy(d_hi[f][:], d_raw[f][:]).then_inc(d_hi_cut, 1)
                    cut_hidden(i, 0)
                    cut(i, 3)
                    silu(i, 1)
                    if not last:
                        cut(i, 4)
                    cut_hidden(i, 1)

                cut(0, 0, True)
                over_pairs(act, body)

            @block.vector
            def _(dve):
                def cut(i, t):
                    dve.wait_ge(w_hi_cut, i * 4 + (t + 1))
                    dve.tensor_tensor(w_lo[t % 2][:], raw[t % 2][:], w_hi[t % 2][:].bitcast(F32),
                                      ALU.subtract).then_inc(w_lo_cut, 1)

                def hidden_tile(i, f):
                    dve.wait_ge(gated, i * 2 + (f + 1))
                    dve.wait_ge(multiplied, i * 4 + (2 * f + 2))
                    group = hid[:].rearrange("p (g t) -> p g t", g=NG)
                    dve.tensor_tensor(group, group, ps_w[1][:, :, 0:TG], ALU.mult).then_inc(hidden, 1)
                    dve.wait_ge(hid_hi, i * 2 + (f + 1))
                    dve.tensor_tensor(h_lo[f][:], hid[:], h_hi[f][:].bitcast(F32), ALU.subtract).then_inc(hid_lo, 1)

                def add_down(i):
                    for u, (n, g) in enumerate(units):
                        dve.wait_ge(down_done, i * U + (u + 1))
                        part = acc[:, n, g * TG:(g + 1) * TG]
                        dve.tensor_tensor(part, part, ps_d[u % 2][:, 0:TG], ALU.add).then_inc(down_added, 1)

                def body(i, first, last):
                    cut(i, 1)
                    if not first:
                        add_down(i - 1)
                    cut(i, 2)
                    for f in range(2):
                        dve.wait_ge(d_hi_cut, i * 2 + (f + 1))
                        dve.tensor_tensor(d_lo[f][:], d_raw[f][:], d_hi[f][:].bitcast(F32), ALU.subtract).then_inc(
                            d_lo_cut, 1)
                    hidden_tile(i, 0)
                    cut(i, 3)
                    if not last:
                        cut(i, 4)
                    hidden_tile(i, 1)

                dve.memset(acc[:], 0.0).then_inc(cleared, 1)
                cut(0, 0)
                dve.wait_ge(cleared, 1)
                over_pairs(dve, body)
                add_down(pairs - 1)

            @block.tensor
            def _(pe):
                def gate_up(i, t, first_use=False):
                    pe.wait_ge(w_lo_cut, i * 4 + (t + 1))
                    if not first_use:
                        pe.wait_ge((gated, hidden)[t % 2], i * 2 + t // 2)
                    for k in range(KD):
                        for n, (a, b) in enumerate(((w_hi, hi), (w_hi, lo), (w_lo, hi))):
                            for g in range(NG):
                                last = pe.matmul(ps_w[t % 2][:, g, 0:TG], a[t % 2][:, k], b[:, k, g * TG:(g + 1) * TG],
                                                 start=(k == 0 and n == 0), stop=(k == KD - 1 and n == 2))
                    last.then_inc(multiplied, 1)

                def down(i, first):
                    pe.wait_ge(hid_lo, i * 2 + 2)
                    pe.wait_ge(d_lo_cut, i * 2 + 2)
                    for u, (n, g) in enumerate(units):
                        if not (first and u < 2):
                            pe.wait_ge(down_added, i * U + (u - 1))
                        for f in range(2):
                            for r, (a, b) in enumerate(((d_hi, h_hi), (d_hi, h_lo), (d_lo, h_hi))):
                                last = pe.matmul(ps_d[u % 2][:, 0:TG], a[f][:, n * P:(n + 1) * P],
                                                 b[f][:, g * TG:(g + 1) * TG], start=(f == 0 and r == 0),
                                                 stop=(f == 1 and r == 2))
                        last.then_inc(down_done, 1)

                gate_up(0, 0, True)
                gate_up(0, 1, True)
                gate_up(0, 2)
                gate_up(0, 3)
                gate_up(1, 0)
                down(0, True)
                for t in range(1, 4):
                    gate_up(1, t)
                with pe.Fori(2, pairs) as i:
                    gate_up(i, 0)
                    down(i - 1, False)
                    for t in range(1, 4):
                        gate_up(i, t)
                down(pairs - 1, False)


def program(nc, m):
    at = nc.alloc_sbuf_tensor_at
    m.xT_dram = nc.dram_tensor("xT_spill", [P, KD, T], F32).ap()
    m.x1_dram = nc.dram_tensor("x1_spill", [P, KD, T], F32).ap()
    constants(nc, m)
    m.vtok = at("vtok", [P, NC + 1, NV], F32, offset=O_VTOK)
    load_and_transpose(nc, m)
    h_hi = at("h_hi", [P, KD, T], F32R, offset=O_H)
    h_lo = at("h_lo", [P, KD, T], F32R, offset=O_H + COLS)
    rms_norm(nc, m, "pre", m.xT, G_PRE_MIX, h_hi, h_lo, O_W)
    project_rows(nc, m, h_hi, h_lo)
    m.proj = at("proj", [P, NPROJ, T], F32, offset=O_PROJ)
    project(nc, m, "in", m.w_in[0], ((0, FIRST_TILES), (COL_QC, QC_TILES)), h_hi, h_lo, m.proj)
    m.yT = at("yT", [P, KD, T], F32, offset=O_H)
    convolve(nc, m)
    gates(nc, m)
    delta_rule(nc, m)
    delta_sample(nc, m)
    fox_prompt(nc, m)
    fox_sample(nc, m)
    y_hi = at("y_hi", [P, KD, T], F32R, offset=O_PROJ)
    y_lo = at("y_lo", [P, KD, T], F32R, offset=O_PROJ + COLS)
    split(nc, m, m.yT, y_hi, y_lo)
    mix = at("mix", [P, KD, T], F32, offset=O_H)
    project(nc, m, "out", m.w_out[0], ((0, KD),), y_hi, y_lo, mix)
    x1 = at("x1", [P, KD, T], F32, offset=O_H + COLS)
    add_normed(nc, m, "mid", mix, G_POST_MIX, x1, O_PROJ, spill=m.x1_dram)
    h2_hi = at("h2_hi", [P, KD, T], F32R, offset=O_PROJ)
    h2_lo = at("h2_lo", [P, KD, T], F32R, offset=O_PROJ + COLS)
    rms_norm(nc, m, "ffn", x1, G_PRE_FFN, h2_hi, h2_lo, O_H)
    acc = at("acc", [P, KD, T], F32, offset=O_PROJ + 2 * COLS)
    feed_forward(nc, m, h2_hi, h2_lo, acc)
    x2 = at("x2", [P, KD, T], F32, offset=O_PROJ)
    add_normed(nc, m, "end", acc, G_POST_FFN, x2, O_PROJ + COLS)


def tables():
    i = np.arange(P)
    row, col = i[:, None], i[None, :]
    t = np.zeros((15, P, P), np.float32)
    t[0] = row == col
    t[1] = row <= col
    t[2] = row > col
    t[3] = 1
    t[4] = row // HD == col // HD
    level = lambda s: (row // (2 * s) == col // (2 * s)) & (row // s % 2 == 1) & (col // s % 2 == 0)
    t[5] = -level(1).T.astype(np.float32)
    t[6] = np.where(col >= row, 0, NEG)
    t[7] = np.where(col <= row, 0, NEG)
    for n in range(7):
        t[8 + n] = -level(1 << n).astype(np.float32)
    return t


def head_table():
    t = np.zeros((2 * H, H, P), np.float32)
    for j in range(H):
        for e in range(2):
            t[2 * j + e, j, e * HD:(e + 1) * HD] = 1
    return t


def build(nc, ins, outs):
    m = Mem()
    (m.x_prompt, m.x_sample, m.cache_k, m.cache_v, m.cache_logf, m.page_table, m.state_conv_a, m.state_conv_b,
     m.state_delta, m.w_in, m.conv_a_w, m.conv_a_b, m.ln_a_g, m.ln_a_b, m.conv_b_w, m.a_log, m.dt_bias, m.norm_b_g,
     m.f_bias, m.w_out, m.g_pre_mix, m.g_post_mix, m.g_pre_ffn, m.g_post_ffn, m.w_gate, m.w_up, m.w_down,
     m.tables, m.head_table) = ins
    (m.o_y_p, m.o_y_s, m.o_k_p, m.o_v_p, m.o_f_p, m.o_conv_a_p, m.o_conv_b_p, m.o_delta_p, m.o_k_s, m.o_v_s, m.o_f_s,
     m.o_conv_a_s, m.o_conv_b_s, m.o_delta_s) = outs
    program(nc, m)


_INS = ["x_prompt", "x_sample", "cache_k", "cache_v", "cache_logf", "page_table", "state_conv_a", "state_conv_b",
        "state_delta", "w_in", "conv_a_w", "conv_a_b", "ln_a_g", "ln_a_b", "conv_b_w", "a_log", "dt_bias", "norm_b_g",
        "f_bias", "w_out", "g_pre_mix", "g_post_mix", "g_pre_ffn", "g_post_ffn", "w_gate", "w_up", "w_down"]
_OUTS = [(1, SEQ, D), (NS, 1, D), (1, 1, SEQ, H, HD), (1, 1, SEQ, H, HD), (1, 1, SEQ, H), (1, 1, KA - 1, CA),
         (1, 1, KB - 1, 3 * DW), (1, 1, H, HD, HD), (1, NS, 1, H, HD), (1, NS, 1, H, HD), (1, NS, 1, H),
         (1, NS, KA - 1, CA), (1, NS, KB - 1, 3 * DW), (1, NS, H, HD, HD)]


def kernel(**inputs):
    import numpy as _np
    import concourse.bacc as _bacc
    from concourse import mybir as _mybir
    from concourse.bass_utils import run_bass_kernel_spmd as _run

    nc = _bacc.Bacc("TRN2", target_bir_lowering=False, num_devices=1)
    arrays, ins = {}, []
    for name in _INS + ["tables", "head_table"]:
        if name == "tables":
            a = tables()
        elif name == "head_table":
            a = head_table()
        else:
            a = _np.ascontiguousarray(inputs[name])
        arrays[f"in_{name}_dram"] = a
        ins.append(nc.dram_tensor(f"in_{name}_dram", a.shape, _mybir.dt.from_np(a.dtype), kind="ExternalInput").ap())
    outs = [nc.dram_tensor(f"out_{i}_dram", shape, _mybir.dt.float32, kind="ExternalOutput").ap()
            for i, shape in enumerate(_OUTS)]
    build(nc, ins, outs)
    r = _run(nc, [arrays], core_ids=[0])
    return tuple(r.results[0][f"out_{i}_dram"] for i in range(len(_OUTS)))
```

```python
from contextlib import ExitStack

import concourse.bass as bass
import numpy as np
from concourse import mybir

F32 = mybir.dt.float32
F32R = mybir.dt.float32r
I32 = mybir.dt.int32
ALU = mybir.AluOpType
ACT = mybir.ActivationFunctionType
AX_X = mybir.AxisListType.X

P = 128
D = 1024
SEQ = 1024
NS = 8
T = SEQ + NS
KD = D // P
NG = 3
TG = T // NG
NT = 12
TT = T // NT
HD = 64
H = 6
PAIRS = H // 2
DW = H * HD
CA = 256
KA = 31
KB = 4
DFF = 2816
NF = DFF // P
NC = SEQ // P
PAGE = 128
NPAGE = 8
NPHYS = 80
COL_BETA = 2 * CA + 4 * DW
COL_QC = COL_BETA + 2 * H
COL_VC = COL_QC + 2 * DW
N_IN = COL_VC + DW + H
NV = DW + 3 * H
FIRST_TILES = COL_BETA // P
QC_TILES = 2 * DW // P
NPROJ = FIRST_TILES + QC_TILES
T_A, T_GATE, T_QB, T_KB, T_VB, T_Z, T_QC, T_KC = 0, 2, 4, 7, 10, 13, 16, 19
NEG = -1e30
SCALE = HD ** -0.5
RMS_EPS = 1e-6
LN_EPS = 1e-5

G_PRE_MIX, G_POST_MIX, G_PRE_FFN, G_POST_FFN, CONV_A_B, LN_G, LN_B, CONV_A_W = 0, 8, 16, 24, 32, 34, 36, 38
N_COLS_A = 38 + 2 * KA
CONV_B_W, NORM_B_G = 0, KB * 9
N_COLS_B = NORM_B_G + 1

BASE = 16512
O_CONST = BASE
O_VTOK = O_CONST + 16640
O_PROJ = O_VTOK + 9 * NV * 4 + 24
O_H = O_PROJ + NPROJ * T * 4
O_W = O_H + 2 * KD * T * 4
O_END = 229344
COLS = KD * T * 4
O_FFN = O_PROJ + 3 * COLS
O_FOX = O_END - 3 * NS * NPAGE * H * 4 - 1024
KV_BYTES = NPAGE * DW * 4
O_TAIL_KV = O_FOX - KV_BYTES
O_VALUES = [O_PROJ, O_TAIL_KV] + [O_PROJ + n * KV_BYTES for n in range(NS - 3)] + [O_TAIL_KV]
EARLY = 2


class Mem:
    pass


class Phase(ExitStack):

    def __init__(self, nc):
        super().__init__()
        self.nc, self.own = nc, []

    def __exit__(self, *error):
        if self.own:
            self.nc.clear_and_free_semaphores(self.own)
            self.nc.all_engine_barrier()
        return super().__exit__(*error)


def semaphores(nc, ctx, *names):
    got = [nc.alloc_semaphore(n) for n in names]
    ctx.own.extend(got)
    return got


def constants(nc, m):
    off = O_CONST

    def put(name, shape, dt=F32):
        nonlocal off
        t = nc.alloc_sbuf_tensor_at(name, shape, dt, offset=off)
        n = 4
        for s in shape[1:]:
            n *= s
        off += (n + 31) // 32 * 32
        return t

    m.ident = put("ident", [P, P])
    m.cumul = put("cumul", [P, P])
    m.later = put("later", [P, P])
    m.ones = put("ones", [P, P])
    m.head_ones = put("head_ones", [P, P])
    m.level_mask = put("level_mask", [P, 7, P])
    m.level1_t = put("level1_t", [P, P])
    m.keep_t = put("keep_t", [P, P])
    m.causal = put("causal", [P, P])
    m.head_rows = put("head_rows", [2 * H, H, P])
    m.cols_a = put("cols_a", [P, N_COLS_A])
    m.cols_b = put("cols_b", [P, N_COLS_B])
    m.rows6 = put("rows6", [P, 3 * H])
    m.state = put("state", [P, PAIRS, HD])
    m.eps = put("eps", [P, 4])
    m.gates = put("gates", [P, NC + 1, 3 * H])
    m.pages = put("pages", [1, NS * NPAGE], I32)
    assert off <= O_VTOK, off


def fox_sample_tensors(nc, m):
    at = nc.alloc_sbuf_tensor_at
    m.fs_logf = at("fs_logf", [P, NS, NPAGE, H], F32, offset=O_FOX)
    m.fs_s = at("fs_s", [P, NS, NPAGE, H], F32, offset=O_FOX + NS * NPAGE * H * 4)
    m.fs_q_rows = at("fs_q_rows", [NS, DW], F32, offset=O_FOX + 2 * NS * NPAGE * H * 4)
    m.fs_own_all = at("fs_own_all", [P, NS * H], F32, offset=O_FOX + 3 * NS * NPAGE * H * 4)
    m.fs_v_cols = at("fs_v_cols", [P, PAIRS, NS], F32, offset=O_FOX + 3 * NS * NPAGE * H * 4 + 192)
    off = O_FOX + 3 * NS * NPAGE * H * 4 + 288
    m.fs_den = at("fs_den", [P, NS * H], F32, offset=off)
    m.fs_out = at("fs_out", [P, PAIRS, NS, 2], F32, offset=off + 192)
    m.fs_p = at("fs_p", [P, NS, NPAGE, H], F32, offset=O_FOX + 2 * NS * NPAGE * H * 4)
    m.fs_keys = at("fs_keys", [P, NPAGE, DW], F32, offset=O_TAIL_KV)
    m.fs_values = [at(f"fs_values{b}", [P, NPAGE, DW], F32, offset=o) for b, o in enumerate(O_VALUES)]
    m.x_spilled = nc.alloc_semaphore("x_spilled")
    m.x1_spilled = nc.alloc_semaphore("x1_spilled")
    m.logf_in = nc.alloc_semaphore("fs_logf_in")
    m.keys_in = nc.alloc_semaphore("fs_keys_in")
    m.values_in = [nc.alloc_semaphore(f"fs_values_in{s}") for s in range(3)]


def fox_values(pe, m, bank, sequences, done):
    for b in sequences:
        pe.wait_ge(m.values_in[min(b, EARLY)], 16 * NPAGE * (1 if b < EARLY else NS - EARLY))
        for g in range(NPAGE):
            last = pe.matmul(bank(b)[0:H, 0:DW], m.fs_p[:, b, g], m.fs_values[b][:, g], start=(g == 0),
                             stop=(g == NPAGE - 1))
        last.then_inc(done, 1)


def turn_fox_rows(pe, m, rows, ps_turned, sequences, done, copied):
    for n, b in enumerate(sequences):
        pe.wait_ge(copied, n + 1)
        for i in range(PAIRS):
            last = pe.transpose(ps_turned[:, i, b], rows[:, n, i * P:(i + 1) * P], m.ident[0:H, 0:H])
    last.then_inc(done, 1)


def load_pages(eng, m, cache, b, to, signal):
    for g in range(NPAGE):
        page = eng.value_load(m.pages[0:1, b * NPAGE + g:b * NPAGE + g + 1], min_val=0, max_val=NPHYS - 1)
        eng.dma_start(to[:, g], cache[0, bass.ds(page, 1)].rearrange("a t h d -> (a t) (h d)")).then_inc(signal, 16)


def load_and_transpose(nc, m):
    with Phase(nc) as ctx:
        sb = lambda n, s, o, dt=F32: nc.alloc_sbuf_tensor_at(n, s, dt, offset=o)
        m.xT = sb("xT", [P, KD, T], O_PROJ)
        x_rows = sb("x_rows", [P, 4, D], O_W)
        rows_a = sb("rows_a", [N_COLS_A, P], O_H)
        rows_b = sb("rows_b", [N_COLS_B, P], O_H + 512)
        ps = ctx.enter_context(nc.psum_tensor("ps_xT", [P, 2, KD, P], F32))
        ps_cols = ctx.enter_context(nc.psum_tensor("ps_cols", [P, 512], F32))
        const_in, params_in, cols_done, x_turned, x_copied_even = semaphores(
            nc, ctx, "const_in", "params_in", "cols_done", "x_turned", "x_copied_even")
        x_in = semaphores(nc, ctx, *[f"x_in{n}" for n in range(4)])
        cols_turned, x_copied_odd = semaphores(nc, ctx, "cols_turned", "x_copied_odd")
        x_copied = (x_copied_even, x_copied_odd)
        tiles = NC + 1
        with nc.Block() as block:

            @block.sync
            def _(sp):
                sp.dma_start(m.ident[:], m.tables[0]).then_inc(const_in, 16)
                for n in range(tiles):
                    if n >= 4:
                        sp.wait_ge(x_turned, n - 3)
                    if n < NC:
                        sp.dma_start(x_rows[:, n % 4], m.x_prompt[0, n * P:(n + 1) * P]).then_inc(x_in[n % 4], 16)
                    else:
                        sp.dma_start(x_rows[0:NS, n % 4], m.x_sample[:, 0]).then_inc(x_in[n % 4], 16)
                sp.wait_ge(x_copied_even, (tiles + 1) // 2)
                sp.wait_ge(x_copied_odd, tiles // 2)
                sp.dma_start(m.xT_dram, m.xT[:]).then_inc(m.x_spilled, 16)

            @block.scalar
            def _(act):
                for t, s in ((m.cumul, 1), (m.later, 2), (m.ones, 3), (m.head_ones, 4), (m.level1_t, 5), (m.keep_t, 6),
                             (m.causal, 7)):
                    act.dma_start(t[:], m.tables[s]).then_inc(const_in, 16)
                act.dma_start(m.level_mask[:], m.tables[8:15].rearrange("l p n -> p l n")).then_inc(const_in, 16)
                act.dma_start(m.head_rows[:], m.head_table).then_inc(const_in, 16)
                for v, r in ((m.g_pre_mix, G_PRE_MIX), (m.g_post_mix, G_POST_MIX), (m.g_pre_ffn, G_PRE_FFN),
                             (m.g_post_ffn, G_POST_FFN)):
                    act.dma_start(rows_a[r:r + KD, :], v.rearrange("l (k p) -> (l k) p", p=P)).then_inc(params_in, 16)
                for v, r in ((m.conv_a_b, CONV_A_B), (m.ln_a_g, LN_G), (m.ln_a_b, LN_B)):
                    act.dma_start(rows_a[r:r + 2, :], v.rearrange("l (k p) -> (l k) p", p=P)).then_inc(params_in, 16)
                act.dma_start(rows_a[CONV_A_W:N_COLS_A, :],
                              m.conv_a_w.rearrange("l w (k p) -> (l w k) p", p=P)).then_inc(params_in, 16)
                act.dma_start(rows_b[0:NORM_B_G, :],
                              m.conv_b_w.rearrange("l w (k p) -> (l w k) p", p=P)).then_inc(params_in, 16)
                for e in range(2):
                    act.dma_start(rows_b[NORM_B_G:N_COLS_B, e * HD:(e + 1) * HD], m.norm_b_g).then_inc(params_in, 16)
                for v, c in ((m.f_bias, 0), (m.a_log, 1), (m.dt_bias, 2)):
                    act.dma_start(m.rows6[:, c * H:(c + 1) * H], v[0:1, :].to_broadcast([P, H])).then_inc(params_in, 16)
                act.dma_start(m.pages[:], m.page_table.rearrange("b n -> (b n)")[None, :]).then_inc(params_in, 16)
                act.wait_ge(params_in, 15 * 16)
                for n in range(1, tiles, 2):
                    act.wait_ge(x_turned, n + 1)
                    act.copy(m.xT[:, :, n * P:n * P + P], ps[:, 1]).then_inc(x_copied_odd, 1)

            @block.tensor
            def _(pe):
                pe.wait_ge(const_in, 10 * 16)
                for n in range(tiles):
                    rows = P if n < NC else NS
                    pe.wait_ge(x_in[n % 4], 16 * (n // 4 + 1))
                    if n >= 2:
                        pe.wait_ge(x_copied[n % 2], n // 2)
                    for k in range(KD):
                        last = pe.transpose(ps[:, n % 2, k, 0:rows], x_rows[0:rows, n % 4, k * P:(k + 1) * P],
                                            m.ident[0:rows, 0:rows])
                    last.then_inc(x_turned, 1)
                pe.wait_ge(params_in, 15 * 16)
                pe.transpose(ps_cols[:, 0:N_COLS_A], rows_a[:], m.ident[0:N_COLS_A, 0:N_COLS_A])
                pe.transpose(ps_cols[:, P:P + N_COLS_B], rows_b[:], m.ident[0:N_COLS_B, 0:N_COLS_B]).then_inc(
                    cols_turned, 1)

            @block.vector
            def _(dve):
                for n in range(0, tiles, 2):
                    w = P if n < NC else NS
                    dve.wait_ge(x_turned, n + 1)
                    dve.tensor_copy(m.xT[:, :, n * P:n * P + w], ps[:, 0, :, 0:w]).then_inc(x_copied_even, 1)
                for c, v in enumerate((RMS_EPS, LN_EPS, 1.0)):
                    dve.memset(m.eps[:, c:c + 1], v).then_inc(cols_done, 1)
                dve.wait_ge(cols_turned, 1)
                dve.tensor_copy(m.cols_a[:], ps_cols[:, 0:N_COLS_A]).then_inc(cols_done, 1)
                dve.tensor_copy(m.cols_b[:], ps_cols[:, P:P + N_COLS_B]).then_inc(cols_done, 1)


class Chain:

    def __init__(self, eng, sem):
        self.eng, self.sem, self.n = eng, sem, 0

    def __call__(self, instruction):
        instruction.then_inc(self.sem, 1)
        self.n += 1
        self.eng.wait_ge(self.sem, self.n)


def root(act, small, eps_ready):
    act.wait_ge(eps_ready, 1)
    return act.activation(small[:, 1], small[:, 0], ACT.Sqrt)


def inverse_root(dve, step, small, rooted):
    dve.wait_ge(rooted, 1)
    step(dve.reciprocal(small[:, 1], small[:, 1]))
    step(dve.tensor_tensor(small[:, 2], small[:, 1], small[:, 1], ALU.mult))
    step(dve.tensor_tensor(small[:, 2], small[:, 2], small[:, 0], ALU.mult))
    step(dve.tensor_scalar(small[:, 2], small[:, 2], -0.5, 1.5, ALU.mult, ALU.add))
    return dve.tensor_tensor(small[:, 1], small[:, 1], small[:, 2], ALU.mult)


def spread_tokens(pe, m, ps, inv):
    for c in range(NT):
        g, t = divmod(c * TT, TG)
        last = pe.matmul(ps[:, g, t:t + TT], inv[:, c:c + 1].to_broadcast([TT, P]), m.ident[0:TT, 0:TT], start=True, stop=True)
    return last


def square_tiles(act, src, sq, squared, added):
    for k in range(KD):
        if k >= 2:
            act.wait_ge(added, k - 1)
        act.activation(sq[:, k % 2], src[:, k], ACT.Square).then_inc(squared, 1)


def add_squares(dve, sq, squared, added):
    for k in range(KD):
        dve.wait_ge(squared, k + 1)
        if k == 0:
            dve.tensor_copy(sq[:, 2], sq[:, 0]).then_inc(added, 1)
        else:
            dve.wait_ge(added, k)
            dve.tensor_tensor(sq[:, 2], sq[:, 2], sq[:, k % 2], ALU.add).then_inc(added, 1)


def sum_partitions(pe, m, ps_sum, sq, added):
    pe.wait_ge(added, KD)
    for c in range(NT):
        last = pe.matmul(ps_sum[:, c:c + 1], sq[:, 2, c * TT:(c + 1) * TT], m.ones[:, 0:1], start=True, stop=True)
    return last


def rms_norm(nc, m, tag, src, g, hi, lo, tmp_at):
    with Phase(nc) as ctx:
        sq = nc.alloc_sbuf_tensor_at(f"{tag}_sq", [P, 3, T], F32, offset=tmp_at)
        small = nc.alloc_sbuf_tensor_at(f"{tag}_small", [TT, 3, NT], F32, offset=tmp_at + 3 * T * 4)
        ps_sum = ctx.enter_context(nc.psum_tensor(f"{tag}_ps_sum", [TT, 512], F32))
        ps = ctx.enter_context(nc.psum_tensor(f"{tag}_ps", [P, NG, 512], F32))
        added, squared, summed, with_eps, rooted, inverted, spread, scaled, hi_done, lo_done, chain = semaphores(
            nc, ctx, *[f"{tag}_{n}" for n in ("squares_added", "squared", "summed", "with_eps", "rooted", "inverted",
                                              "spread", "scaled", "hi_done", "lo_done", "chain")])
        on_pool = [1, 4, 6]
        pool_lo_done, = semaphores(nc, ctx, f"{tag}_pool_lo_done")
        with nc.Block() as block:

            @block.gpsimd
            def _(pool):
                for k in on_pool:
                    pool.wait_ge(hi_done, k + 1)
                    pool.tensor_tensor(lo[:, k], sq[:, k % 3], hi[:, k].bitcast(F32), ALU.subtract).then_inc(
                        pool_lo_done, 1)

            @block.scalar
            def _(act):
                square_tiles(act, src, sq, squared, added)
                root(act, small, with_eps).then_inc(rooted, 1)
                for k in range(KD):
                    act.wait_ge(scaled, k + 1)
                    act.copy(hi[:, k], sq[:, k % 3]).then_inc(hi_done, 1)

            @block.tensor
            def _(pe):
                sum_partitions(pe, m, ps_sum, sq, added).then_inc(summed, 1)
                pe.wait_ge(inverted, 1)
                spread_tokens(pe, m, ps, small[:, 1]).then_inc(spread, 1)

            @block.vector
            def _(dve):
                step = Chain(dve, chain)
                add_squares(dve, sq, squared, added)
                dve.wait_ge(summed, 1)
                dve.tensor_scalar(small[:, 0], ps_sum[:, 0:NT], 1.0 / D, RMS_EPS, ALU.mult, ALU.add).then_inc(
                    with_eps, 1)
                inverse_root(dve, step, small, rooted).then_inc(inverted, 1)
                dve.wait_ge(spread, 1)

                def scale(k):
                    if k >= 3:
                        if k - 3 in on_pool:
                            dve.wait_ge(pool_lo_done, on_pool.index(k - 3) + 1)
                        else:
                            dve.wait_ge(lo_done, sum(n not in on_pool for n in range(k - 2)))
                    dve.scalar_tensor_tensor(
                        out=sq[:, k % 3].rearrange("p (g t) -> p g t", g=NG),
                        in0=src[:, k].rearrange("p (g t) -> p g t", g=NG), scalar=m.cols_a[:, g + k:g + k + 1],
                        in1=ps[:, :, 0:TG], op0=ALU.mult, op1=ALU.mult).then_inc(scaled, 1)

                scale(0)
                for k in range(KD):
                    if k + 1 < KD:
                        scale(k + 1)
                    if k not in on_pool:
                        dve.wait_ge(hi_done, k + 1)
                        dve.tensor_tensor(lo[:, k], sq[:, k % 3], hi[:, k].bitcast(F32), ALU.subtract).then_inc(
                            lo_done, 1)


class WeightRing:

    def __init__(self, nc, ctx, tag, off):
        at = nc.alloc_sbuf_tensor_at
        self.raw = [at(f"{tag}_raw{s}", [P, KD, P], F32, offset=off + s * 4096) for s in range(2)]
        self.hi = [at(f"{tag}_whi{s}", [P, KD, P], F32R, offset=off + 8192 + s * 4096) for s in range(2)]
        self.lo = [at(f"{tag}_wlo{s}", [P, KD, P], F32R, offset=off + 16384 + s * 4096) for s in range(2)]


class Taps:

    PAIRS_OF_INPUTS = 2
    FIRST_LOOP = 3
    PER_TILE = 3

    def __init__(self, nc, m, ctx):
        self.m = m
        self.a_val, self.gate = m.proj[:, T_A:T_A + 2], m.proj[:, T_GATE:T_GATE + 2]
        self.pad = nc.alloc_sbuf_tensor_at("tp_pad", [P, 2, KA - 1 + SEQ], F32, offset=O_PROJ + T_QC * T * 4)
        self.gated, self.u_done, self.zeroed, self.padded, self.a_conv = semaphores(
            nc, ctx, "tp_gated", "tp_u_done", "tp_zeroed", "tp_padded", "tp_a_conv")
        self.end_loop = self.FIRST_LOOP + (KA - 1) // (2 * self.PER_TILE)
        assert (KA - 1) % (2 * self.PER_TILE) == 0 and 2 * self.end_loop <= T_QC

    def w(self, j, tap):
        c = CONV_A_W + 2 * tap + j
        return self.m.cols_a[:, c:c + 1]

    def scalar(self, act):
        act.activation(self.gate, self.gate, ACT.Sigmoid).then_inc(self.gated, 1)
        act.wait_ge(self.u_done, 1)
        act.copy(self.pad[:, :, KA - 1:], self.a_val[:, :, 0:SEQ]).then_inc(self.padded, 1)

    def gpsimd(self, pool):
        pool.memset(self.pad[:, :, 0:KA - 1], 0.0).then_inc(self.zeroed, 1)

    def multiply(self, dve):
        dve.wait_ge(self.gated, 1)
        dve.tensor_tensor(self.a_val, self.a_val, self.gate, ALU.mult).then_inc(self.u_done, 1)

    def first(self, dve):
        dve.wait_ge(self.zeroed, 1)
        dve.wait_ge(self.padded, 1)
        for j in range(2):
            dve.tensor_scalar(self.gate[:, j, 0:SEQ], self.pad[:, j, 0:SEQ], self.w(j, 0),
                              self.m.cols_a[:, CONV_A_B + j:CONV_A_B + j + 1], ALU.mult, ALU.add).then_inc(
                                  self.a_conv, 1)

    def some(self, dve, i, s):
        for n in range(self.PER_TILE):
            tap = lambda scale, more: i * (2 * self.PER_TILE * scale) + (
                (s * self.PER_TILE + n + 1 - 2 * self.PER_TILE * self.FIRST_LOOP) * scale + more)
            for j in range(2):
                dve.wait_ge(self.a_conv, tap(2, j - 1))
                dve.scalar_tensor_tensor(
                    out=self.gate[:, j, 0:SEQ], in0=self.pad[:, j, bass.ds(tap(1, 0), SEQ)],
                    scalar=self.m.cols_a[:, bass.ds(tap(2, CONV_A_W + j), 1)], in1=self.gate[:, j, 0:SEQ],
                    op0=ALU.mult, op1=ALU.add).then_inc(self.a_conv, 1)


def project(nc, m, tag, w, spans, hi, lo, out, with_taps=False):
    with Phase(nc) as ctx:
        ring = WeightRing(nc, ctx, tag, O_W)
        ps = [ctx.enter_context(nc.psum_tensor(f"{tag}_ps{s}", [P, NG, 512], F32)) for s in range(2)]
        w_hi, w_lo_2_ahead, multiplied_2_ahead, copied_2_ahead = semaphores(
            nc, ctx, *[f"{tag}_{n}" for n in ("w_hi", "w_lo_2_ahead", "multiplied_2_ahead", "copied_2_ahead")])
        w_in = semaphores(nc, ctx, f"{tag}_w_in0", f"{tag}_w_in1")
        firsts = [sum(n for _, n in spans[:i]) for i in range(len(spans))]
        pairs = sum(n for _, n in spans) // 2
        taps = Taps(nc, m, ctx) if with_taps else None
        with nc.Block() as block:

            @block.gpsimd
            def _(pool):
                if taps:
                    taps.gpsimd(pool)

            @block.sync
            def _(sp):
                for (col, tiles), t0 in zip(spans, firsts):
                    with sp.Fori(0, tiles // 2) as i:
                        for s in range(2):
                            sp.wait_ge(w_lo_2_ahead, i * 2 + (t0 + s + 1))
                            sp.dma_start(ring.raw[s][:], w.rearrange("(k p) n -> p k n", p=P)[
                                :, :, bass.ds(i * (2 * P) + (col + s * P), P)]).then_inc(w_in[s], 16)

            @block.scalar
            def _(act):
                def cut(i, s):
                    act.wait_ge(w_in[s], i * 16 + 16)
                    act.wait_ge(multiplied_2_ahead, i * 2 + (s + 1))
                    act.copy(ring.hi[s][:], ring.raw[s][:]).then_inc(w_hi, 1)

                first = 0
                if taps:
                    first = Taps.FIRST_LOOP
                    for i in range(first):
                        for s in range(2):
                            cut(i, s)
                    act.wait_ge(copied_2_ahead, 2 + 2 * Taps.PAIRS_OF_INPUTS)
                    taps.scalar(act)
                with act.Fori(first, pairs) as i:
                    for s in range(2):
                        cut(i, s)

            @block.vector
            def _(dve):
                dve.sem_inc(w_lo_2_ahead, 2)
                dve.sem_inc(copied_2_ahead, 2)

                def cut(i, s):
                    dve.wait_ge(w_hi, i * 2 + (s + 1))
                    dve.tensor_tensor(ring.lo[s % 2][:], ring.raw[s % 2][:], ring.hi[s % 2][:].bitcast(F32),
                                      ALU.subtract).then_inc(w_lo_2_ahead, 1)

                def copy(i, s):
                    dve.wait_ge(multiplied_2_ahead, i * 2 + (s + 3))
                    dve.tensor_copy(out[:, bass.ds(i * 2 + s, 1), :].rearrange("p a (g t) -> p (a g) t", g=NG),
                                    ps[s][:, :, 0:TG]).then_inc(copied_2_ahead, 1)

                def pair(i, between):
                    for s in range(2):
                        cut(i, s + 1)
                        between(i, s)
                        copy(i, s)

                nothing = lambda i, s: None
                cut(0, 0)
                if taps:
                    with dve.Fori(0, Taps.PAIRS_OF_INPUTS) as i:
                        pair(i, nothing)
                    pair(Taps.PAIRS_OF_INPUTS, lambda i, s: taps.first(dve) if s else taps.multiply(dve))
                    with dve.Fori(Taps.FIRST_LOOP, taps.end_loop) as i:
                        pair(i, lambda i, s: taps.some(dve, i, s))
                    dve.wait_ge(taps.a_conv, 2 * KA)
                with dve.Fori(taps.end_loop if taps else 0, pairs - 1) as i:
                    pair(i, nothing)
                cut(pairs - 1, 1)
                copy(pairs - 1, 0)
                copy(pairs - 1, 1)

            @block.tensor
            def _(pe):
                pe.sem_inc(multiplied_2_ahead, 2)
                with pe.Fori(0, pairs) as i:
                    for s in range(2):
                        pe.wait_ge(w_lo_2_ahead, i * 2 + (s + 3))
                        pe.wait_ge(copied_2_ahead, i * 2 + (s + 1))
                        for k in range(KD):
                            for n, (a, b) in enumerate(((ring.hi, hi), (ring.hi, lo), (ring.lo, hi))):
                                for g in range(NG):
                                    last = pe.matmul(ps[s][:, g, 0:TG], a[s][:, k],
                                                     b[:, k, g * TG:(g + 1) * TG],
                                                     start=(k == 0 and n == 0),
                                                     stop=(k == KD - 1 and n == 2))
                        last.then_inc(multiplied_2_ahead, 1)


def project_rows(nc, m, hi, lo):
    with Phase(nc) as ctx:
        at = nc.alloc_sbuf_tensor_at
        raw = at("wv_raw", [P, KD, NV], F32, offset=O_PROJ)
        w_hi = at("wv_hi", [P, KD, NV], F32R, offset=O_PROJ + KD * NV * 4)
        w_lo = at("wv_lo", [P, KD, NV], F32R, offset=O_PROJ + 2 * KD * NV * 4)
        ps = ctx.enter_context(nc.psum_tensor("ps_rows", [P, 4, 512], F32))
        w_in, hi_cut, lo_cut, multiplied, copied = semaphores(
            nc, ctx, "wv_in", "wv_hi_cut", "wv_lo_cut", "rows_multiplied", "rows_copied")
        w = m.w_in[0].rearrange("(k p) n -> p k n", p=P)
        cleared, = semaphores(nc, ctx, "rows_cleared")
        with nc.Block() as block:

            @block.gpsimd
            def _(pool):
                pool.memset(m.vtok[:, NC], 0.0).then_inc(cleared, 1)

            @block.sync
            def _(sp):
                sp.wait_ge(m.x_spilled, 16)
                for k in range(KD):
                    sp.dma_start(raw[:, k, 0:DW + H], w[:, k, COL_VC:N_IN]).then_inc(w_in, 16)
                sp.dma_start(raw[:, :, DW + H:NV], w[:, :, COL_BETA:COL_QC]).then_inc(w_in, 16)

            @block.scalar
            def _(act):
                act.wait_ge(w_in, 16 * (KD + 1))
                for k in range(KD):
                    act.copy(w_hi[:, k], raw[:, k]).then_inc(hi_cut, 1)

            @block.vector
            def _(dve):
                for k in range(KD):
                    dve.wait_ge(hi_cut, k + 1)
                    dve.tensor_tensor(w_lo[:, k], raw[:, k], w_hi[:, k].bitcast(F32), ALU.subtract).then_inc(lo_cut, 1)
                for c in range(NC + 1):
                    rows = P if c < NC else NS
                    dve.wait_ge(multiplied, c + 1)
                    if c == NC:
                        dve.wait_ge(cleared, 1)
                    dve.tensor_copy(m.vtok[0:rows, c], ps[0:rows, c % 4, 0:NV]).then_inc(copied, 1)

            @block.tensor
            def _(pe):
                for c in range(NC + 1):
                    rows = P if c < NC else NS
                    if c >= 4:
                        pe.wait_ge(copied, c - 3)
                    for k in range(KD):
                        if c == 0:
                            pe.wait_ge(lo_cut, k + 1)
                        for n, (a, b) in enumerate(((hi, w_hi), (lo, w_hi), (hi, w_lo))):
                            last = pe.matmul(ps[0:rows, c % 4, 0:NV], a[:, k, c * P:c * P + rows], b[:, k],
                                             start=(k == 0 and n == 0), stop=(k == KD - 1 and n == 2))
                    last.then_inc(multiplied, 1)


def convolve(nc, m):
    with Phase(nc) as ctx:
        at = nc.alloc_sbuf_tensor_at
        off = O_H + KD * T * 4
        acc = at("cv_acc", [P, 3, T], F32, offset=off)
        off += 3 * T * 4
        sa_rows = at("cv_sa_rows", [4 * (KA - 1), 2, CA], F32, offset=off)
        sb_rows = at("cv_sb_rows", [NS * (KB - 1), 3 * DW], F32, offset=off + 2048)
        sa = at("cv_sa", [P, 2, NS, KA - 1], F32, offset=off + 6656)
        sb = at("cv_sb", [P, 9, NS, KB - 1], F32, offset=off + 8576)
        tap_a = at("cv_tap_a", [P, NS, KA - 1], F32, offset=off + 9440)
        part = at("cv_part", [P, NS], F32, offset=off + 10400)
        part_b = at("cv_part_b", [P, 9 * NS], F32, offset=off + 10432)
        tap_b = at("cv_tap_b", [P, 9, NS, KB - 1], F32, offset=off + 21344)
        a_rows = at("cv_a_rows", [KA - 1 + NS, CA], F32, offset=off + 10720)
        b_rows = at("cv_b_rows", [KB - 1 + NS, 3 * DW], F32, offset=off + 11744)
        k_rows = at("cv_k_rows", [P, 2, DW], F32, offset=off + 16384)
        small = at("cv_small", [TT, 3, NT * 2 * H], F32, offset=off + 19456)
        small_a = at("cv_small_a", [TT, 3, NT], F32, offset=off + 21184)
        assert off + 22208 + 2 * T * 4 <= O_FOX
        sq_a = at("cv_sq_a", [P, 2, T], F32, offset=off + 22208)
        a_val, a_sum = m.proj[:, T_A:T_A + 2], m.proj[:, T_GATE:T_GATE + 2]
        ps = ctx.enter_context(nc.psum_tensor("cv_ps", [P, 8, 512], F32))
        ps_rows, ps_state, ps_a, ps_k = ps[:, 0:3], ps[:, 3:5], ps[:, 5], ps[:, 6:8]
        wide = lambda n: ps[:, 3 * (n % 2):3 * (n % 2) + 3, 0:TG]
        names = ("states_in", "states_turned", "states_copied", "a_turned",
                 "a_rows_done", "b_turned", "b_rows_done", "k_turned", "k_copied", "b_conv", "b_free_3_ahead", "b_squared",
                 "b_silu", "b_eps", "b_rooted", "b_inverted", "b_inv_turned", "b_inv_copied", "b_spread", "b_normed", "chain", "z_silu",
                 "a_samples", "a_mean", "a_centred", "a_squared", "a_summed", "a_eps", "a_rooted", "a_inverted", "a_spread",
                 "a_scaled", "stored")
        (states_in, states_turned, states_copied, a_turned, a_rows_done, b_turned,
         b_rows_done, k_turned, k_copied, b_conv, b_free_3_ahead, b_squared, b_silu, b_eps, b_rooted, b_inverted, b_inv_turned, b_inv_copied, b_spread,
         b_normed, chain, z_silu, a_samples, a_mean, a_centred, a_squared, a_summed, a_eps, a_rooted, a_inverted,
         a_spread, a_scaled, stored) = semaphores(nc, ctx, *["cv_" + n for n in names])
        k_stored = semaphores(nc, ctx, "cv_k_stored0", "cv_k_stored1")
        grouped = lambda x: x.rearrange("p (g t) -> p g t", g=NG)
        w_a = lambda j, tap, n=1: m.cols_a[:, CONV_A_W + 2 * tap + j:CONV_A_W + 2 * (tap + n - 1) + j + 1:2]
        w_b = lambda j, tap, n=1: m.cols_b[:, 9 * tap + j:9 * (tap + n - 1) + j + 1:9]
        y_a = m.yT[:, 0:2]
        with nc.Block() as block:

            @block.sync
            def _(sp):
                for e in range(2):
                    sp.dma_start(sa_rows[:, e], m.state_conv_a[0, e * 4:(e + 1) * 4].rearrange(
                        "b w c -> (b w) c")).then_inc(states_in, 16)
                sp.dma_start(sb_rows[:], m.state_conv_b[0].rearrange("b w c -> (b w) c")).then_inc(states_in, 16)
                sp.dma_start(m.o_conv_a_s[0, :, 0:KA - 2], m.state_conv_a[0, :, 1:KA - 1]).then_inc(stored, 16)
                sp.dma_start(m.o_conv_b_s[0, :, 0:KB - 2], m.state_conv_b[0, :, 1:KB - 1]).then_inc(stored, 16)
                sp.wait_ge(b_rows_done, 1)
                sp.dma_start(m.o_conv_b_p[0, 0], b_rows[0:KB - 1]).then_inc(stored, 16)
                sp.dma_start(m.o_conv_b_s[0, :, KB - 2], b_rows[KB - 1:KB - 1 + NS]).then_inc(stored, 16)
                sp.wait_ge(a_rows_done, 1)
                sp.dma_start(m.o_conv_a_p[0, 0], a_rows[0:KA - 1]).then_inc(stored, 16)
                sp.dma_start(m.o_conv_a_s[0, :, KA - 2], a_rows[KA - 1:KA - 1 + NS]).then_inc(stored, 16)
                sp.dma_start(m.o_v_p[0, 0].rearrange("(c p) h d -> p c (h d)", p=P), m.vtok[:, 0:NC, 0:DW]).then_inc(
                    stored, 16)
                sp.dma_start(m.o_v_s[0, :, 0].rearrange("b h d -> b (h d)"), m.vtok[0:NS, NC, 0:DW]).then_inc(
                    stored, 16)
                for c in range(NC + 1):
                    sp.wait_ge(k_copied, c + 1)
                    if c < NC:
                        sp.dma_start(m.o_k_p[0, 0, c * P:(c + 1) * P].rearrange("t h d -> t (h d)"),
                                     k_rows[:, c % 2]).then_inc(k_stored[c % 2], 16)
                    else:
                        sp.dma_start(m.o_k_s[0, :, 0].rearrange("b h d -> b (h d)"),
                                     k_rows[0:NS, c % 2]).then_inc(k_stored[c % 2], 16)
                sp.wait_ge(k_stored[0], 16 * 5)
                sp.wait_ge(k_stored[1], 16 * 4)
                sp.wait_ge(stored, 16 * 8)

            @block.tensor
            def _(pe):
                pe.sem_inc(b_free_3_ahead, 3)
                for j in range(9):
                    last = pe.transpose(ps_rows[0:11, j // 3, j % 3 * P:j % 3 * P + P],
                                        m.proj[:, T_QB + j, SEQ - KB + 1:T], m.ident[:])
                last.then_inc(b_turned, 1)
                pe.wait_ge(states_in, 48)
                for e in range(2):
                    for j in range(2):
                        pe.transpose(ps_state[:, 0, (2 * j + e) * 120:(2 * j + e + 1) * 120],
                                     sa_rows[:, e, j * P:(j + 1) * P], m.ident[0:120, 0:120])
                for j in range(9):
                    last = pe.transpose(ps_state[:, 1, j * 24:(j + 1) * 24], sb_rows[:, j * P:(j + 1) * P],
                                        m.ident[0:24, 0:24])
                last.then_inc(states_turned, 1)
                for j in range(2):
                    last = pe.transpose(ps_a[0:KA - 1 + NS, j * P:(j + 1) * P], a_val[:, j, SEQ - KA + 1:T], m.ident[:])
                last.then_inc(a_turned, 1)
                for c in range(NC + 1):
                    rows = P if c < NC else NS
                    if c >= 2:
                        pe.wait_ge(k_copied, c - 1)
                    for j in range(PAIRS):
                        last = pe.transpose(ps_k[0:rows, c % 2, j * P:(j + 1) * P],
                                            m.proj[:, T_KC + j, c * P:c * P + rows], m.ident[:])
                    last.then_inc(k_turned, 1)
                pe.wait_ge(a_samples, 2)
                pe.wait_ge(states_copied, 1)
                pe.wait_ge(a_rows_done, 1)
                for j in range(2):
                    for g in range(NG):
                        last = pe.matmul(wide(1)[:, g], m.ones[:], a_sum[:, j, g * TG:(g + 1) * TG],
                                         start=(j == 0), stop=(j == 1))
                last.then_inc(a_mean, 1)
                pe.wait_ge(k_copied, NC + 1)
                for j in range(6):
                    pe.wait_ge(b_squared, j + 1)
                    for c in range(NT):
                        last = pe.matmul(ps_k[0:TT, 0, c * 12 + 2 * j:c * 12 + 2 * j + 2],
                                         acc[:, j % 3, c * TT:(c + 1) * TT], m.head_ones[:, 0:P:HD],
                                         start=True, stop=True)
                    last.then_inc(b_free_3_ahead, 1)
                for j in range(2):
                    pe.wait_ge(a_squared, j + 1)
                    for c in range(NT):
                        last = pe.matmul(ps_k[0:TT, 1, c:c + 1], sq_a[:, j, c * TT:(c + 1) * TT], m.ones[:, 0:1],
                                         start=(j == 0 and c == 0), stop=(j == 1), skip_group_check=True)
                last.then_inc(a_summed, 1)
                pe.wait_ge(b_inverted, 1)
                for c in range(NT):
                    g, t = divmod(c * TT, TG)
                    last = pe.transpose(ps_rows[0:2 * H, g, t:t + TT], small[:, 1, c * 2 * H:(c + 1) * 2 * H],
                                        m.ident[0:TT, 0:TT])
                last.then_inc(b_inv_turned, 1)
                pe.wait_ge(b_inv_copied, 1)
                for j in range(6):
                    if j >= 2:
                        pe.wait_ge(b_normed, j - 1)
                    for g in range(NG):
                        last = pe.matmul(wide(j)[:, g], m.head_rows[:, j], acc[0:2 * H, 0, g * TG:(g + 1) * TG],
                                         start=True, stop=True)
                    last.then_inc(b_spread, 1)
                pe.wait_ge(a_inverted, 1)
                pe.wait_ge(b_normed, 5)
                spread_tokens(pe, m, ps_rows, small_a[:, 1]).then_inc(a_spread, 1)

            @block.scalar
            def _(act):
                act.wait_ge(b_turned, 1)
                for g in range(NG):
                    last = act.copy(b_rows[:, g * DW:(g + 1) * DW], ps_rows[0:11, g, 0:DW])
                last.then_inc(b_rows_done, 1)
                act.wait_ge(states_turned, 1)
                act.copy(sa[:].rearrange("p j b w -> p (j b w)"), ps_state[:, 0, 0:480])
                act.copy(sb[:].rearrange("p j b w -> p (j b w)"), ps_state[:, 1, 0:216]).then_inc(states_copied, 1)
                act.wait_ge(a_turned, 1)
                act.copy(a_rows[:], ps_a[0:KA - 1 + NS, 0:CA]).then_inc(a_rows_done, 1)
                for c in range(NC + 1):
                    rows = P if c < NC else NS
                    act.wait_ge(k_turned, c + 1)
                    if c >= 2:
                        act.wait_ge(k_stored[c % 2], 16 * (c // 2))
                    act.copy(k_rows[0:rows, c % 2], ps_k[0:rows, c % 2, 0:DW]).then_inc(k_copied, 1)
                for j in range(3):
                    act.activation(m.proj[:, T_Z + j], m.proj[:, T_Z + j], ACT.Silu).then_inc(z_silu, 1)
                for j in range(9):
                    act.wait_ge(b_conv, 5 * (j + 1))
                    act.activation(m.proj[:, T_QB + j], acc[:, j % 3], ACT.Silu).then_inc(b_silu, 1)
                    if j < 6:
                        act.wait_ge(b_silu, j + 1)
                        act.activation(acc[:, j % 3], m.proj[:, T_QB + j], ACT.Square).then_inc(b_squared, 1)
                for j in range(2):
                    act.wait_ge(a_centred, j + 1)
                    act.activation(sq_a[:, j], y_a[:, j], ACT.Square).then_inc(a_squared, 1)
                act.wait_ge(b_eps, 1)
                act.activation(small[:, 1], small[:, 0], ACT.Sqrt).then_inc(b_rooted, 1)
                root(act, small_a, a_eps).then_inc(a_rooted, 1)
                act.wait_ge(b_inv_turned, 1)
                act.copy(grouped(acc[0:2 * H, 0]), ps_rows[0:2 * H, :, 0:TG]).then_inc(b_inv_copied, 1)
                for j in range(2):
                    act.wait_ge(a_scaled, j + 1)
                    act.activation(y_a[:, j], y_a[:, j], ACT.Silu, scale=m.cols_a[:, LN_G + j:LN_G + j + 1],
                                   bias=m.cols_a[:, LN_B + j:LN_B + j + 1])

            @block.gpsimd
            def _(pool):
                for b in range(NS):
                    for g in range(NPAGE):
                        page = pool.value_load(m.pages[0:1, b * NPAGE + g:b * NPAGE + g + 1], min_val=0,
                                               max_val=NPHYS - 1)
                        pool.dma_start(m.fs_logf[:, b, g], m.cache_logf[0, bass.ds(page, 1)].rearrange(
                            "a t h -> (a t) h")).then_inc(m.logf_in, 16)

            @block.vector
            def _(dve):
                step = Chain(dve, chain)
                dve.wait_ge(states_copied, 1)
                for j in range(2):
                    step(dve.tensor_tensor(tap_a[:], sa[:, j], w_a(j, 0, KA - 1).unsqueeze(1).broadcast_to(
                        [P, NS, KA - 1]), ALU.mult))
                    step(dve.tensor_reduce(part[:], tap_a[:], AX_X, ALU.add))
                    step(dve.scalar_tensor_tensor(out=part[:], in0=a_val[:, j, SEQ:T], scalar=w_a(j, KA - 1),
                                                  in1=part[:], op0=ALU.mult, op1=ALU.add))
                    dve.tensor_scalar(a_sum[:, j, SEQ:T], part[:], m.cols_a[:, CONV_A_B + j:CONV_A_B + j + 1],
                                      None, ALU.add).then_inc(a_samples, 1)
                for j in range(9):
                    last = dve.tensor_tensor(tap_b[:, j], sb[:, j], w_b(j, 0, KB - 1).unsqueeze(1).broadcast_to(
                        [P, NS, KB - 1]), ALU.mult)
                step(last)
                step(dve.tensor_reduce(part_b[:], tap_b[:].rearrange("p j b w -> p (j b) w"), AX_X, ALU.add))

                dve.wait_ge(b_turned, 1)
                with dve.Fori(0, 3) as i:
                    for s in range(3):
                        tile = m.proj[:, bass.ds(i * 3 + (T_QB + s), 1), :].rearrange("p a t -> p (a t)")
                        w = lambda tap: m.cols_b[:, bass.ds(i * 3 + (9 * tap + s), 1)]
                        dve.wait_ge(b_free_3_ahead, i * 3 + (s + 1))
                        dve.tensor_scalar(acc[:, s, 0:T], tile, w(3), None, ALU.mult).then_inc(b_conv, 1)
                        for n, tap in enumerate((2, 1, 0)):
                            dve.wait_ge(b_conv, i * 15 + (s * 5 + n + 1))
                            dve.scalar_tensor_tensor(out=acc[:, s, n + 1:SEQ], in0=tile[:, 0:SEQ - n - 1],
                                                     scalar=w(tap), in1=acc[:, s, n + 1:SEQ],
                                                     op0=ALU.mult, op1=ALU.add).then_inc(b_conv, 1)
                        dve.tensor_tensor(acc[:, s, SEQ:T], acc[:, s, SEQ:T], part_b[:, bass.ds(i * 24 + s * 8, NS)],
                                          ALU.add).then_inc(b_conv, 1)

                dve.wait_ge(a_mean, 1)
                for j in range(2):
                    dve.scalar_tensor_tensor(out=grouped(y_a[:, j]), in0=wide(1), scalar=-1.0 / CA,
                                             in1=grouped(a_sum[:, j]), op0=ALU.mult, op1=ALU.add).then_inc(a_centred, 1)
                dve.wait_ge(b_free_3_ahead, 3 + 6)
                dve.tensor_scalar(small[:, 0], ps_k[0:TT, 0, 0:NT * 2 * H], 1e-6, None, ALU.add).then_inc(b_eps, 1)
                dve.wait_ge(a_summed, 1)
                dve.tensor_scalar(small_a[:, 0], ps_k[0:TT, 1, 0:NT], 1.0 / CA, LN_EPS, ALU.mult, ALU.add).then_inc(
                    a_eps, 1)
                inverse_root(dve, step, small, b_rooted).then_inc(b_inverted, 1)
                inverse_root(dve, step, small_a, a_rooted).then_inc(a_inverted, 1)
                for j in range(6):
                    dve.wait_ge(b_spread, j + 1)
                    tile = grouped(m.proj[:, T_QB + j])
                    dve.scalar_tensor_tensor(out=tile, in0=tile, scalar=SCALE if j < 3 else 1.0,
                                             in1=wide(j), op0=ALU.mult, op1=ALU.mult).then_inc(b_normed, 1)
                dve.wait_ge(a_spread, 1)
                for j in range(2):
                    dve.tensor_tensor(grouped(y_a[:, j]), grouped(y_a[:, j]), ps_rows[:, :, 0:TG],
                                      ALU.mult).then_inc(a_scaled, 1)


def gates(nc, m):
    with Phase(nc) as ctx:
        off = O_H + KD * T * 4
        at = nc.alloc_sbuf_tensor_at
        n = NC + 1
        x = at("gt_x", [P, n, 2 * H], F32, offset=off)
        e = at("gt_e", [P, n, 2 * H], F32, offset=off + 512)
        w = at("gt_w", [P, n, 2 * H], F32, offset=off + 1024)
        ln = at("gt_ln", [P, n, 2 * H], F32, offset=off + 1536)
        rate = at("gt_rate", [P, H], F32, offset=off + 2048)
        b = at("gt_b", [P, n, H], F32, offset=off + 2080)
        args, exps, ones, logs, chain, stored, done = semaphores(
            nc, ctx, "gt_args", "gt_exps", "gt_ones", "gt_logs", "gt_chain", "gt_stored", "gt_done")
        spread = lambda v: v.unsqueeze(1).broadcast_to([P, n, H])
        raw = m.vtok[:, :, DW:NV]
        later = at("gt_later", [P, NS, NPAGE, H], F32, offset=off + 2560)
        k_rows = at("gt_k_rows", [NS, DW], F32, offset=off + 4096)
        own = at("gt_own", [NS, H], F32, offset=off + 5632)
        ps_q, ps_k, ps_v, ps_bias = [ctx.enter_context(nc.psum_tensor(f"gt_ps_{t}", [P, 512], F32))
                                     for t in ("q", "k", "v", "bias")]
        turned, rows_done, own_done, own_spread, later_summed, biased = semaphores(
            nc, ctx, *["gt_" + t for t in ("turned", "rows_done", "own_done", "own_spread", "later_summed", "biased")])
        flat = lambda t: t.rearrange("p b g h -> p (b g h)")
        with nc.Block() as block:

            @block.sync
            def _(sp):
                sp.wait_ge(done, 1)
                sp.dma_start(m.o_f_p[0, 0].rearrange("(c p) h -> p c h", p=P), m.gates[:, 0:NC, 0:H]).then_inc(
                    stored, 16)
                sp.dma_start(m.o_f_s[0, :, 0], m.gates[0:NS, NC, 0:H]).then_inc(stored, 16)
                sp.wait_ge(stored, 32)

            @block.tensor
            def _(pe):
                for i in range(PAIRS):
                    pe.transpose(ps_q[0:NS, i * P:(i + 1) * P], m.proj[:, T_QC + i, SEQ:T], m.ident[:])
                    pe.transpose(ps_k[0:NS, i * P:(i + 1) * P], m.proj[:, T_KC + i, SEQ:T], m.ident[:])
                    last = pe.transpose(ps_v[:, i * NS:(i + 1) * NS], m.vtok[0:NS, NC, i * P:(i + 1) * P],
                                        m.ident[0:NS, 0:NS])
                last.then_inc(turned, 1)
                pe.wait_ge(later_summed, NPAGE)
                pe.matmul(ps_bias[:, 0:NS * NPAGE * H], m.later[:], flat(m.fs_logf[:]), start=True, stop=False)
                pe.matmul(ps_bias[:, 0:NS * NPAGE * H], m.ones[:], flat(later[:]), start=False, stop=True).then_inc(
                    biased, 1)
                pe.wait_ge(own_done, 1)
                pe.wait_ge(rows_done, 3)
                for b in range(NS):
                    last = pe.matmul(ps_k[:, b * H:(b + 1) * H], m.ident[0:NS, b:b + 1].to_broadcast([NS, P]), own[:],
                                     start=True, stop=True)
                last.then_inc(own_spread, 1)

            @block.scalar
            def _(act):
                act.activation(rate[:], m.rows6[:, H:2 * H], ACT.Exp).then_inc(exps, 1)
                act.activation(b[:], raw[:, :, H:2 * H], ACT.Exp, scale=-1.0).then_inc(exps, 1)
                act.wait_ge(args, 1)
                act.activation(e[:], w[:], ACT.Exp, scale=-1.0).then_inc(exps, 1)
                act.wait_ge(ones, 1)
                act.activation(ln[:], w[:], ACT.Ln).then_inc(logs, 1)
                act.wait_ge(turned, 1)
                act.mul(m.fs_q_rows[:], ps_q[0:NS, 0:DW], SCALE).then_inc(rows_done, 1)
                act.copy(k_rows[:], ps_k[0:NS, 0:DW]).then_inc(rows_done, 1)
                act.copy(m.fs_v_cols[:].rearrange("p m b -> p (m b)"), ps_v[:, 0:PAIRS * NS]).then_inc(rows_done, 1)
                act.wait_ge(biased, 1)
                act.copy(flat(m.fs_logf[:]), ps_bias[:, 0:NS * NPAGE * H])
                act.wait_ge(own_spread, 1)
                act.copy(m.fs_own_all[:], ps_k[:, 0:NS * H])

            @block.vector
            def _(dve):
                step = Chain(dve, chain)
                step(dve.tensor_tensor(x[:, :, 0:H], raw[:, :, 0:H], spread(m.rows6[:, 0:H]), ALU.add))
                step(dve.tensor_scalar(x[:, :, 0:H], x[:, :, 0:H], -1.0, None, ALU.mult))
                step(dve.tensor_tensor(x[:, :, H:2 * H], raw[:, :, 2 * H:3 * H], spread(m.rows6[:, 2 * H:3 * H]),
                                       ALU.add))
                step(dve.scalar_tensor_tensor(out=w[:], in0=x[:], scalar=-1.0, in1=x[:], op0=ALU.mult, op1=ALU.max))
                dve.sem_inc(args, 1)
                dve.wait_ge(exps, 3)
                step(dve.tensor_scalar(w[:], e[:], 1.0, None, ALU.add))
                dve.sem_inc(ones, 1)
                dve.wait_ge(logs, 1)
                step(dve.scalar_tensor_tensor(out=e[:], in0=w[:], scalar=-1.0, in1=e[:], op0=ALU.add,
                                              op1=ALU.subtract))
                step(dve.reciprocal(w[:], w[:]))
                step(dve.tensor_tensor(e[:], e[:], w[:], ALU.mult))
                step(dve.tensor_tensor(ln[:], ln[:], e[:], ALU.subtract))
                step(dve.scalar_tensor_tensor(out=ln[:], in0=x[:], scalar=0.0, in1=ln[:], op0=ALU.max, op1=ALU.add))
                step(dve.tensor_scalar(m.gates[:, :, 0:H], ln[:, :, 0:H], -1.0, None, ALU.mult))
                dve.sem_inc(done, 1)
                step(dve.tensor_scalar(rate[:], rate[:], -1.0, None, ALU.mult))
                step(dve.tensor_tensor(m.gates[:, :, H:2 * H], ln[:, :, H:2 * H], spread(rate[:]), ALU.mult))
                step(dve.tensor_scalar(b[:], b[:], 1.0, None, ALU.add))
                step(dve.reciprocal(m.gates[:, :, 2 * H:3 * H], b[:]))

                dve.wait_ge(rows_done, 3)
                step(dve.tensor_tensor(k_rows[:], k_rows[:], m.fs_q_rows[:], ALU.mult))
                step(dve.tensor_reduce(own[:], k_rows[:].rearrange("p (h d) -> p h d", h=H), AX_X, ALU.add))
                dve.tensor_tensor(own[:], own[:], m.gates[0:NS, NC, 0:H], ALU.subtract).then_inc(own_done, 1)
                dve.memset(later[:, :, NPAGE - 1], 0.0).then_inc(later_summed, 1)
                dve.wait_ge(m.logf_in, 16 * NS * NPAGE)
                for g in reversed(range(NPAGE - 1)):
                    dve.wait_ge(later_summed, NPAGE - 1 - g)
                    dve.tensor_tensor(later[:, :, g], later[:, :, g + 1], m.fs_logf[:, :, g + 1], ALU.add).then_inc(
                        later_summed, 1)


def delta_rule(nc, m):
    with Phase(nc) as ctx:
        off = O_H + KD * T * 4

        def put(name, shape):
            nonlocal off
            t = nc.alloc_sbuf_tensor_at("dl_" + name, shape, F32, offset=off)
            n = 4
            for d in shape[1:]:
                n *= d
            off += (n + 31) // 32 * 32
            return t

        qkv = put("qkv", [P, 9, P])
        gb = put("gb", [P, 2 * H])
        cums = put("cums", [P, 3 * H])
        exps = put("exps", [P, 3 * H])
        beta_exp = put("beta_exp", [P, H])
        decay = put("decay", [P, 2, 3, P])
        beta_decay = put("beta_decay", [P, 2, 3, P])
        lower_t = put("lower_t", [P, 2, 3, P])
        qk_t = put("qk_t", [P, 2, 3, P])
        y = put("y", [P, 2, 3, P])
        t_tt = put("t_tt", [P, 2, 2, 3, P])
        rhs = put("rhs", [P, H, P])
        k_decayed = put("k_decayed", [P, H, HD])
        q_exp = put("q_exp", [P, PAIRS, P])
        q_decayed = put("q_decayed", [P, PAIRS, P])
        neg_w = put("neg_w", [P, PAIRS, P])
        v_new = put("v_new", [P, 2, 3, HD])
        sequence = put("sequence", [NS, 1])
        assert off <= O_TAIL_KV, off
        ps = ctx.enter_context(nc.psum_tensor("dl_ps", [P, 8, 512], F32))
        three = lambda b: ps[:, b, 0:3 * P].rearrange("p (m t) -> p m t", m=3)
        bx = lambda e: three(e)
        btt = lambda e, n: three(2 + 2 * e + n)
        bs = lambda e: three(6 + e)
        half = lambda e: slice(e * HD, (e + 1) * HD)
        LEVELS = 6
        names = ("staged_1", "gate_staged", "cum_ready", "exp_ready", "beta_ready", "prod_ready", "diff_done",
                 "decay_done", "q_exp_done", "beta_used", "lower_done", "qk_done", "lower_turned", "t_init", "tt_init",
                 "kv_turned_1", "rhs_done", "x_done", "y_done", "tt_done", "t_done", "w_done", "neg_w_done",
                 "v_done", "v_copied", "q_decayed_1", "o_done", "o_copied_2", "s_done", "s_updated_1", "chain",
                 "s_zero", "final_stored", "cums_copied", "sequence_set", "q_spread", "q_used", "scored")
        (staged, gate_staged, cum_ready, exp_ready, beta_ready, prod_ready, diff_done, decay_done, q_exp_done,
         beta_used, lower_done, qk_done, lower_turned, t_init, tt_init, kv_turned_1, rhs_done, x_done, y_done,
         tt_done, t_done, w_done, neg_w_done, v_done, v_copied, q_decayed_1, o_done, o_copied_2, s_done,
         s_updated_1, chain, s_zero, final_stored, cums_copied, sequence_set, q_spread, q_used, scored) = semaphores(nc, ctx, *["dl_" + n for n in names])
        with nc.Block() as block:

            @block.sync
            def _(sp):
                load_pages(sp, m, m.cache_k, 0, m.fs_keys, m.keys_in)
                load_pages(sp, m, m.cache_v, 0, m.fs_values[0], m.values_in[0])
                for b in range(1, NS):
                    sp.wait_ge(scored, b)
                    load_pages(sp, m, m.cache_k, b, m.fs_keys, m.keys_in)
                sp.wait_ge(s_updated_1, NC + 1)
                for e in range(2):
                    sp.dma_start(m.o_delta_p[0, 0].rearrange("(m e) k v -> e k m v", e=2)[e],
                                 m.state[half(e)]).then_inc(final_stored, 16)
                sp.wait_ge(final_stored, 32)

            @block.scalar
            def _(act):
                act.sem_inc(o_copied_2, 2)
                with act.Fori(0, NC) as c:
                    act.wait_ge(kv_turned_1, c + 1)
                    act.wait_ge(q_decayed_1, c + 1)
                    act.copy(qkv[:], m.proj[:, T_QB:T_QB + 9, bass.ds(c * P, P)]).then_inc(staged, 1)
                    act.wait_ge(cums_copied, c + 1)
                    act.wait_ge(s_updated_1, c + 1)
                    act.activation(exps[:], cums[:], ACT.Exp).then_inc(exp_ready, 1)
                    act.copy(sequence[:], m.ident[0:NS, bass.ds(c, 1)]).then_inc(sequence_set, 1)
                    for e in range(2):
                        act.wait_ge(diff_done, c * 2 + (e + 1))
                        act.activation(q_exp[half(e)], bx(e)[half(e)], ACT.Exp).then_inc(q_exp_done, 1)
                        act.activation(decay[:, e], decay[:, e], ACT.Exp).then_inc(decay_done, 1)
                    for lv in range(LEVELS):
                        for e in range(2):
                            act.wait_ge(tt_done, c * (2 * LEVELS) + (2 * lv + e + 1))
                            if lv < LEVELS - 1:
                                act.copy(t_tt[:, e].rearrange("p n m t -> p n (m t)"),
                                         ps[:, 2 + 2 * e:4 + 2 * e, 0:3 * P]).then_inc(t_done, 1)
                            else:
                                act.copy(t_tt[:, e, 1], btt(e, 1)).then_inc(t_done, 1)
                    for e in range(2):
                        act.wait_ge(w_done, c * 2 + (e + 1))
                        act.mul(neg_w[half(e)], bs(e)[half(e)], -1.0).then_inc(neg_w_done, 1)
                    for e in range(2):
                        act.wait_ge(v_done, c * 2 + (e + 1))
                        act.copy(v_new[:, e], bx(e)[:, :, 0:HD]).then_inc(v_copied, 1)
                    for e in range(2):
                        act.wait_ge(o_done, c * 2 + (e + 1))
                        act.copy(m.yT[half(e), 2:2 + PAIRS, bass.ds(c * P, P)], bs(e)[half(e)]).then_inc(o_copied_2, 1)

            @block.gpsimd
            def _(pool):
                pool.sem_inc(q_decayed_1, 1)
                with pool.Fori(0, NC) as c:
                    pool.wait_ge(q_exp_done, c * 2 + 2)
                    pool.wait_ge(staged, c + 1)
                    pool.tensor_tensor(q_decayed[:], qkv[:, 0:3], q_exp[:], ALU.mult).then_inc(q_decayed_1, 1)
                    for e in range(2):
                        pool.wait_ge(lower_done, c * 2 + (e + 1))
                        pool.tensor_tensor(t_tt[:, e, 1], lower_t[:, e],
                                           m.level1_t[:].unsqueeze(1).broadcast_to([P, 3, P]), ALU.mult).then_inc(
                                               chain, 1)
                        pool.wait_ge(chain, c * 2 + (e + 1))
                        pool.tensor_tensor(t_tt[:, e, 1], t_tt[:, e, 1],
                                           m.ident[:].unsqueeze(1).broadcast_to([P, 3, P]), ALU.add).then_inc(
                                               tt_init, 1)

            @block.vector
            def _(dve):
                dve.sem_inc(s_updated_1, 1)
                dve.memset(m.state[:], 0.0).then_inc(s_zero, 1)
                ident3 = m.ident[:].unsqueeze(1).broadcast_to([P, 3, P])
                mask3 = lambda lv: m.level_mask[:, lv].unsqueeze(1).broadcast_to([P, 3, P])
                dve.wait_ge(s_zero, 1)
                with dve.Fori(0, NC) as c:
                    dve.tensor_copy(gb[:].rearrange("p (a h) -> p a h", a=1),
                                    m.gates[:, bass.ds(c, 1), H:3 * H]).then_inc(gate_staged, 1)
                    dve.wait_ge(cum_ready, c + 1)
                    dve.tensor_copy(cums[:], ps[:, 5, 0:3 * H]).then_inc(cums_copied, 1)
                    dve.wait_ge(cums_copied, c + 1)
                    for e in range(2):
                        dve.wait_ge(beta_ready, c * 2 + (e + 1))
                        for i in range(3):
                            last = dve.scalar_tensor_tensor(
                                out=decay[:, e, i], in0=bx(e)[:, i], scalar=cums[:, 2 * i + e:2 * i + e + 1],
                                in1=m.keep_t[:], op0=ALU.subtract, op1=ALU.min)
                        last.then_inc(diff_done, 1)
                    for e in range(2):
                        dve.wait_ge(decay_done, c * 2 + (e + 1))
                        dve.tensor_tensor(beta_decay[:, e], bs(e), decay[:, e], ALU.mult).then_inc(beta_used, 1)
                        dve.wait_ge(prod_ready, c * 2 + (e + 1))
                        dve.wait_ge(beta_used, c * 2 + (e + 1))
                        dve.tensor_tensor(lower_t[:, e], btt(e, 0), beta_decay[:, e], ALU.mult).then_inc(lower_done, 1)
                        dve.tensor_tensor(qk_t[:, e], btt(e, 1), decay[:, e], ALU.mult).then_inc(qk_done, 1)
                    for e in range(2):
                        dve.wait_ge(lower_turned, c * 2 + (e + 1))
                        dve.tensor_tensor(t_tt[:, e, 0], bx(e), mask3(0), ALU.mult).then_inc(t_init, 1)
                        dve.wait_ge(t_init, c * 4 + (2 * e + 1))
                        dve.tensor_tensor(t_tt[:, e, 0], t_tt[:, e, 0], ident3, ALU.add).then_inc(t_init, 1)
                    for lv in range(LEVELS):
                        for e in range(2):
                            dve.wait_ge(x_done, c * (2 * LEVELS) + (2 * lv + e + 1))
                            dve.tensor_tensor(y[:, e], bx(e), mask3(lv + 1), ALU.mult).then_inc(y_done, 1)
                            dve.wait_ge(y_done, c * (4 * LEVELS) + (4 * lv + 2 * e + 1))
                            dve.tensor_tensor(y[:, e], y[:, e], ident3, ALU.add).then_inc(y_done, 1)
                        if lv == 0:
                            dve.wait_ge(exp_ready, c + 1)
                            dve.wait_ge(kv_turned_1, c + 2)
                            heads = lambda v: v.unsqueeze(2).broadcast_to([P, H, HD])
                            rows = lambda b: ps[:, b, 0:DW].rearrange("p (h d) -> p h d", h=H)
                            dve.tensor_tensor(beta_exp[:], gb[:, H:2 * H], exps[:, 0:H], ALU.mult).then_inc(rhs_done, 1)
                            dve.tensor_tensor(rhs[:, :, 0:HD], rows(7), heads(gb[:, H:2 * H]), ALU.mult).then_inc(
                                rhs_done, 1)
                            dve.tensor_tensor(k_decayed[:], rows(6), heads(exps[:, H:2 * H]), ALU.mult).then_inc(
                                rhs_done, 1)
                            dve.wait_ge(rhs_done, c * 4 + 1)
                            dve.tensor_tensor(rhs[:, :, HD:P], rows(6), heads(beta_exp[:]), ALU.mult).then_inc(
                                rhs_done, 1)
                    dve.wait_ge(m.keys_in, c * (16 * NPAGE) + 16 * NPAGE)
                    dve.wait_ge(q_spread, c + 1)
                    keys = m.fs_keys
                    dve.tensor_tensor(keys[:], keys[:], ps[:, 2, 0:DW].unsqueeze(1).broadcast_to([P, NPAGE, DW]),
                                      ALU.mult).then_inc(q_used, 1)
                    dve.wait_ge(q_used, c + 1)
                    dve.tensor_reduce(m.fs_s[:].rearrange("p b g h -> p (b g h)")[:, bass.ds(c * (NPAGE * H), NPAGE * H)],
                                      keys[:].rearrange("p g (h d) -> p (g h) d", h=H), AX_X, ALU.add).then_inc(scored, 1)
                    dve.wait_ge(s_done, c * 2 + 2)
                    for e in range(2):
                        dve.tensor_tensor(m.state[half(e)], m.state[half(e)],
                                          exps[half(e), 2 * H + e:3 * H:2].unsqueeze(2).broadcast_to([HD, PAIRS, HD]),
                                          ALU.mult).then_inc(s_zero, 1)
                    dve.wait_ge(s_zero, c * 4 + 3)
                    dve.tensor_tensor(m.state[half(0)], m.state[half(0)], btt(0, 0)[half(0), :, 0:HD], ALU.add).then_inc(
                        s_zero, 1)
                    dve.tensor_tensor(m.state[half(1)], m.state[half(1)], btt(1, 0)[half(1), :, 0:HD], ALU.add).then_inc(
                        s_zero, 1)
                    dve.wait_ge(s_zero, c * 4 + 5)
                    dve.sem_inc(s_updated_1, 1)

            @block.tensor
            def _(pe):
                pe.sem_inc(kv_turned_1, 1)
                with pe.Fori(0, NC) as c:
                    pe.wait_ge(gate_staged, c + 1)
                    pe.wait_ge(o_copied_2, c * 2 + 2)
                    for n, t in enumerate((m.cumul, m.later, m.ones)):
                        last = pe.matmul(ps[:, 5, n * H:(n + 1) * H], t[:], gb[:, 0:H],
                                         start=True, stop=True)
                    last.then_inc(cum_ready, 1)
                    for e in range(2):
                        for i in range(3):
                            h = 2 * i + e
                            pe.matmul(bx(e)[:, i], gb[:, h:h + 1].to_broadcast([P, P]), m.cumul[:], start=True, stop=True)
                            last = pe.matmul(bs(e)[:, i], gb[:, H + h:H + h + 1].to_broadcast([P, P]), m.ident[:],
                                             start=True, stop=True)
                        last.then_inc(beta_ready, 1)
                    pe.wait_ge(staged, c + 1)
                    pe.wait_ge(cums_copied, c + 1)
                    pe.wait_ge(s_updated_1, c + 1)
                    for e in range(2):
                        for i in range(3):
                            k = qkv[half(e), 3 + i]
                            pe.matmul(btt(e, 0)[:, i], k, k, start=True, stop=True)
                            last = pe.matmul(btt(e, 1)[:, i], k, qkv[half(e), i], start=True, stop=True)
                        last.then_inc(prod_ready, 1)
                    pe.wait_ge(beta_used, c * 2 + 2)
                    for i in range(3):
                        pe.transpose(bs(0)[:, i], qkv[:, 3 + i], m.ident[:])
                        last = pe.transpose(bs(1)[:, i], qkv[:, 6 + i], m.ident[:])
                    last.then_inc(kv_turned_1, 1)
                    for e in range(2):
                        pe.wait_ge(lower_done, c * 2 + (e + 1))
                        pe.wait_ge(q_exp_done, c * 2 + (e + 1))
                        for i in range(3):
                            last = pe.transpose(bx(e)[:, i], lower_t[:, e, i], m.ident[:])
                        last.then_inc(lower_turned, 1)
                    for lv in range(LEVELS):
                        for e in range(2):
                            if lv == 0:
                                pe.wait_ge(t_init, c * 4 + (2 * e + 2))
                                pe.wait_ge(tt_init, c * 2 + (e + 1))
                                pe.wait_ge(qk_done, c * 2 + (e + 1))
                            else:
                                pe.wait_ge(t_done, c * (2 * LEVELS) + (2 * lv + e - 1))
                            for i in range(3):
                                last = pe.matmul(bx(e)[:, i], lower_t[:, e, i], t_tt[:, e, 0, i], start=True, stop=True)
                            last.then_inc(x_done, 1)
                        for e in range(2):
                            pe.wait_ge(y_done, c * (4 * LEVELS) + (4 * lv + 2 * e + 2))
                            for i in range(3):
                                if lv < LEVELS - 1:
                                    pe.matmul(btt(e, 0)[:, i], t_tt[:, e, 1, i], y[:, e, i], start=True, stop=True)
                                last = pe.matmul(btt(e, 1)[:, i], y[:, e, i], t_tt[:, e, 1, i], start=True, stop=True)
                            last.then_inc(tt_done, 1)
                    pe.wait_ge(sequence_set, c + 1)
                    pe.matmul(ps[:, 2, 0:DW], sequence[:].to_broadcast([NS, P]), m.fs_q_rows[:], start=True,
                              stop=True).then_inc(q_spread, 1)
                    pe.wait_ge(rhs_done, c * 4 + 4)
                    for e in range(2):
                        pe.wait_ge(t_done, c * (2 * LEVELS) + (2 * LEVELS - 1 + e))
                        for i in range(3):
                            last = pe.matmul(bs(e)[half(e), i], rhs[:, 2 * i + e, HD:P], t_tt[:, e, 1, i],
                                             start=True, stop=True)
                        last.then_inc(w_done, 1)
                    for e in range(2):
                        pe.wait_ge(neg_w_done, c * 2 + (e + 1))
                        for i in range(3):
                            pe.matmul(bx(e)[:, i, 0:HD], t_tt[:, e, 1, i], rhs[:, 2 * i + e, 0:HD],
                                      start=True, stop=False)
                            last = pe.matmul(bx(e)[:, i, 0:HD], neg_w[half(e), i], m.state[half(e), i],
                                             start=False, stop=True)
                        last.then_inc(v_done, 1)
                    pe.wait_ge(q_decayed_1, c + 2)
                    for e in range(2):
                        pe.wait_ge(v_copied, c * 2 + (e + 1))
                        for i in range(3):
                            pe.matmul(bs(e)[half(e), i], v_new[:, e, i], qk_t[:, e, i], start=True, stop=False)
                            last = pe.matmul(bs(e)[half(e), i], m.state[half(e), i], q_decayed[half(e), i],
                                             start=False, stop=True)
                        last.then_inc(o_done, 1)
                    pe.wait_ge(q_used, c + 1)
                    for e in range(2):
                        for i in range(3):
                            last = pe.matmul(btt(e, 0)[half(e), i, 0:HD], k_decayed[:, 2 * i + e], v_new[:, e, i],
                                             start=True, stop=True)
                        last.then_inc(s_done, 1)


def samples(nc, m):
    with Phase(nc) as ctx:
        off = O_H + KD * T * 4
        at = nc.alloc_sbuf_tensor_at
        keys = at("ds_keys", [P, 3, NS, PAIRS], F32, offset=off + 12288 + 1536 + 64 + 384)
        decay_all = at("ds_decay_all", [P, NS, PAIRS], F32, offset=off + 12288 + 1536 + 64 + 384 + 288)
        state = at("ds_state", [P, NS, PAIRS, HD], F32, offset=off)
        x = at("ds_x", [P, NS, PAIRS, HD], F32, offset=off + 6144)
        v_rows = at("ds_v_rows", [NS, DW], F32, offset=off + 12288)
        ab = at("ds_ab", [NS, 2 * H], F32, offset=off + 13824)
        ab_all = at("ds_ab_all", [P, NS, 2 * H], F32, offset=off + 13888)
        small = at("ds_small", [TT, 3, NT * H], F32, offset=off + 14720)
        inv_rows = at("ds_inv_rows", [H, T], F32, offset=off + 15584)
        sq = m.proj[:, T_QB:T_QB + PAIRS]
        off += 15584 + T * 4 + 32

        def put(name, shape):
            nonlocal off
            t = at("fs_" + name, shape, F32, offset=off)
            n = 4
            for d in shape[1:]:
                n *= d
            off += (n + 31) // 32 * 32
            return t

        N = NS * H
        s_raw, own_all, p, den = m.fs_s, m.fs_own_all, m.fs_p, m.fs_den
        peak = put("peak", [P, N])
        top = put("top", [N, 1])
        top_diag = put("top_diag", [N, N])
        rows = put("rows", [H, EARLY, DW])
        assert off <= O_TAIL_KV, off
        ps = ctx.enter_context(nc.psum_tensor("ds_ps", [P, 8, 512], F32))
        (states_in, decay_done, turned, rows_done, ab_turned, ab_done, keys_scaled, x_ready, x_chain, o_done,
         o_copied, stored, squared, summed, with_eps, rooted, inverted, inv_turned, inv_copied, spread, normed,
         chain) = semaphores(
             nc, ctx, *["ds_" + n for n in (
                 "states_in", "decay_done", "turned", "rows_done", "ab_turned", "ab_done", "keys_scaled", "x_ready",
                 "x_chain", "o_done", "o_copied", "stored", "squared", "summed", "with_eps", "rooted",
                 "inverted", "inv_turned", "inv_copied", "spread", "normed", "chain")])
        (peaked, peak_turned, topped, diag_done, top_spread, shifted, exp_done, added, den_spread, den_copied,
         values_done, values_copied, values_turned, fox_chain) = semaphores(
             nc, ctx, *["fs_" + n for n in (
                 "peaked", "peak_turned", "topped", "diag_done", "top_spread", "shifted", "exp_done", "added",
                 "den_spread", "den_copied", "values_done", "values_copied", "values_turned", "chain")])
        flat = lambda t: t.rearrange("p b g h -> p (b g h)")
        ps_fox = ps[:, 7]
        ps_o = ps[:, 7, 0:PAIRS * NS * H].rearrange("p (m b h) -> p m b h", m=PAIRS, b=NS)
        half = lambda e: slice(e * HD, (e + 1) * HD)
        seq_banks = lambda e: ps[:, 3 * e:3 * e + 3].rearrange("p b n -> p (b n)").rearrange(
            "p (b m v) -> p b m v", b=NS, m=PAIRS)
        per_head = lambda e, c: ab_all[half(e), :, c + e:c + H:2]
        with nc.Block() as block:

            @block.sync
            def _(sp):
                for e in range(2):
                    for i in range(PAIRS):
                        sp.dma_start(state[half(e), :, i], m.state_delta[0, :, 2 * i + e].rearrange(
                            "b k v -> k b v")).then_inc(states_in, 16)
                load_pages(sp, m, m.cache_v, 1, m.fs_values[1], m.values_in[1])
                sp.wait_ge(x_chain, 5)
                for e in range(2):
                    for i in range(PAIRS):
                        sp.dma_start(m.o_delta_s[0, :, 2 * i + e].rearrange("b k v -> k b v"),
                                     state[half(e), :, i]).then_inc(stored, 16)
                sp.wait_ge(stored, 96)

            @block.tensor
            def _(pe):
                for i in range(PAIRS):
                    last = pe.transpose(ps[0:NS, 3, i * P:(i + 1) * P], m.proj[:, T_VB + i, SEQ:T], m.ident[:])
                last.then_inc(turned, 1)
                pe.wait_ge(decay_done, 2)
                for b in range(NS):
                    last = pe.matmul(ps[:, 6, b * 2 * H:(b + 1) * 2 * H], m.ident[0:NS, b:b + 1].to_broadcast([NS, P]),
                                     ab[:], start=True, stop=True)
                last.then_inc(ab_turned, 1)
                pe.wait_ge(peaked, 1)
                pe.transpose(ps_fox[0:N, 0:P], peak[:], m.ident[:]).then_inc(peak_turned, 1)
                pe.wait_ge(rows_done, 1)
                for e in range(2):
                    for b in range(NS):
                        for i in range(PAIRS):
                            h = 2 * i + e
                            if e + b + i == 0:
                                pe.wait_ge(keys_scaled, 5)
                                pe.wait_ge(states_in, 96)
                            pe.matmul(seq_banks(e)[half(e), b, i], m.ident[0:NS, b:b + 1].to_broadcast([NS, HD]),
                                      v_rows[:, h * HD:(h + 1) * HD], start=True, stop=False)
                            last = pe.matmul(seq_banks(e)[half(e), b, i],
                                             keys[half(e), 0, b, i:i + 1].to_broadcast([HD, HD]), state[half(e), b, i],
                                             start=False, stop=True)
                    last.then_inc(x_ready, 1)
                    if e == 0:
                        pe.wait_ge(diag_done, 1)
                        pe.matmul(ps_fox[:, 0:N], m.ones[0:N, :], top_diag[:], start=True, stop=True).then_inc(
                            top_spread, 1)
                for i in range(PAIRS):
                    pe.wait_ge(squared, i + 1)
                    for c in range(NT - 1):
                        pe.matmul(ps[0:TT, 6, c * H + 2 * i:c * H + 2 * i + 2], sq[:, i, c * TT:(c + 1) * TT],
                                  m.head_ones[:, 0:P:HD], start=True, stop=True)
                pe.wait_ge(added, 1)
                pe.matmul(ps_fox[:, 0:N], m.ones[:], den[:], start=True, stop=True).then_inc(den_spread, 1)
                pe.wait_ge(x_chain, 5)
                for e in range(2):
                    for b in range(NS):
                        for i in range(PAIRS):
                            last = pe.matmul(ps[half(e), 3 * e, i * NS + b:i * NS + b + 1], state[half(e), b, i],
                                             m.proj[half(e), T_QB + i, SEQ + b:SEQ + b + 1], start=True, stop=True)
                last.then_inc(o_done, 1)
                fox_values(pe, m, lambda b: ps[:, 1 + b], range(EARLY), values_done)
                pe.wait_ge(squared, 2 * PAIRS)
                c = NT - 1
                for i in range(PAIRS):
                    last = pe.matmul(ps[0:TT, 6, c * H + 2 * i:c * H + 2 * i + 2], sq[:, i, c * TT:(c + 1) * TT],
                                     m.head_ones[:, 0:P:HD], start=True, stop=True)
                last.then_inc(summed, 1)
                pe.wait_ge(den_copied, 1)
                turn_fox_rows(pe, m, rows, ps_o, range(EARLY), values_turned, values_copied)
                pe.wait_ge(inverted, 1)
                for c in range(NT):
                    g, t = divmod(c * TT, TG)
                    last = pe.transpose(ps[0:H, g, t:t + TT], small[:, 1, c * H:(c + 1) * H], m.ident[0:TT, 0:TT])
                last.then_inc(inv_turned, 1)
                pe.wait_ge(inv_copied, 1)
                for i in range(PAIRS):
                    if i >= 2:
                        pe.wait_ge(normed, 1)
                    for g in range(NG):
                        last = pe.matmul(ps[:, 3 - 3 * (i % 2) + g, 0:TG], m.head_rows[0:H, i],
                                         inv_rows[:, g * TG:(g + 1) * TG], start=True, stop=True)
                    last.then_inc(spread, 1)

            @block.scalar
            def _(act):
                act.copy(ab[:, H:2 * H], m.gates[0:NS, NC, 2 * H:3 * H]).then_inc(decay_done, 1)
                act.activation(ab[:, 0:H], m.gates[0:NS, NC, H:2 * H], ACT.Exp).then_inc(decay_done, 1)
                act.wait_ge(turned, 1)
                act.copy(v_rows[:], ps[0:NS, 3, 0:DW]).then_inc(rows_done, 1)
                act.wait_ge(ab_turned, 1)
                act.copy(ab_all[:].rearrange("p b n -> p (b n)"), ps[:, 6, 0:NS * 2 * H]).then_inc(ab_done, 1)
                for i in range(PAIRS):
                    act.activation(sq[:, i, 0:SEQ], m.yT[:, 2 + i, 0:SEQ], ACT.Square).then_inc(squared, 1)
                act.wait_ge(shifted, 2)
                act.activation(flat(p[:]), flat(s_raw[:]), ACT.Exp).then_inc(exp_done, 1)
                act.activation(own_all[:], own_all[:], ACT.Exp).then_inc(exp_done, 1)
                act.wait_ge(o_done, 1)
                for e in range(2):
                    last = act.copy(m.yT[half(e), 2:2 + PAIRS, SEQ:T], ps[half(e), 3 * e, 0:PAIRS * NS].rearrange(
                        "p (m b) -> p m b", m=PAIRS)).then_inc(o_copied, 1)
                act.wait_ge(o_copied, 2)
                for i in range(PAIRS):
                    act.activation(sq[:, i, SEQ:T], m.yT[:, 2 + i, SEQ:T], ACT.Square).then_inc(squared, 1)
                for b in range(EARLY):
                    act.wait_ge(values_done, b + 1)
                    act.copy(rows[:, b], ps[0:H, 1 + b, 0:DW]).then_inc(values_copied, 1)
                root(act, small, with_eps).then_inc(rooted, 1)
                act.wait_ge(inv_turned, 1)
                act.copy(inv_rows[:].rearrange("p (g t) -> p g t", g=NG), ps[0:H, 0:NG, 0:TG]).then_inc(inv_copied, 1)
                act.wait_ge(values_turned, 1)
                for i in range(PAIRS):
                    act.copy(m.fs_out[:, i, 0:EARLY], ps_o[:, i, 0:EARLY, 2 * i:2 * i + 2])

            @block.vector
            def _(dve):
                step = Chain(dve, chain)
                fox_step = Chain(dve, fox_chain)
                dve.wait_ge(ab_done, 1)
                for e in range(2):
                    k = m.proj[half(e), T_KB:T_KB + PAIRS, SEQ:T].rearrange("p m b -> p b m")
                    dve.tensor_tensor(keys[half(e), 1], k, per_head(e, H), ALU.mult)
                    dve.tensor_tensor(keys[half(e), 2], k, per_head(e, 0), ALU.mult).then_inc(keys_scaled, 1)
                    dve.tensor_copy(decay_all[half(e)], per_head(e, 0)).then_inc(keys_scaled, 1)
                dve.wait_ge(keys_scaled, 4)
                dve.tensor_scalar(keys[:, 0], keys[:, 2], -1.0, None, ALU.mult).then_inc(keys_scaled, 1)
                fox_step(dve.tensor_tensor(flat(s_raw[:]), flat(s_raw[:]), flat(m.fs_logf[:]), ALU.add))
                for b in range(NS):
                    last = dve.tensor_reduce(peak[:, b * H:(b + 1) * H], s_raw[:, b].rearrange("p g h -> p h g"), AX_X,
                                             ALU.max)
                fox_step(last)
                dve.tensor_tensor(peak[:], peak[:], own_all[:], ALU.max).then_inc(peaked, 1)
                dve.wait_ge(peak_turned, 1)
                dve.tensor_reduce(top[:], ps_fox[0:N, 0:P], AX_X, ALU.max).then_inc(topped, 1)
                dve.wait_ge(topped, 1)
                dve.tensor_scalar(top_diag[:], m.ident[0:N, 0:N], top[:], None, ALU.mult).then_inc(diag_done, 1)
                dve.wait_ge(top_spread, 1)
                for b in range(NS):
                    last = dve.tensor_tensor(s_raw[:, b], s_raw[:, b], ps_fox[:, b * H:(b + 1) * H].unsqueeze(
                        1).broadcast_to([P, NPAGE, H]), ALU.subtract)
                last.then_inc(shifted, 1)
                dve.tensor_tensor(own_all[:], own_all[:], ps_fox[:, 0:N], ALU.subtract).then_inc(shifted, 1)
                for e in range(2):
                    dve.wait_ge(x_ready, e + 1)
                    dve.tensor_tensor(x[half(e)], seq_banks(e)[half(e)], keys[half(e), 1].unsqueeze(3).broadcast_to(
                        [HD, NS, PAIRS, HD]), ALU.mult).then_inc(x_chain, 1)
                dve.tensor_tensor(state[:], state[:], decay_all[:].unsqueeze(3).broadcast_to([P, NS, PAIRS, HD]),
                                  ALU.mult).then_inc(x_chain, 1)
                dve.wait_ge(x_chain, 3)
                dve.tensor_tensor(state[:], state[:], x[:], ALU.add).then_inc(x_chain, 2)

                dve.wait_ge(exp_done, 2)
                for b in range(NS):
                    last = dve.tensor_reduce(den[:, b * H:(b + 1) * H], p[:, b].rearrange("p g h -> p h g"), AX_X, ALU.add)
                last.then_inc(added, 1)
                dve.wait_ge(den_spread, 1)
                fox_step(dve.tensor_tensor(den[:], ps_fox[:, 0:N], own_all[:], ALU.add))
                dve.sem_inc(den_copied, 1)
                fox_step(dve.reciprocal(den[:], den[:]))

                dve.wait_ge(summed, 1)
                dve.tensor_scalar(small[:, 0], ps[0:TT, 6, 0:NT * H], 1.0 / HD, RMS_EPS, ALU.mult, ALU.add).then_inc(
                    with_eps, 1)
                inverse_root(dve, step, small, rooted).then_inc(inverted, 1)
                for i in range(PAIRS):
                    dve.wait_ge(spread, i + 1)
                    tile = m.yT[:, 2 + i]
                    group = tile.rearrange("p (g t) -> p g t", g=NG)
                    dve.scalar_tensor_tensor(out=group, in0=group, scalar=m.cols_b[:, NORM_B_G:NORM_B_G + 1],
                                             in1=ps[:, 3 - 3 * (i % 2):6 - 3 * (i % 2), 0:TG], op0=ALU.mult,
                                             op1=ALU.mult).then_inc(normed, 1)
                    dve.wait_ge(normed, 2 * i + 1)
                    dve.tensor_tensor(tile, tile, m.proj[:, T_Z + i], ALU.mult).then_inc(normed, 1)


def fox_prompt(nc, m):
    with Phase(nc) as ctx:
        off = O_H + KD * T * 4

        def put(name, shape):
            nonlocal off
            t = nc.alloc_sbuf_tensor_at("fx_" + name, shape, F32, offset=off)
            n = 4
            for d in shape[1:]:
                n *= d
            off += (n + 31) // 32 * 32
            return t

        before = put("before", [P, NC, H])
        neg_c = put("neg_c", [P, H, NC])
        neg_c2 = put("neg_c2", [P, 2, NC])
        q = put("q", [P, SEQ])
        k = put("k", [P, SEQ])
        off_x = off
        bias = [put(f"bias{e}", [P, SEQ]) for e in range(2)]
        x = [put(f"x{s}", [P, SEQ]) for s in range(2)]
        pt = [put(f"pt{s}", [P, NC, P]) for s in range(2)]
        neg_max = put("neg_max", [P, 16])
        total = put("total", [P, 2, NC])
        assert off <= O_TAIL_KV, off
        o = nc.alloc_sbuf_tensor_at("fx_o_rows", [P, NC, P], F32, offset=O_PROJ + (NS - 3) * KV_BYTES)
        assert (NS - 3) * KV_BYTES + NC * P * 4 <= T_QC * T * 4
        ps_s = [ctx.enter_context(nc.psum_tensor(f"fx_s{s}", [P, 2 * 512], F32)) for s in range(2)]
        ps_t = [ctx.enter_context(nc.psum_tensor(f"fx_t{s}", [P, 512], F32)) for s in range(2)]
        ps_o = [ctx.enter_context(nc.psum_tensor(f"fx_o{e}", [P, NC, HD], F32)) for e in range(2)]
        (summed_before, cum_done, neg_c_done, pair_done_1, bias_spread, bias_done, s_done, shifted, maxed,
         exp_done, turned, copied_dve, copied_act, pv_done, inv_done, o_scaled, o_turned, y_done, waited,
         mask_done) = semaphores(
             nc, ctx, *["fx_" + n for n in (
                 "summed_before", "cum_done", "neg_c_done", "pair_done_1", "bias_spread", "bias_done",
                 "s_done", "shifted", "maxed", "exp_done", "turned", "copied_dve", "copied_act", "pv_done",
                 "inv_done", "o_scaled", "o_turned", "y_done", "waited", "mask_done")])
        sample_copied, sample_turned, sample_values, sample_mixed, bias_staged, q_staged, k_staged = semaphores(
            nc, ctx, "fx_sample_copied", "fx_sample_turned", "fx_sample_values", "fx_sample_mixed", "fx_bias_staged", "fx_q_staged", "fx_k_staged")
        one = lambda t: t.rearrange("p a t -> p (a t)")
        half = lambda e: slice(e * HD, (e + 1) * HD)
        units = [(e, i) for e in range(2) for i in reversed(range(NC))]
        U = len(units)
        groups, of_unit = [], []
        for u, (e, i) in enumerate(units):
            mine = [(u, b, min(b + 4, i + 1)) for b in range(0, i + 1, 4)]
            of_unit.append(range(len(groups), len(groups) + len(mine)))
            groups += mine
        G = len(groups)
        assert G % 2 == 0

        late = range(EARLY, NS)
        rows = nc.alloc_sbuf_tensor_at("fx_rows", [H, len(late), DW], F32, offset=off_x)
        ps_sample = ps_t[0][:, 0:PAIRS * NS * H].rearrange("p (m b h) -> p m b h", m=PAIRS, b=NS)
        late_bank = lambda b: [ps_s[0][:, 0:512], ps_s[0][:, 512:1024], ps_s[1][:, 0:512], ps_s[1][:, 512:1024],
                               ps_t[1][:], ps_o[0][:].rearrange("p b d -> p (b d)")][b - EARLY]
        with nc.Block() as block:

            @block.sync
            def _(sp):
                for b in range(EARLY, NS):
                    load_pages(sp, m, m.cache_v, b, m.fs_values[b], m.values_in[EARLY])

            @block.gpsimd
            def _(pool):
                pool.wait_ge(neg_c_done, 1)
                with pool.Fori(0, PAIRS) as j:
                    pool.wait_ge(pair_done_1, j + 1)
                    pool.tensor_copy(neg_c2[:], neg_c[:, bass.ds(j * 2, 2)]).then_inc(bias_staged, 1)

            @block.tensor
            def _(pe):
                logf = m.gates[:, 0:NC, 0:H]
                idle = m.ident[:].bitcast(mybir.dt.bfloat16)
                pe.wait_ge(summed_before, NC)
                pe.matmul(ps_t[0][:, 0:NC * H], m.cumul[:], logf, start=True, stop=False)
                pe.matmul(ps_t[0][:, 0:NC * H], m.ones[:], before[:], start=False, stop=True).then_inc(cum_done, 1)
                pe.sem_inc(pair_done_1, 1)

                def scores(j, u):
                    e, i = units[u]
                    if u >= 2:
                        pe.wait_ge(maxed, j * U + (u - 1))
                    else:
                        pe.wait_ge(bias_done, j * 2 + (u + 1))
                    n = (i + 1) * P
                    for b in range(0, n, 512):
                        w = min(512, n - b)
                        last = pe.matmul(ps_s[u % 2][:, b:b + w], q[half(e), i * P:(i + 1) * P], k[half(e), b:b + w],
                                         start=True, stop=True)
                    last.then_inc(s_done, 1)

                def turns(j, u):
                    n = of_unit[u][0]
                    pe.wait_ge((copied_dve, copied_act)[n % 2], j * (G // 2) + (n // 2 + 1))
                    for _ in range(2):
                        pe.matmul(ps_t[n % 2][:, 0:2 * P], idle[:, 0:P], idle[:], start=True, stop=True)
                    pe.wait_ge(exp_done, j * U + (u + 1))
                    for n in of_unit[u]:
                        _, b0, b1 = groups[n]
                        pe.wait_ge((copied_dve, copied_act)[n % 2], j * (G // 2) + (n // 2 + 1))
                        for b in range(b0, b1):
                            last = pe.transpose(ps_t[n % 2][:, (b - b0) * P:(b - b0 + 1) * P],
                                                x[u % 2][:, b * P:(b + 1) * P], m.ident[:])
                        last.then_inc(turned, 1)

                def values(j, u):
                    e, i = units[u]
                    for n in of_unit[u]:
                        pe.wait_ge((copied_dve, copied_act)[n % 2], j * (G // 2) + (n // 2 + 2))
                    for b in range(i + 1):
                        last = pe.matmul(ps_o[e][:, i], pt[u % 2][:, b],
                                         m.vtok[:, b, bass.ds(j * P + e * HD, HD)], start=(b == 0), stop=(b == i))
                    last.then_inc(pv_done, 1)

                with pe.Fori(0, PAIRS) as j:
                    pe.wait_ge(bias_staged, j + 1)
                    for e in range(2):
                        for b in range(NC):
                            last = pe.matmul(ps_s[e][:, b * P:(b + 1) * P], neg_c2[:, e, b:b + 1].to_broadcast([P, P]),
                                             m.ident[:], start=True, stop=True)
                        last.then_inc(bias_spread, 1)
                    pe.wait_ge(q_staged, j + 1)
                    pe.wait_ge(k_staged, j + 1)
                    scores(j, 0)
                    for u in range(U):
                        if u + 1 < U:
                            scores(j, u + 1)
                        turns(j, u)
                        if u >= 1:
                            values(j, u - 1)
                    values(j, U - 1)
                    pe.wait_ge(o_scaled, j * 2 + 2)
                    for b in range(NC):
                        last = pe.transpose(ps_s[b // 4][:, b % 4 * P:(b % 4 + 1) * P], o[:, b], m.ident[:])
                        if b % 4 == 3:
                            last.then_inc(o_turned, 1)
                    pe.wait_ge(y_done, j * 2 + 2)
                    pe.sem_inc(pair_done_1, 1)
                fox_values(pe, m, late_bank, late, sample_values)
                turn_fox_rows(pe, m, rows, ps_sample, late, sample_turned, sample_copied)

            @block.scalar
            def _(act):
                act.sem_inc(copied_act, 1)
                act.wait_ge(cum_done, 1)
                act.mul(neg_c[:], ps_t[0][:, 0:NC * H].rearrange("p (t h) -> p h t", h=H), -1.0 / SCALE).then_inc(
                    neg_c_done, 1)
                with act.Fori(0, PAIRS) as j:
                    act.wait_ge(pair_done_1, j + 1)
                    act.copy(q[:], one(m.proj[:, bass.ds(j + T_QC, 1), 0:SEQ])).then_inc(q_staged, 1)
                    for e in range(2):
                        act.wait_ge(bias_spread, j * 2 + (e + 1))
                        act.copy(bias[e][:], ps_s[e][:]).then_inc(bias_done, 1)
                    for u, (e, i) in enumerate(units):
                        act.wait_ge(maxed, j * U + (u + 1))
                        w = (i + 1) * P
                        act.activation(x[u % 2][:, 0:w], x[u % 2][:, 0:w], ACT.Exp, bias=neg_max[:, u:u + 1], scale=-1.0,
                                       accum_out=total[:, e, i:i + 1]).then_inc(exp_done, 1)
                        for n in of_unit[u]:
                            if n % 2:
                                _, b0, b1 = groups[n]
                                act.wait_ge(turned, j * G + (n + 1))
                                if u >= 2:
                                    act.wait_ge(pv_done, j * U + (u - 1))
                                act.copy(pt[u % 2][:, b0:b1].rearrange("p b t -> p (b t)"),
                                         ps_t[1][:, 0:(b1 - b0) * P]).then_inc(copied_act, 1)
                    for b in range(2):
                        act.wait_ge(o_turned, j * 2 + (b + 1))
                        act.copy(m.yT[:, bass.ds(j + 5, 1), b * 512:(b + 1) * 512].rearrange("p a t -> p (a t)"),
                                 ps_s[b][:, 0:512]).then_inc(y_done, 1)
                for n, b in enumerate(late):
                    act.wait_ge(sample_values, n + 1)
                    act.copy(rows[:, n], late_bank(b)[0:H, 0:DW]).then_inc(sample_copied, 1)

            @block.vector
            def _(dve):
                dve.sem_inc(copied_dve, 1)
                dve.memset(before[:, 0], 0.0).then_inc(summed_before, 1)
                for t in range(1, NC):
                    dve.wait_ge(summed_before, t)
                    dve.tensor_tensor(before[:, t], before[:, t - 1], m.gates[:, t - 1, 0:H], ALU.add).then_inc(
                        summed_before, 1)
                dve.wait_ge(neg_c_done, 1)
                with dve.Fori(0, PAIRS) as j:

                    def shift(u):
                        e, i = units[u]
                        if i == NC - 1:
                            dve.wait_ge(bias_done, j * 2 + (e + 1))
                        if u >= 1:
                            dve.wait_ge(maxed, j * U + u)
                        diag = bias[e][:, i * P:(i + 1) * P]
                        dve.tensor_tensor(diag, diag, m.causal[:], ALU.add).then_inc(mask_done, 1)
                        dve.wait_ge(mask_done, j * U + (u + 1))
                        dve.wait_ge(s_done, j * U + (u + 1))
                        if u >= 2:
                            dve.wait_ge(turned, j * G + (of_unit[u - 2][-1] + 1))
                        dve.sem_inc(waited, 1)
                        w = (i + 1) * P
                        dve.tensor_tensor_reduce(x[u % 2][:, 0:w], ps_s[u % 2][:, 0:w], bias[e][:, 0:w], -SCALE, 3e38,
                                                 ALU.add, ALU.min, neg_max[:, u:u + 1]).then_inc(maxed, 1)

                    dve.wait_ge(pair_done_1, j + 1)
                    dve.tensor_copy(k[:], one(m.proj[:, bass.ds(j + T_KC, 1), 0:SEQ])).then_inc(k_staged, 1)
                    shift(0)
                    for u in range(U):
                        if u + 1 < U:
                            shift(u + 1)
                        for n in of_unit[u]:
                            if n % 2 == 0:
                                _, b0, b1 = groups[n]
                                dve.wait_ge(turned, j * G + (n + 1))
                                if u >= 2:
                                    dve.wait_ge(pv_done, j * U + (u - 1))
                                dve.tensor_copy(pt[u % 2][:, b0:b1].rearrange("p b t -> p (b t)"),
                                                ps_t[0][:, 0:(b1 - b0) * P]).then_inc(copied_dve, 1)
                    for e in range(2):
                        dve.wait_ge(exp_done, j * U + NC * (e + 1))
                        dve.reciprocal(total[:, e], total[:, e]).then_inc(inv_done, 1)
                        dve.wait_ge(inv_done, j * 2 + (e + 1))
                        dve.wait_ge(pv_done, j * U + NC * (e + 1))
                        dve.tensor_tensor(o[:, :, half(e)], ps_o[e][:], total[:, e].unsqueeze(2).broadcast_to(
                            [P, NC, HD]), ALU.mult).then_inc(o_scaled, 1)
                step = Chain(dve, sample_mixed)
                out = m.fs_out
                dve.wait_ge(sample_turned, 1)
                for i in range(PAIRS):
                    dve.tensor_copy(out[:, i, EARLY:NS], ps_sample[:, i, EARLY:NS, 2 * i:2 * i + 2])
                for e in range(2):
                    of_heads = lambda t: t[half(e), :].rearrange("p (b m e) -> p e m b", m=PAIRS, e=2)[:, e]
                    step(dve.tensor_tensor(m.fs_v_cols[half(e)], m.fs_v_cols[half(e)], of_heads(m.fs_own_all), ALU.mult))
                    step(dve.tensor_tensor(out[half(e), :, :, e], out[half(e), :, :, e], m.fs_v_cols[half(e)], ALU.add))
                    step(dve.tensor_tensor(m.yT[half(e), 5:8, SEQ:T], out[half(e), :, :, e], of_heads(m.fs_den),
                                           ALU.mult))


def split(nc, m, src, hi, lo):
    with Phase(nc) as ctx:
        hi_cut, lo_cut = semaphores(nc, ctx, "y_hi_cut", "y_lo_cut")
        with nc.Block() as block:

            @block.scalar
            def _(act):
                for k in range(KD):
                    act.copy(hi[:, k], src[:, k]).then_inc(hi_cut, 1)

            @block.vector
            def _(dve):
                for k in range(KD):
                    dve.wait_ge(hi_cut, k + 1)
                    dve.tensor_tensor(lo[:, k], src[:, k], hi[:, k].bitcast(F32), ALU.subtract).then_inc(lo_cut, 1)


def add_normed(nc, m, tag, src, g, base, tmp_at, spill=None, rows_out=None):
    with Phase(nc) as ctx:
        sq = nc.alloc_sbuf_tensor_at(f"{tag}_sq", [P, 3, T], F32, offset=tmp_at)
        small = nc.alloc_sbuf_tensor_at(f"{tag}_small", [TT, 3, NT], F32, offset=tmp_at + 3 * T * 4)
        rows = nc.alloc_sbuf_tensor_at(f"{tag}_rows", [P, 4, D], F32, offset=tmp_at + 3 * T * 4 + 160)
        ps_sum = ctx.enter_context(nc.psum_tensor(f"{tag}_ps_sum", [TT, 512], F32))
        ps = ctx.enter_context(nc.psum_tensor(f"{tag}_ps", [P, NG, 512], F32))
        ps_rows = ctx.enter_context(nc.psum_tensor(f"{tag}_ps_rows", [P, 2, 2, 512], F32))
        (squares_added, squared, summed, with_eps, rooted, inverted, spread, scaled, added, base_in, rows_turned, chain,
         copied_act, copied_dve) = semaphores(
            nc, ctx, *[f"{tag}_{n}" for n in ("squares_added", "squared", "summed", "with_eps", "rooted", "inverted",
                                              "spread", "scaled", "added", "base_in", "rows_turned", "chain",
                                              "copied_act", "copied_dve")])
        rows_stored = semaphores(nc, ctx, *[f"{tag}_rows_stored{s}" for s in range(4)])
        grouped = lambda t: t.rearrange("p (g t) -> p g t", g=NG)
        on_pool = [1, 4, 6]
        pool_added, = semaphores(nc, ctx, f"{tag}_pool_added")

        def wait_added(eng, tiles):
            pooled = sum(k < tiles for k in on_pool)
            eng.wait_ge(added, tiles - pooled)
            eng.wait_ge(pool_added, pooled)

        with nc.Block() as block:

            @block.gpsimd
            def _(pool):
                pool.wait_ge(base_in, 16)
                for k in on_pool:
                    pool.wait_ge(scaled, k + 1)
                    pool.tensor_tensor(base[:, k], base[:, k], src[:, k], ALU.add).then_inc(pool_added, 1)

            @block.sync
            def _(sp):
                sp.wait_ge(m.x_spilled if spill is not None else m.x1_spilled, 16 if spill is not None else 32)
                sp.dma_start(base[:], m.xT_dram if spill is not None else m.x1_dram).then_inc(base_in, 16)
                if spill is not None:
                    for n in range(2):
                        wait_added(sp, KD // 2 * (n + 1))
                        part = slice(n * KD // 2, (n + 1) * KD // 2)
                        sp.dma_start(spill[:, part], base[:, part]).then_inc(m.x1_spilled, 16)
                else:
                    for c in range(NC + 1):
                        sp.wait_ge((copied_dve, copied_act)[c % 2], c // 2 + 1)
                        if c < NC:
                            sp.dma_start(m.o_y_p[0, c * P:(c + 1) * P], rows[:, c % 4]).then_inc(rows_stored[c % 4], 16)
                        else:
                            sp.dma_start(m.o_y_s[:, 0], rows[0:NS, c % 4]).then_inc(rows_stored[c % 4], 16)
                    for s in range(4):
                        sp.wait_ge(rows_stored[s], 16 * len(range(s, NC + 1, 4)))

            @block.scalar
            def _(act):
                square_tiles(act, src, sq, squared, squares_added)
                root(act, small, with_eps).then_inc(rooted, 1)
                if spill is None:
                    for c in range(1, NC + 1, 2):
                        act.wait_ge(rows_turned, c + 1)
                        if c >= 4:
                            act.wait_ge(rows_stored[c % 4], 16 * (c // 4))
                        act.copy(rows[:, c % 4].rearrange("p (a n) -> p a n", a=2), ps_rows[:, 1]).then_inc(copied_act, 1)

            @block.tensor
            def _(pe):
                sum_partitions(pe, m, ps_sum, sq, squares_added).then_inc(summed, 1)
                pe.wait_ge(inverted, 1)
                spread_tokens(pe, m, ps, small[:, 1]).then_inc(spread, 1)
                if spill is None:
                    wait_added(pe, KD)
                    for c in range(NC + 1):
                        n = P if c < NC else NS
                        if c >= 2:
                            pe.wait_ge((copied_dve, copied_act)[c % 2], c // 2)
                        for k in range(KD):
                            last = pe.transpose(ps_rows[0:n, c % 2, k // 4, k % 4 * P:(k % 4 + 1) * P],
                                                base[:, k, c * P:c * P + n], m.ident[:])
                        last.then_inc(rows_turned, 1)

            @block.vector
            def _(dve):
                step = Chain(dve, chain)
                add_squares(dve, sq, squared, squares_added)
                dve.wait_ge(summed, 1)
                dve.tensor_scalar(small[:, 0], ps_sum[:, 0:NT], 1.0 / D, RMS_EPS, ALU.mult, ALU.add).then_inc(
                    with_eps, 1)
                inverse_root(dve, step, small, rooted).then_inc(inverted, 1)
                dve.wait_ge(spread, 1)
                dve.wait_ge(base_in, 16)
                for k in range(KD + 1):
                    if k < KD:
                        dve.scalar_tensor_tensor(out=grouped(src[:, k]), in0=grouped(src[:, k]),
                                                 scalar=m.cols_a[:, g + k:g + k + 1], in1=ps[:, :, 0:TG],
                                                 op0=ALU.mult, op1=ALU.mult).then_inc(scaled, 1)
                    if k >= 1 and k - 1 not in on_pool:
                        dve.wait_ge(scaled, k)
                        dve.tensor_tensor(base[:, k - 1], base[:, k - 1], src[:, k - 1], ALU.add).then_inc(added, 1)
                if spill is None:
                    for c in range(0, NC + 1, 2):
                        n = P if c < NC else NS
                        dve.wait_ge(rows_turned, c + 1)
                        if c >= 4:
                            dve.wait_ge(rows_stored[c % 4], 16 * (c // 4))
                        dve.tensor_copy(rows[0:n, c % 4].rearrange("p (a n) -> p a n", a=2), ps_rows[0:n, 0]).then_inc(
                            copied_dve, 1)


def feed_forward(nc, m, hi, lo, acc):
    with Phase(nc) as ctx:
        off = O_FFN
        at = nc.alloc_sbuf_tensor_at

        def put(name, shape, dt=F32):
            nonlocal off
            t = at("ff_" + name, shape, dt, offset=off)
            n = 4
            for d in shape[1:]:
                n *= d
            off += n
            return t

        raw = [put(f"raw{s}", [P, KD, P]) for s in range(2)]
        w_hi = [put(f"w_hi{s}", [P, KD, P], F32R) for s in range(2)]
        w_lo = [put(f"w_lo{s}", [P, KD, P], F32R) for s in range(2)]
        d_raw = [put(f"d_raw{s}", [P, D]) for s in range(2)]
        d_hi = [put(f"d_hi{s}", [P, D], F32R) for s in range(2)]
        d_lo = [put(f"d_lo{s}", [P, D], F32R) for s in range(2)]
        h_hi = [put(f"h_hi{s}", [P, T], F32R) for s in range(2)]
        h_lo = [put(f"h_lo{s}", [P, T], F32R) for s in range(2)]
        hid = put("hid", [P, T])
        assert off <= O_END, off
        ps_w = [ctx.enter_context(nc.psum_tensor(f"ff_ps{s}", [P, NG, 512], F32)) for s in range(2)]
        ps_d = [ctx.enter_context(nc.psum_tensor(f"ff_psd{s}", [P, 512], F32)) for s in range(2)]
        (w_hi_cut, w_lo_cut, d_hi_cut, d_lo_cut, multiplied, gated, hidden, hid_hi, hid_lo, down_done, down_added,
         cleared) = semaphores(
             nc, ctx, *["ff_" + n for n in ("w_hi_cut", "w_lo_cut", "d_hi_cut", "d_lo_cut", "multiplied", "gated",
                                            "hidden", "hid_hi", "hid_lo", "down_done", "down_added", "cleared")])
        w_in = semaphores(nc, ctx, "ff_w_in0", "ff_w_in1")
        d_in = semaphores(nc, ctx, "ff_d_in0", "ff_d_in1")
        pairs = NF // 2
        units = [(n, g) for n in range(KD) for g in range(NG)]
        U = len(units)
        by_k = lambda w: w[0].rearrange("(k p) n -> p k n", p=P)
        weights = (by_k(m.w_gate), by_k(m.w_up))

        def over_pairs(eng, body):
            body(0, True, False)
            with eng.Fori(1, pairs - 1) as i:
                body(i, False, False)
            body(pairs - 1, False, True)

        with nc.Block() as block:

            @block.gpsimd
            def _(pool):
                pool.memset(acc[:], 0.0).then_inc(cleared, 1)

            @block.sync
            def _(sp):
                def load(i, t, first_use):
                    if not first_use:
                        sp.wait_ge(w_lo_cut, i * 4 + (t - 1))
                    sp.dma_start(raw[t % 2][:], weights[t % 2][:, :, bass.ds(i * (2 * P) + t // 2 * P, P)]).then_inc(
                        w_in[t % 2], 16)

                def body(i, first, last):
                    load(i, 2, False)
                    load(i, 3, False)
                    for f in range(2):
                        if not first:
                            sp.wait_ge(d_lo_cut, i * 2)
                        sp.dma_start(d_raw[f][:], m.w_down[0, bass.ds(i * (2 * P) + f * P, P)]).then_inc(d_in[f], 16)
                    if not last:
                        load(i, 4, False)
                        load(i, 5, False)

                sp.wait_ge(m.x1_spilled, 32)
                load(0, 0, True)
                load(0, 1, True)
                over_pairs(sp, body)

            @block.scalar
            def _(act):
                def cut(i, t, first_use=False):
                    act.wait_ge(w_in[t % 2], i * 32 + (t // 2 + 1) * 16)
                    if not first_use:
                        act.wait_ge(multiplied, i * 4 + (t - 1))
                    act.copy(w_hi[t % 2][:], raw[t % 2][:]).then_inc(w_hi_cut, 1)

                def silu(i, f, first=False):
                    act.wait_ge(multiplied, i * 4 + (2 * f + 1))
                    if not first:
                        act.wait_ge(hid_lo, i * 2 + f)
                    act.activation(hid[:].rearrange("p (g t) -> p g t", g=NG), ps_w[0][:, :, 0:TG], ACT.Silu).then_inc(
                        gated, 1)

                def cut_hidden(i, f):
                    act.wait_ge(hidden, i * 2 + (f + 1))
                    act.copy(h_hi[f][:], hid[:]).then_inc(hid_hi, 1)

                def body(i, first, last):
                    cut(i, 1, first)
                    silu(i, 0, first)
                    cut(i, 2)
                    for f in range(2):
                        act.wait_ge(d_in[f], i * 16 + 16)
                        if not first:
                            act.wait_ge(down_done, i * U)
                        act.copy(d_hi[f][:], d_raw[f][:]).then_inc(d_hi_cut, 1)
                    cut_hidden(i, 0)
                    cut(i, 3)
                    silu(i, 1)
                    if not last:
                        cut(i, 4)
                    cut_hidden(i, 1)

                cut(0, 0, True)
                over_pairs(act, body)

            @block.vector
            def _(dve):
                def cut(i, t):
                    dve.wait_ge(w_hi_cut, i * 4 + (t + 1))
                    dve.tensor_tensor(w_lo[t % 2][:], raw[t % 2][:], w_hi[t % 2][:].bitcast(F32),
                                      ALU.subtract).then_inc(w_lo_cut, 1)

                def hidden_tile(i, f):
                    dve.wait_ge(gated, i * 2 + (f + 1))
                    dve.wait_ge(multiplied, i * 4 + (2 * f + 2))
                    group = hid[:].rearrange("p (g t) -> p g t", g=NG)
                    dve.tensor_tensor(group, group, ps_w[1][:, :, 0:TG], ALU.mult).then_inc(hidden, 1)
                    dve.wait_ge(hid_hi, i * 2 + (f + 1))
                    dve.tensor_tensor(h_lo[f][:], hid[:], h_hi[f][:].bitcast(F32), ALU.subtract).then_inc(hid_lo, 1)

                def add_down(i):
                    for u, (n, g) in enumerate(units):
                        dve.wait_ge(down_done, i * U + (u + 1))
                        part = acc[:, n, g * TG:(g + 1) * TG]
                        dve.tensor_tensor(part, part, ps_d[u % 2][:, 0:TG], ALU.add).then_inc(down_added, 1)

                def body(i, first, last):
                    cut(i, 1)
                    if not first:
                        add_down(i - 1)
                    cut(i, 2)
                    for f in range(2):
                        dve.wait_ge(d_hi_cut, i * 2 + (f + 1))
                        dve.tensor_tensor(d_lo[f][:], d_raw[f][:], d_hi[f][:].bitcast(F32), ALU.subtract).then_inc(
                            d_lo_cut, 1)
                    hidden_tile(i, 0)
                    cut(i, 3)
                    if not last:
                        cut(i, 4)
                    hidden_tile(i, 1)
                    if first:
                        dve.wait_ge(cleared, 1)

                cut(0, 0)
                over_pairs(dve, body)
                add_down(pairs - 1)

            @block.tensor
            def _(pe):
                def gate_up(i, t, first_use=False):
                    pe.wait_ge(w_lo_cut, i * 4 + (t + 1))
                    if not first_use:
                        pe.wait_ge((gated, hidden)[t % 2], i * 2 + t // 2)
                    for k in range(KD):
                        for n, (a, b) in enumerate(((w_hi, hi), (w_hi, lo), (w_lo, hi))):
                            for g in range(NG):
                                last = pe.matmul(ps_w[t % 2][:, g, 0:TG], a[t % 2][:, k], b[:, k, g * TG:(g + 1) * TG],
                                                 start=(k == 0 and n == 0), stop=(k == KD - 1 and n == 2))
                    last.then_inc(multiplied, 1)

                def down(i, first):
                    pe.wait_ge(hid_lo, i * 2 + 2)
                    pe.wait_ge(d_lo_cut, i * 2 + 2)
                    for u, (n, g) in enumerate(units):
                        if not (first and u < 2):
                            pe.wait_ge(down_added, i * U + (u - 1))
                        for f in range(2):
                            for r, (a, b) in enumerate(((d_hi, h_hi), (d_hi, h_lo), (d_lo, h_hi))):
                                last = pe.matmul(ps_d[u % 2][:, 0:TG], a[f][:, n * P:(n + 1) * P],
                                                 b[f][:, g * TG:(g + 1) * TG], start=(f == 0 and r == 0),
                                                 stop=(f == 1 and r == 2))
                        last.then_inc(down_done, 1)

                gate_up(0, 0, True)
                gate_up(0, 1, True)
                gate_up(0, 2)
                gate_up(0, 3)
                gate_up(1, 0)
                down(0, True)
                for t in range(1, 4):
                    gate_up(1, t)
                with pe.Fori(2, pairs) as i:
                    gate_up(i, 0)
                    down(i - 1, False)
                    for t in range(1, 4):
                        gate_up(i, t)
                down(pairs - 1, False)


def program(nc, m):
    at = nc.alloc_sbuf_tensor_at
    m.xT_dram = nc.dram_tensor("xT_spill", [P, KD, T], F32).ap()
    m.x1_dram = nc.dram_tensor("x1_spill", [P, KD, T], F32).ap()
    constants(nc, m)
    m.vtok = at("vtok", [P, NC + 1, NV], F32, offset=O_VTOK)
    fox_sample_tensors(nc, m)
    load_and_transpose(nc, m)
    h_hi = at("h_hi", [P, KD, T], F32R, offset=O_H)
    h_lo = at("h_lo", [P, KD, T], F32R, offset=O_H + COLS)
    rms_norm(nc, m, "pre", m.xT, G_PRE_MIX, h_hi, h_lo, O_W)
    project_rows(nc, m, h_hi, h_lo)
    m.proj = at("proj", [P, NPROJ, T], F32, offset=O_PROJ)
    project(nc, m, "in", m.w_in[0], ((0, FIRST_TILES), (COL_QC, QC_TILES)), h_hi, h_lo, m.proj,
            with_taps=True)
    m.yT = at("yT", [P, KD, T], F32, offset=O_H)
    convolve(nc, m)
    gates(nc, m)
    delta_rule(nc, m)
    samples(nc, m)
    fox_prompt(nc, m)
    y_hi = at("y_hi", [P, KD, T], F32R, offset=O_PROJ)
    y_lo = at("y_lo", [P, KD, T], F32R, offset=O_PROJ + COLS)
    split(nc, m, m.yT, y_hi, y_lo)
    mix = at("mix", [P, KD, T], F32, offset=O_H)
    project(nc, m, "out", m.w_out[0], ((0, KD),), y_hi, y_lo, mix)
    x1 = at("x1", [P, KD, T], F32, offset=O_H + COLS)
    add_normed(nc, m, "mid", mix, G_POST_MIX, x1, O_PROJ, spill=m.x1_dram)
    h2_hi = at("h2_hi", [P, KD, T], F32R, offset=O_PROJ)
    h2_lo = at("h2_lo", [P, KD, T], F32R, offset=O_PROJ + COLS)
    rms_norm(nc, m, "ffn", x1, G_PRE_FFN, h2_hi, h2_lo, O_H)
    acc = at("acc", [P, KD, T], F32, offset=O_PROJ + 2 * COLS)
    feed_forward(nc, m, h2_hi, h2_lo, acc)
    x2 = at("x2", [P, KD, T], F32, offset=O_PROJ)
    add_normed(nc, m, "end", acc, G_POST_FFN, x2, O_PROJ + COLS)


def tables():
    i = np.arange(P)
    row, col = i[:, None], i[None, :]
    t = np.zeros((15, P, P), np.float32)
    t[0] = row == col
    t[1] = row <= col
    t[2] = row > col
    t[3] = 1
    t[4] = row // HD == col // HD
    level = lambda s: (row // (2 * s) == col // (2 * s)) & (row // s % 2 == 1) & (col // s % 2 == 0)
    t[5] = -level(1).T.astype(np.float32)
    t[6] = np.where(col >= row, 0, NEG)
    t[7] = np.where(col <= row, 0, NEG)
    for n in range(7):
        t[8 + n] = -level(1 << n).astype(np.float32)
    return t


def head_table():
    t = np.zeros((2 * H, H, P), np.float32)
    for j in range(H):
        for e in range(2):
            t[2 * j + e, j, e * HD:(e + 1) * HD] = 1
    return t


def build(nc, ins, outs):
    m = Mem()
    (m.x_prompt, m.x_sample, m.cache_k, m.cache_v, m.cache_logf, m.page_table, m.state_conv_a, m.state_conv_b,
     m.state_delta, m.w_in, m.conv_a_w, m.conv_a_b, m.ln_a_g, m.ln_a_b, m.conv_b_w, m.a_log, m.dt_bias, m.norm_b_g,
     m.f_bias, m.w_out, m.g_pre_mix, m.g_post_mix, m.g_pre_ffn, m.g_post_ffn, m.w_gate, m.w_up, m.w_down,
     m.tables, m.head_table) = ins
    (m.o_y_p, m.o_y_s, m.o_k_p, m.o_v_p, m.o_f_p, m.o_conv_a_p, m.o_conv_b_p, m.o_delta_p, m.o_k_s, m.o_v_s, m.o_f_s,
     m.o_conv_a_s, m.o_conv_b_s, m.o_delta_s) = outs
    program(nc, m)


_INS = ["x_prompt", "x_sample", "cache_k", "cache_v", "cache_logf", "page_table", "state_conv_a", "state_conv_b",
        "state_delta", "w_in", "conv_a_w", "conv_a_b", "ln_a_g", "ln_a_b", "conv_b_w", "a_log", "dt_bias", "norm_b_g",
        "f_bias", "w_out", "g_pre_mix", "g_post_mix", "g_pre_ffn", "g_post_ffn", "w_gate", "w_up", "w_down"]
_OUTS = [(1, SEQ, D), (NS, 1, D), (1, 1, SEQ, H, HD), (1, 1, SEQ, H, HD), (1, 1, SEQ, H), (1, 1, KA - 1, CA),
         (1, 1, KB - 1, 3 * DW), (1, 1, H, HD, HD), (1, NS, 1, H, HD), (1, NS, 1, H, HD), (1, NS, 1, H),
         (1, NS, KA - 1, CA), (1, NS, KB - 1, 3 * DW), (1, NS, H, HD, HD)]


def kernel(**inputs):
    import numpy as _np
    import concourse.bacc as _bacc
    from concourse import mybir as _mybir
    from concourse.bass_utils import run_bass_kernel_spmd as _run

    nc = _bacc.Bacc("TRN2", target_bir_lowering=False, num_devices=1)
    arrays, ins = {}, []
    for name in _INS + ["tables", "head_table"]:
        if name == "tables":
            a = tables()
        elif name == "head_table":
            a = head_table()
        else:
            a = _np.ascontiguousarray(inputs[name])
        arrays[f"in_{name}_dram"] = a
        ins.append(nc.dram_tensor(f"in_{name}_dram", a.shape, _mybir.dt.from_np(a.dtype), kind="ExternalInput").ap())
    outs = [nc.dram_tensor(f"out_{i}_dram", shape, _mybir.dt.float32, kind="ExternalOutput").ap()
            for i, shape in enumerate(_OUTS)]
    build(nc, ins, outs)
    r = _run(nc, [arrays], core_ids=[0])
    return tuple(r.results[0][f"out_{i}_dram"] for i in range(len(_OUTS)))
```
